# Optimizing a Trainium2 kernel written in Bass

```python
import math
import jax, jax.numpy as jnp
from jax import lax
import numpy as np

D_MODEL = 1024
BATCH = 1
SEQ = 256
DEPTH = 1

N_HEADS = 8
HEAD_DIM = D_MODEL // (2 * N_HEADS)
V_DIM = 2 * HEAD_DIM
ATT_QK_WIDTH = N_HEADS * 2 * HEAD_DIM
ATT_V_WIDTH = N_HEADS * V_DIM
ROPE_DIM = HEAD_DIM // 4
ROPE_THETA = 500000.0
Q_BLOCK = 128
POOL_WINDOWS = (2, 4, 8, 16)
N_POOL_GROUPS = 4
POOL_GROUP_IN = 128
POOL_WIDTH = N_POOL_GROUPS * POOL_GROUP_IN
POOL_GROUP_OUT = D_MODEL // N_POOL_GROUPS
N_BRANCHES = 2
D_FF = 4 * D_MODEL
IN_WIDTH = 2 * ATT_QK_WIDTH + ATT_V_WIDTH + POOL_WIDTH + N_BRANCHES * D_MODEL
RMS_EPS = 1e-6


def lambda_init(layer_idx):
    return 0.8 - 0.6 * math.exp(-0.3 * layer_idx)

def rmsnorm(x, g):
    xf = x.astype(jnp.float32)
    y = xf * lax.rsqrt(jnp.mean(xf * xf, axis=-1, keepdims=True) + RMS_EPS)
    return (y * g.astype(jnp.float32)).astype(x.dtype)

def rope_partial(t, cos, sin):
    half = ROPE_DIM // 2
    t1 = t[..., :half]
    t2 = t[..., half:ROPE_DIM]
    rest = t[..., ROPE_DIM:]
    return jnp.concatenate([t1 * cos - t2 * sin, t2 * cos + t1 * sin, rest], axis=-1)

def diff_attention(q, k, v, positions, lam, subln_g, lam_init):
    B, S = q.shape[0], q.shape[1]
    inv_freq = ROPE_THETA ** (-jnp.arange(0, ROPE_DIM, 2, dtype=jnp.float32) / ROPE_DIM)
    ang = positions.astype(jnp.float32)[..., None] * inv_freq
    cos = jnp.cos(ang)[:, :, None, :].astype(q.dtype)
    sin = jnp.sin(ang)[:, :, None, :].astype(q.dtype)
    q = rope_partial(q.reshape(B, S, N_HEADS * 2, HEAD_DIM), cos, sin).reshape(B, S, N_HEADS, 2, HEAD_DIM)
    k = rope_partial(k.reshape(B, S, N_HEADS * 2, HEAD_DIM), cos, sin).reshape(B, S, N_HEADS, 2, HEAD_DIM)
    q = q * (HEAD_DIM ** -0.5)
    outs = []
    for i in range(S // Q_BLOCK):
        q0 = i * Q_BLOCK
        kend = q0 + Q_BLOCK
        qb = q[:, q0:kend]
        kb = k[:, :kend]
        vb = v[:, :kend]
        s = jnp.einsum('bqhcd,bkhcd->bhcqk', qb, kb).astype(jnp.float32)
        mask = jnp.arange(kend)[None, :] <= (q0 + jnp.arange(Q_BLOCK))[:, None]
        s = jnp.where(mask, s, -jnp.inf)
        p = jax.nn.softmax(s, axis=-1)
        w = p[:, :, 0] - lam * p[:, :, 1]
        outs.append(jnp.einsum('bhqk,bkhd->bqhd', w.astype(v.dtype), vb))
    o = jnp.concatenate(outs, axis=1)
    o = rmsnorm(o, subln_g) * (1.0 - lam_init)
    return o.reshape(B, S, ATT_V_WIDTH)

def multiscale_pool(u, w_pool, pool_scale):
    B, S = u.shape[0], u.shape[1]
    uf = u.astype(jnp.float32).reshape(B, S, N_POOL_GROUPS, POOL_GROUP_IN)
    c = lax.cumsum(uf, axis=1)
    idx = jnp.arange(S)
    parts = []
    for g, w in enumerate(POOL_WINDOWS):
        cg = c[:, :, g]
        c_prev = jnp.pad(cg, ((0, 0), (w, 0), (0, 0)))[:, :S]
        cnt = jnp.minimum(idx + 1, w).astype(jnp.float32)[None, :, None]
        parts.append((cg - c_prev) / cnt - uf[:, :, g])
    d = jnp.stack(parts, axis=2).astype(u.dtype)
    y = jnp.einsum('bsgc,gcd->bsgd', d, w_pool).reshape(B, S, D_MODEL)
    return y * pool_scale

def first_inputs(seed: int = 0) -> dict:
    key = jax.random.key(seed)
    ks = jax.random.split(key, 18)
    f32 = jnp.float32
    x = jax.random.normal(ks[0], (BATCH, SEQ, D_MODEL), f32)
    offs = jax.random.randint(ks[1], (BATCH, 1), 0, 1024, dtype=jnp.int32)
    positions = (offs + jnp.arange(SEQ, dtype=jnp.int32)[None, :]).astype(jnp.int32)
    gain = lambda k, n: 1.0 + 0.02 * jax.random.normal(k, (DEPTH, n), f32)
    return {
        "x": x,
        "positions": positions,
        "norm_attn_g": gain(ks[2], D_MODEL),
        "w_in": jax.random.normal(ks[3], (DEPTH, D_MODEL, IN_WIDTH), f32) * D_MODEL ** -0.5,
        "lam_q1": 0.1 * jax.random.normal(ks[4], (DEPTH, HEAD_DIM), f32),
        "lam_k1": 0.1 * jax.random.normal(ks[5], (DEPTH, HEAD_DIM), f32),
        "lam_q2": 0.1 * jax.random.normal(ks[6], (DEPTH, HEAD_DIM), f32),
        "lam_k2": 0.1 * jax.random.normal(ks[7], (DEPTH, HEAD_DIM), f32),
        "subln_g": gain(ks[8], V_DIM),
        "w_pool": jax.random.normal(ks[9], (DEPTH, N_POOL_GROUPS, POOL_GROUP_IN, POOL_GROUP_OUT), f32) * POOL_GROUP_IN ** -0.5,
        "pool_scale": 1.0 + 0.1 * jax.random.normal(ks[10], (DEPTH, D_MODEL), f32),
        "w_out": jax.random.normal(ks[11], (DEPTH, D_MODEL, D_MODEL), f32) * D_MODEL ** -0.5,
        "norm_mlp_g": gain(ks[12], D_MODEL),
        "w_up": jax.random.normal(ks[13], (DEPTH, D_MODEL, D_FF), f32) * D_MODEL ** -0.5,
        "w_down": jax.random.normal(ks[14], (DEPTH, D_FF, D_MODEL), f32) * D_FF ** -0.5,
        "final_norm_g": 1.0 + 0.02 * jax.random.normal(ks[15], (D_MODEL,), f32),
    }

def first_block(x, positions, norm_attn_g, w_in, lam_q1, lam_k1, lam_q2, lam_k2, subln_g,
              w_pool, pool_scale, w_out, norm_mlp_g, w_up, w_down, final_norm_g):
    B, S = x.shape[0], x.shape[1]
    splits = np.cumsum([ATT_QK_WIDTH, ATT_QK_WIDTH, ATT_V_WIDTH, POOL_WIDTH]).tolist()
    for l in range(DEPTH):
        lam_init = lambda_init(l)
        h = rmsnorm(x, norm_attn_g[l])
        u = h @ w_in[l]
        u_q, u_k, u_v, u_pool, u_gate = jnp.split(u, splits, axis=-1)
        q = u_q.reshape(B, S, N_HEADS, 2, HEAD_DIM)
        k = u_k.reshape(B, S, N_HEADS, 2, HEAD_DIM)
        v = u_v.reshape(B, S, N_HEADS, V_DIM)
        lam = (jnp.exp(jnp.sum(lam_q1[l].astype(jnp.float32) * lam_k1[l].astype(jnp.float32)))
               - jnp.exp(jnp.sum(lam_q2[l].astype(jnp.float32) * lam_k2[l].astype(jnp.float32)))
               + lam_init)
        a = diff_attention(q, k, v, positions, lam, subln_g[l], lam_init)
        p = multiscale_pool(u_pool, w_pool[l], pool_scale[l])
        gates = jax.nn.sigmoid(u_gate.reshape(B, S, N_BRANCHES, D_MODEL))
        merged = gates[:, :, 0] * a + gates[:, :, 1] * p
        x = x + (merged @ w_out[l]).astype(x.dtype)
        h2 = rmsnorm(x, norm_mlp_g[l])
        z = jnp.square(jax.nn.relu(h2 @ w_up[l]))
        x = x + (z @ w_down[l]).astype(x.dtype)
    return rmsnorm(x, final_norm_g)


MEM_LEN = 256

HEAD_DIM_2 = 64
NSA_HEADS = D_MODEL // 128
NSA_KV_HEADS = NSA_HEADS // 4
NSA_GROUP = NSA_HEADS // NSA_KV_HEADS
NSA_WIDTH = NSA_HEADS * HEAD_DIM_2
NSA_KV_WIDTH = NSA_KV_HEADS * HEAD_DIM_2
CMP_BLOCK = 32
CMP_STRIDE = 16
CMP_HIDDEN = 2 * HEAD_DIM_2
SLC_BLOCK = 64
N_SELECT = 8
WINDOW = 256
NSA_QBLOCK = SLC_BLOCK

GLA_HEADS = 4
GLA_DK = 64
GLA_DV = 128
GLA_KEY_WIDTH = GLA_HEADS * GLA_DK
GLA_VAL_WIDTH = GLA_HEADS * GLA_DV
GLA_GATE_RANK = 16
GLA_TAU = 16.0
GLA_CHUNK = 64

XATTN_HEADS = 4
XATTN_HEAD_DIM = 128
XATTN_WIDTH = XATTN_HEADS * XATTN_HEAD_DIM

FFN_DIM = 2816
CONV_WIDTH = 3

NEG_INF = -1e30

IN_SPLITS = (NSA_WIDTH, 6 * NSA_KV_WIDTH, 3 * NSA_HEADS,
             GLA_KEY_WIDTH, GLA_KEY_WIDTH, GLA_VAL_WIDTH, GLA_VAL_WIDTH, GLA_GATE_RANK,
             2 * D_MODEL)
IN_WIDTH_2 = (NSA_WIDTH + 6 * NSA_KV_WIDTH + 3 * NSA_HEADS + 2 * GLA_KEY_WIDTH
            + 2 * GLA_VAL_WIDTH + GLA_GATE_RANK + 2 * D_MODEL)


def rms_norm(x, g):
    x32 = x.astype(jnp.float32)
    y = x32 * lax.rsqrt(jnp.mean(x32 * x32, axis=-1, keepdims=True) + RMS_EPS)
    return (y * g.astype(jnp.float32)).astype(x.dtype)

def alibi_slopes(n):
    return 2.0 ** (-8.0 * jnp.arange(1, n + 1, dtype=jnp.float32) / n)

def masked_softmax(s, mask):
    s = jnp.where(mask, s, NEG_INF)
    return jnp.where(mask, jax.nn.softmax(s, axis=-1), 0.0)

def compress_blocks(kv, pos_emb, w1, w2):
    B, S, H, dh = kv.shape
    c = kv.reshape(B, S // CMP_STRIDE, CMP_STRIDE, H, dh)
    blocks = jnp.concatenate([c[:, :-1], c[:, 1:]], axis=2) + pos_emb[None, None, :, None, :]
    n_cmp = blocks.shape[1]
    flat = blocks.transpose(0, 1, 3, 2, 4).reshape(B, n_cmp, H, CMP_BLOCK * dh)
    return jax.nn.gelu(flat @ w1) @ w2

def nsa_attention(q, kc, vc, ks, vs, kw, vw, gate_logits,
                  cmp_pos_k, cmp_w1_k, cmp_w2_k, cmp_pos_v, cmp_w1_v, cmp_w2_v):
    B, S = q.shape[:2]
    f32 = jnp.float32
    q = q.reshape(B, S, NSA_KV_HEADS, NSA_GROUP, HEAD_DIM_2) * (HEAD_DIM_2 ** -0.5)
    kv_shape = (B, S, NSA_KV_HEADS, HEAD_DIM_2)
    kc, vc, ks, vs, kw, vw = [a.reshape(kv_shape) for a in (kc, vc, ks, vs, kw, vw)]
    gates = jax.nn.sigmoid(gate_logits.astype(f32)).reshape(B, S, NSA_KV_HEADS, NSA_GROUP, 3)
    slopes = alibi_slopes(NSA_HEADS).reshape(NSA_KV_HEADS, NSA_GROUP)

    k_cmp = compress_blocks(kc, cmp_pos_k, cmp_w1_k, cmp_w2_k)
    v_cmp = compress_blocks(vc, cmp_pos_v, cmp_w1_v, cmp_w2_v)
    n_cmp = k_cmp.shape[1]
    cmp_end = jnp.arange(n_cmp) * CMP_STRIDE + CMP_BLOCK - 1

    n_slc = S // SLC_BLOCK
    n_sel = min(N_SELECT, n_slc)
    cmp_tok = jnp.arange(n_cmp)[:, None] * CMP_STRIDE + jnp.arange(CMP_BLOCK)[None, :]
    overlap = jax.nn.one_hot(cmp_tok // SLC_BLOCK, n_slc, dtype=f32).sum(axis=1) / CMP_BLOCK

    ks_blk = ks.reshape(B, n_slc, SLC_BLOCK, NSA_KV_HEADS, HEAD_DIM_2).transpose(0, 3, 1, 2, 4)
    vs_blk = vs.reshape(B, n_slc, SLC_BLOCK, NSA_KV_HEADS, HEAD_DIM_2).transpose(0, 3, 1, 2, 4)
    kw_pad = jnp.pad(kw, ((0, 0), (WINDOW, 0), (0, 0), (0, 0)))
    vw_pad = jnp.pad(vw, ((0, 0), (WINDOW, 0), (0, 0), (0, 0)))
    b_ix = jnp.arange(B)[:, None, None, None]
    h_ix = jnp.arange(NSA_KV_HEADS)[None, :, None, None]
    forced_score = float(NSA_GROUP + 1)

    def query_block(i):
        t0 = i * NSA_QBLOCK
        qb = lax.dynamic_slice_in_dim(q, t0, NSA_QBLOCK, axis=1)
        gb = lax.dynamic_slice_in_dim(gates, t0, NSA_QBLOCK, axis=1)
        t = t0 + jnp.arange(NSA_QBLOCK)

        dist = (t[:, None] - cmp_end[None, :]).astype(f32)
        s = jnp.einsum('bqhgd,bnhd->bhgqn', qb, k_cmp).astype(f32)
        s = s - slopes[:, :, None, None] * dist
        p_cmp = masked_softmax(s, dist >= 0)
        o_cmp = jnp.einsum('bhgqn,bnhd->bqhgd', p_cmp.astype(v_cmp.dtype), v_cmp)

        imp = jnp.einsum('bhgqn,nj->bhqj', p_cmp, overlap)
        cur = t // SLC_BLOCK
        j = jnp.arange(n_slc)
        forced = (j[None, :] == 0) | (j[None, :] == cur[:, None]) | (j[None, :] == cur[:, None] - 1)
        future = j[None, :] > cur[:, None]
        imp = jnp.where(forced, forced_score, jnp.where(future, -1.0, imp))
        _, idx = lax.top_k(imp, n_sel)
        kg = ks_blk[b_ix, h_ix, idx]
        vg = vs_blk[b_ix, h_ix, idx]
        kpos = idx[..., None] * SLC_BLOCK + jnp.arange(SLC_BLOCK)
        dist = (t[:, None, None] - kpos).astype(f32)[:, :, None]
        s = jnp.einsum('bqhgd,bhqnld->bhgqnl', qb, kg).astype(f32)
        s = s - slopes[None, :, :, None, None, None] * dist
        n_keys = n_sel * SLC_BLOCK
        s = s.reshape(B, NSA_KV_HEADS, NSA_GROUP, NSA_QBLOCK, n_keys)
        mask = (dist >= 0).reshape(B, NSA_KV_HEADS, 1, NSA_QBLOCK, n_keys)
        p_slc = masked_softmax(s, mask)
        vg = vg.reshape(B, NSA_KV_HEADS, NSA_QBLOCK, n_keys, HEAD_DIM_2)
        o_slc = jnp.einsum('bhgqk,bhqkd->bqhgd', p_slc.astype(vg.dtype), vg)

        kwb = lax.dynamic_slice_in_dim(kw_pad, t0, NSA_QBLOCK + WINDOW, axis=1)
        vwb = lax.dynamic_slice_in_dim(vw_pad, t0, NSA_QBLOCK + WINDOW, axis=1)
        kpos = t0 - WINDOW + jnp.arange(NSA_QBLOCK + WINDOW)
        dist_i = t[:, None] - kpos[None, :]
        mask = (dist_i >= 0) & (dist_i < WINDOW) & (kpos[None, :] >= 0)
        s = jnp.einsum('bqhgd,bkhd->bhgqk', qb, kwb).astype(f32)
        s = s - slopes[:, :, None, None] * dist_i.astype(f32)
        p_win = masked_softmax(s, mask)
        o_win = jnp.einsum('bhgqk,bkhd->bqhgd', p_win.astype(vwb.dtype), vwb)

        return gb[..., 0:1] * o_cmp + gb[..., 1:2] * o_slc + gb[..., 2:3] * o_win

    out = lax.map(query_block, jnp.arange(S // NSA_QBLOCK))
    out = out.transpose(1, 0, 2, 3, 4, 5).reshape(B, S, NSA_WIDTH)
    return out.astype(q.dtype)

def gla(q, k, v, r, a_low, w_alpha2, b_alpha, norm_g):
    B, S = q.shape[:2]
    f32 = jnp.float32
    nc = S // GLA_CHUNK
    shp_k = (B, nc, GLA_CHUNK, GLA_HEADS, GLA_DK)
    shp_v = (B, nc, GLA_CHUNK, GLA_HEADS, GLA_DV)
    q = q.reshape(shp_k).astype(f32) * (GLA_DK ** -0.5)
    k = k.reshape(shp_k).astype(f32)
    v = v.reshape(shp_v).astype(f32)
    log_a = jax.nn.log_sigmoid((a_low @ w_alpha2 + b_alpha).astype(f32)) / GLA_TAU
    b = jnp.cumsum(log_a.reshape(shp_k), axis=2)
    b_last = b[:, :, -1:]
    q_d = q * jnp.exp(b)
    k_d = k * jnp.exp(-b)
    k_s = k * jnp.exp(b_last - b)
    causal = jnp.tril(jnp.ones((GLA_CHUNK, GLA_CHUNK), dtype=bool))
    att = jnp.where(causal, jnp.einsum('bnihd,bnjhd->bnhij', q_d, k_d), 0.0)
    o_intra = jnp.einsum('bnhij,bnjhe->bnihe', att, v)
    state_inc = jnp.einsum('bnjhd,bnjhe->bnhde', k_s, v)
    decay = jnp.exp(b_last[:, :, 0])

    def step(state, xs):
        dec, inc = xs
        return dec[..., None] * state + inc, state

    init = jnp.zeros((B, GLA_HEADS, GLA_DK, GLA_DV), f32)
    _, states = lax.scan(step, init, (decay.swapaxes(0, 1), state_inc.swapaxes(0, 1)))
    states = states.swapaxes(0, 1)
    o_inter = jnp.einsum('bnihd,bnhde->bnihe', q_d, states)
    o = (o_intra + o_inter).reshape(B, S, GLA_HEADS, GLA_DV)
    o = o * lax.rsqrt(jnp.mean(o * o, axis=-1, keepdims=True) + RMS_EPS) * norm_g.astype(f32)
    o = o * jax.nn.silu(r.reshape(B, S, GLA_HEADS, GLA_DV).astype(f32))
    return o.reshape(B, S, GLA_VAL_WIDTH).astype(r.dtype)

def memory_cross_attention(h, mem_n, w_xq, w_xkv, w_xo):
    B, S = h.shape[:2]
    M = mem_n.shape[1]
    q = (h @ w_xq).reshape(B, S, XATTN_HEADS, XATTN_HEAD_DIM) * (XATTN_HEAD_DIM ** -0.5)
    k, v = jnp.split(mem_n @ w_xkv, 2, axis=-1)
    k = k.reshape(B, M, XATTN_HEADS, XATTN_HEAD_DIM)
    v = v.reshape(B, M, XATTN_HEADS, XATTN_HEAD_DIM)
    p = jax.nn.softmax(jnp.einsum('bshd,bmhd->bhsm', q, k).astype(jnp.float32), axis=-1)
    o = jnp.einsum('bhsm,bmhd->bshd', p.astype(v.dtype), v).reshape(B, S, XATTN_WIDTH)
    return o @ w_xo

def conv_ffn(h, w_up, conv_w, conv_b, w_down):
    S = h.shape[1]
    u, g = jnp.split(h @ w_up, 2, axis=-1)
    u_pad = jnp.pad(u, ((0, 0), (CONV_WIDTH - 1, 0), (0, 0)))
    u = sum(conv_w[tap] * u_pad[:, tap:tap + S] for tap in range(CONV_WIDTH)) + conv_b
    return (jax.nn.gelu(u) * g) @ w_down

def second_inputs(seed: int = 0) -> dict:
    key = jax.random.key(seed)
    ks = jax.random.split(key, 28)
    f32 = jnp.float32
    L = DEPTH

    def dense(k, shape, fan_in):
        return jax.random.normal(k, shape, f32) * fan_in ** -0.5

    def gain(k, shape):
        return 1.0 + 0.02 * jax.random.normal(k, shape, f32)

    def small(k, shape, scale):
        return scale * jax.random.normal(k, shape, f32)

    return {
        "x": jax.random.normal(ks[0], (BATCH, SEQ, D_MODEL), f32),
        "mem": jax.random.normal(ks[1], (BATCH, MEM_LEN, D_MODEL), f32),
        "ln_mix_g": gain(ks[2], (L, D_MODEL)),
        "w_in": dense(ks[3], (L, D_MODEL, IN_WIDTH_2), D_MODEL),
        "nsa_gate_b": small(ks[4], (L, 3 * NSA_HEADS), 0.1),
        "cmp_pos_k": small(ks[5], (L, CMP_BLOCK, HEAD_DIM_2), 0.1),
        "cmp_w1_k": dense(ks[6], (L, CMP_BLOCK * HEAD_DIM_2, CMP_HIDDEN), CMP_BLOCK * HEAD_DIM_2),
        "cmp_w2_k": dense(ks[7], (L, CMP_HIDDEN, HEAD_DIM_2), CMP_HIDDEN),
        "cmp_pos_v": small(ks[8], (L, CMP_BLOCK, HEAD_DIM_2), 0.1),
        "cmp_w1_v": dense(ks[9], (L, CMP_BLOCK * HEAD_DIM_2, CMP_HIDDEN), CMP_BLOCK * HEAD_DIM_2),
        "cmp_w2_v": dense(ks[10], (L, CMP_HIDDEN, HEAD_DIM_2), CMP_HIDDEN),
        "gla_w_alpha2": dense(ks[11], (L, GLA_GATE_RANK, GLA_KEY_WIDTH), GLA_GATE_RANK),
        "gla_b_alpha": small(ks[12], (L, GLA_KEY_WIDTH), 0.1),
        "gla_norm_g": gain(ks[13], (L, GLA_DV)),
        "w_branch_nsa": dense(ks[14], (L, NSA_WIDTH, D_MODEL), NSA_WIDTH),
        "w_branch_gla": dense(ks[15], (L, GLA_VAL_WIDTH, D_MODEL), GLA_VAL_WIDTH),
        "w_out": dense(ks[16], (L, D_MODEL, D_MODEL), D_MODEL),
        "ln_x_g": gain(ks[17], (L, D_MODEL)),
        "ln_mem_g": gain(ks[18], (L, D_MODEL)),
        "w_xq": dense(ks[19], (L, D_MODEL, XATTN_WIDTH), D_MODEL),
        "w_xkv": dense(ks[20], (L, D_MODEL, 2 * XATTN_WIDTH), D_MODEL),
        "w_xo": dense(ks[21], (L, XATTN_WIDTH, D_MODEL), XATTN_WIDTH),
        "ln_ffn_g": gain(ks[22], (L, D_MODEL)),
        "w_up": dense(ks[23], (L, D_MODEL, 2 * FFN_DIM), D_MODEL),
        "conv_w": dense(ks[24], (L, CONV_WIDTH, FFN_DIM), CONV_WIDTH),
        "conv_b": small(ks[25], (L, FFN_DIM), 0.02),
        "w_down": dense(ks[26], (L, FFN_DIM, D_MODEL), FFN_DIM),
        "ln_final_g": gain(ks[27], (D_MODEL,)),
    }

def second_block(x, mem, ln_mix_g, w_in, nsa_gate_b, cmp_pos_k, cmp_w1_k, cmp_w2_k,
              cmp_pos_v, cmp_w1_v, cmp_w2_v, gla_w_alpha2, gla_b_alpha, gla_norm_g,
              w_branch_nsa, w_branch_gla, w_out, ln_x_g, ln_mem_g, w_xq, w_xkv, w_xo,
              ln_ffn_g, w_up, conv_w, conv_b, w_down, ln_final_g):
    split_points = np.cumsum(IN_SPLITS)[:-1].tolist()
    for l in range(DEPTH):
        h = rms_norm(x, ln_mix_g[l])
        q_a, kv_a, gate_a, q_b, k_b, v_b, r_b, alpha_b, merge = jnp.split(h @ w_in[l], split_points, axis=-1)
        kc, vc, ks_, vs_, kw, vw = jnp.split(kv_a, 6, axis=-1)
        o_nsa = nsa_attention(q_a, kc, vc, ks_, vs_, kw, vw, gate_a + nsa_gate_b[l],
                              cmp_pos_k[l], cmp_w1_k[l], cmp_w2_k[l],
                              cmp_pos_v[l], cmp_w1_v[l], cmp_w2_v[l])
        o_gla = gla(q_b, k_b, v_b, r_b, alpha_b, gla_w_alpha2[l], gla_b_alpha[l], gla_norm_g[l])
        g_nsa, g_gla = jnp.split(jax.nn.sigmoid(merge), 2, axis=-1)
        mix = g_nsa * (o_nsa @ w_branch_nsa[l]) + g_gla * (o_gla @ w_branch_gla[l])
        x = x + (mix @ w_out[l]).astype(x.dtype)
        mem_n = rms_norm(mem, ln_mem_g[l])
        x = x + memory_cross_attention(rms_norm(x, ln_x_g[l]), mem_n, w_xq[l], w_xkv[l], w_xo[l]).astype(x.dtype)
        x = x + conv_ffn(rms_norm(x, ln_ffn_g[l]), w_up[l], conv_w[l], conv_b[l], w_down[l]).astype(x.dtype)
    return rms_norm(x, ln_final_g)


def setup_inputs(seed=0):
    out = dict(first_inputs(seed))
    for name, value in second_inputs(seed + 1).items():
        if name != "x":
            out[name + "_2"] = value
    return out


def reference(
    x, positions, norm_attn_g, w_in, lam_q1, lam_k1, lam_q2, lam_k2, subln_g, w_pool,
    pool_scale, w_out, norm_mlp_g, w_up, w_down, final_norm_g, mem_2, ln_mix_g_2, w_in_2,
    nsa_gate_b_2, cmp_pos_k_2, cmp_w1_k_2, cmp_w2_k_2, cmp_pos_v_2, cmp_w1_v_2, cmp_w2_v_2,
    gla_w_alpha2_2, gla_b_alpha_2, gla_norm_g_2, w_branch_nsa_2, w_branch_gla_2, w_out_2,
    ln_x_g_2, ln_mem_g_2, w_xq_2, w_xkv_2, w_xo_2, ln_ffn_g_2, w_up_2, conv_w_2, conv_b_2,
    w_down_2, ln_final_g_2,
):
    x = first_block(
        x, positions, norm_attn_g, w_in, lam_q1, lam_k1, lam_q2, lam_k2, subln_g, w_pool,
        pool_scale, w_out, norm_mlp_g, w_up, w_down, final_norm_g,
    )
    return second_block(
        x, mem_2, ln_mix_g_2, w_in_2, nsa_gate_b_2, cmp_pos_k_2, cmp_w1_k_2, cmp_w2_k_2,
        cmp_pos_v_2, cmp_w1_v_2, cmp_w2_v_2, gla_w_alpha2_2, gla_b_alpha_2, gla_norm_g_2,
        w_branch_nsa_2, w_branch_gla_2, w_out_2, ln_x_g_2, ln_mem_g_2, w_xq_2, w_xkv_2, w_xo_2,
        ln_ffn_g_2, w_up_2, conv_w_2, conv_b_2, w_down_2, ln_final_g_2,
    )


_drawn_inputs = setup_inputs


def setup_inputs(seed=0):
    import zlib

    import numpy as np

    out = dict(_drawn_inputs(seed))
    spreads = {}
    factors = {'lam_k1': 3.466,
     'lam_q2': 3.657,
     'subln_g': 5.096,
     'norm_mlp_g': 2.691,
     'ln_mix_g_2': 3.661,
     'nsa_gate_b_2': 5.892,
     'cmp_pos_k_2': 8.0,
     'gla_b_alpha_2': 3.26,
     'gla_norm_g_2': 8.0,
     'ln_x_g_2': 8.0,
     'ln_mem_g_2': 8.0,
     'ln_ffn_g_2': 13.692,
     'conv_b_2': 18.196,
     'ln_final_g_2': 7.948,
     'cmp_pos_v_2': 3.666}
    for name, (base, spread) in spreads.items():
        noise = np.random.default_rng([zlib.crc32(name.encode()), seed]).standard_normal(out[name].shape)
        drawn = base * np.exp(spread * noise) if base else spread * noise
        out[name] = __import__('jax').numpy.asarray(drawn.astype(out[name].dtype))
    for name, factor in factors.items():
        out[name] = (out[name] * factor).astype(out[name].dtype)
    return out
```

```python
import math
from contextlib import ExitStack

import numpy as np
import concourse.bass as bass
from concourse import mybir

F32 = mybir.dt.float32
I32 = mybir.dt.int32
ALU = mybir.AluOpType
ACT = mybir.ActivationFunctionType
AX = mybir.AxisListType.X
EPS = 1e-6
NSLOT = 4
SLOT = 4096
ROPE_THETA = 500000.0
TWO_PI = 2.0 * math.pi
C1 = 6.28125
C2 = float(np.float32(np.round((TWO_PI - C1) * 2 ** 21) / 2 ** 21))
C3 = float(np.float32(TWO_PI - C1 - C2))
MAGIC = 12582912.0
FAR = 1e34

CONST = {}
_at = 0
for _name, _width in (("ident", 128), ("cm", 256), ("dist", 384), ("cdist", 30), ("cmask", 30), ("up", 128),
                      ("un", 128), ("reset", 256), ("freq", 8), ("pool", 1536)):
    CONST[_name] = (_at, _width)
    _at += _width
NCONST = _at


def shape_constants():
    c = np.zeros((128, NCONST), np.float32)

    def put(name, a):
        o, w = CONST[name]
        c[:, o:o + w] = np.asarray(a, np.float32).reshape(128, w)

    p = np.arange(128)
    put("ident", np.eye(128))
    causal = p[None, :] <= p[:, None]
    put("cm", np.concatenate([np.zeros((128, 128)), np.where(causal, 0.0, -1e30)], 1))
    d0 = np.where(causal, p[:, None] - p[None, :], FAR)
    d1 = np.where(np.arange(256)[None, :] <= p[:, None] + 128, p[:, None] + 128 - np.arange(256)[None, :], FAR)
    put("dist", np.concatenate([d0, d1], 1))
    end = np.arange(15) * 16 + 31
    t = p[:, None] + 128 * np.arange(2)[None, :]
    dc = t[:, :, None] - end
    put("cdist", np.where(dc >= 0, dc, FAR))
    put("cmask", dc >= 0)
    ok = (p[:, None] <= p[None, :]) & (p[:, None] // 64 == p[None, :] // 64)
    put("up", np.where(ok, 3.4028235e38, 0.0))
    put("un", np.where(ok, -3.4028235e38, 0.0))
    put("reset", np.broadcast_to((np.arange(256) % 64 != 0), (128, 256)))
    put("freq", np.broadcast_to(np.float32(ROPE_THETA) ** (-np.arange(0, 16, 2, dtype=np.float32) / 16), (128, 8)))
    pool = np.zeros((128, 4, 3, 128), np.float64)
    for g, w in enumerate((2, 4, 8, 16)):
        for n, (so, to) in enumerate(((0, 0), (0, 128), (128, 128))):
            s, tt = so + p[:, None], to + p[None, :]
            pool[:, g, n] = np.where((s <= tt) & (s > tt - w), 1.0 / np.minimum(tt + 1, w), 0.0) - (s == tt)
    put("pool", pool)
    return c


class Tok:

    def __init__(self, eng=None, sem=None, val=None):
        self.eng, self.sem, self.val, self.sig = eng, sem, val, False


class Prog:

    def __init__(self, nc, ctx):
        self.nc = nc
        self.ctx = ctx
        self.q = {e: [] for e in ("pe", "act", "dve", "pool", "sp")}
        self.sem = {e: ctx.enter_context(nc.semaphore("s_" + e)) for e in self.q}
        self.dmas = {}

    def put(self, eng, fn, after):
        t = Tok(eng=eng)
        self.q[eng].append((fn, tuple(after), t, None))
        return t

    def dma(self, eng, fns, after, sem):
        for fn in fns:
            self.dmas[sem] = self.dmas.get(sem, 0) + 16
            self.q[eng].append((fn, tuple(after), None, sem))
        return Tok(sem=sem, val=self.dmas[sem])

    def emit(self):
        for q in self.q.values():
            for _, after, _, _ in q:
                for t in after:
                    if t.sem is None:
                        t.sig = True
        for e, q in self.q.items():
            n = 0
            for _, _, t, _ in q:
                if t is not None and t.sig:
                    n += 1
                    t.val = n
        block = self.ctx.enter_context(self.nc.Block())

        def run(name):
            def body(eng):
                seen = {}
                for fn, after, t, dsem in self.q[name]:
                    need = {}
                    for a in after:
                        s = a.sem if a.sem is not None else self.sem[a.eng]
                        if a.val > seen.get(s, 0) and a.val > need.get(s, 0):
                            need[s] = a.val
                    for s, v in need.items():
                        eng.wait_ge(s, v)
                        seen[s] = v
                    if fn is None:
                        continue
                    ins = fn()
                    if dsem is not None:
                        ins.then_inc(dsem, 16)
                    elif t.sig:
                        ins.then_inc(self.sem[name], 1)
            return body

        block.tensor(run("pe"))
        block.scalar(run("act"))
        block.vector(run("dve"))
        block.gpsimd(run("pool"))
        block.sync(run("sp"))


class Bank:
    def __init__(self, ap):
        self.ap = ap
        self.free = []


class Banks:

    def __init__(self, aps):
        self.b = [Bank(a) for a in aps]
        self.n = 0

    def take(self):
        b = self.b[self.n % len(self.b)]
        self.n += 1
        return b


def two_blocks(nc, A, out):
    ctx = ExitStack()
    with ctx:
        P = Prog(nc, ctx)

        def sb(name, *shape, dt=F32):
            return ctx.enter_context(nc.sbuf_tensor(name, list(shape), dt))

        def sem(name):
            return ctx.enter_context(nc.semaphore(name))

        def mm(o, l, r, start, stop, after=()):
            return P.put("pe", lambda: nc.tensor.matmul(o, l, r, start=start, stop=stop,
                                                        skip_group_check=True), after)

        def tr(o, i, after=()):
            n = i.shape[0]
            return P.put("pe", lambda: nc.tensor.transpose(o, i, ident[0:n, 0:n]), after)

        def act(o, i, f, after=(), bias=0.0, scale=1.0, acc=None):
            if acc is None:
                return P.put("act", lambda: nc.scalar.activation(o, i, f, bias=bias, scale=scale), after)
            return P.put("act", lambda: nc.scalar.activation(o, i, f, bias=bias, scale=scale, accum_out=acc), after)

        def tt(o, a, b, op, after=()):
            return P.put("dve", lambda: nc.vector.tensor_tensor(o, a, b, op), after)

        def gtt(o, a, b, op, after=()):
            return P.put("pool", lambda: nc.gpsimd.tensor_tensor(o, a, b, op), after)

        def ts(o, a, s1, s2, op0, op1=None, after=()):
            if op1 is None:
                return P.put("dve", lambda: nc.vector.tensor_scalar(o, a, s1, None, op0), after)
            return P.put("dve", lambda: nc.vector.tensor_scalar(o, a, s1, s2, op0, op1), after)

        def stt(o, a, s, b, op0, op1, after=()):
            return P.put("dve", lambda: nc.vector.scalar_tensor_tensor(o, a, s, b, op0, op1), after)

        def cp(o, a, after=()):
            return P.put("dve", lambda: nc.vector.tensor_copy(o, a), after)

        def acp(o, a, after=()):
            return act(o, a, ACT.Copy, after)

        def rmax(o, a, after=()):
            return P.put("dve", lambda: nc.vector.reduce_max(o, a, AX), after)

        def rsum(o, a, after=()):
            return P.put("dve", lambda: nc.vector.reduce_sum(o, a, AX), after)

        def recip(o, a, after=()):
            return P.put("dve", lambda: nc.vector.reciprocal(o, a), after)

        def load(eng, name, *pairs, after=()):
            e = {"sp": nc.sync, "act": nc.scalar, "pool": nc.gpsimd}[eng]
            return P.dma(eng, [(lambda d=d, s=s: e.dma_start(d, s)) for d, s in pairs], after, sem("l_" + name))

        cst = sb("cst", 128, NCONST)

        def const(name):
            o, w = CONST[name]
            return cst[:, o:o + w]

        ident = const("ident")
        X = sb("X", 128, 2, 1024)
        XN = sb("XN", 128, 2, 1024)
        HT = sb("HT", 128, 8, 256)
        ring = [sb(f"ring{i}", 128, SLOT) for i in range(NSLOT)]
        grow = sb("grow", 128, 1024)
        psc = sb("psc", 128, 1024)
        subg = sb("subg", 128, 128)
        glag = sb("glag", 128, 128)
        gateb = sb("gateb", 128, 24)
        lamv = sb("lamv", 128, 4, 64)
        wpool = sb("wpool", 128, 4, 256)
        walp = sb("walp", 16, 256)
        w2 = sb("w2", 128, 3, 64)
        VR = sb("VR", 128, 2, 128)
        VC = sb("VC", 128, 2, 88)
        posi = sb("posi", 128, 2, dt=I32)
        st = sb("st", 128, 96)
        AR = sb("AR", 128, 18432)
        WK = sb("WK", 128, 4096)
        eps = sb("eps", 128, 2)

        def ar(off, *shape):
            n = int(np.prod(shape))
            assert off + n <= 18432, (off, shape)
            v = AR[:, off:off + n]
            if len(shape) == 1:
                return v
            names = "abcd"[:len(shape)]
            return v.rearrange("p (" + " ".join(names) + ") -> p " + " ".join(names),
                               **{names[k]: shape[k] for k in range(len(shape) - 1)})

        def wk(off, *shape):
            n = int(np.prod(shape))
            assert off + n <= 4096
            v = WK[:, off:off + n]
            if len(shape) == 1:
                return v
            names = "abcd"[:len(shape)]
            return v.rearrange("p (" + " ".join(names) + ") -> p " + " ".join(names),
                               **{names[k]: shape[k] for k in range(len(shape) - 1)})

        PS = ctx.enter_context(nc.psum_tensor("PS", [128, 8, 512], F32))
        big = Banks([PS[:, i, :] for i in range(4)])
        scb = Banks([PS[:, 4:6, :]])
        tpb = Banks([PS[:, 6, :]])
        ob = Banks([PS[:, 7, :]])

        slots = [{"sem": sem(f"ring_s{i}"), "free": []} for i in range(NSLOT)]
        state = {"n": 0, "ev": 0}

        def chunk(*pairs):
            k = state["n"] % NSLOT
            state["n"] += 1
            s = slots[k]
            ap = ring[k]
            assert state["n"] <= NSLOT or s["free"], "slot not released"
            t = P.dma("sp", [(lambda d=f(ap), src=src: nc.sync.dma_start(d, src)) for f, src in pairs],
                      s["free"], s["sem"])
            s["free"] = []
            return ap, t, s

        def v3(ap, K, n):
            return ap[:, 0:K * n].rearrange("p (k n) -> p k n", k=K)

        def wcols(w, c0, n):
            K = w.shape[0] // 128
            ap, t, s = chunk((lambda a: v3(a, K, n), w[:, c0:c0 + n].rearrange("(k p) n -> p k n", p=128)))
            return v3(ap, K, n), t, s

        def wrows(w, k0, K):
            n = w.shape[1]
            ap, t, s = chunk((lambda a: v3(a, K, n),
                              w[k0 * 128:(k0 + K) * 128, :].rearrange("(k p) n -> p k n", p=128)))
            return v3(ap, K, n), t, s

        def evac(o, a, after, scale=None):
            state["ev"] ^= 1
            return acp(o, a, after) if state["ev"] else cp(o, a, after)

        def natural(w, t, hT, i, c0, n, after):
            b = big.take()
            K = w.shape[1]
            for k in range(K):
                m = mm(b.ap[:, 0:n], hT[:, k, i * 128:i * 128 + 128], w[:, k, c0:c0 + n], k == 0, k == K - 1,
                       [t, *after, *b.free] if k == 0 else [])
            return b, m

        def turned(cols, t, hT, o, b, K, after, n=256):
            for k in range(K):
                m = mm(o, cols(k), hT[:, k, 0:n], k == 0, k == K - 1, [t, *after, *b.free] if k == 0 else [])
            return m

        t_x = load("sp", "x", (X[:], A["x"][0].rearrange("(i p) d -> p i d", p=128)))
        t_cst = load("act", "cst", (cst[:], A["shape_constants"]))

        def rows(v, k):
            return v.rearrange("(k p) -> k p", p=128)

        vr0 = [("norm_attn_g", 0, 8), ("norm_mlp_g", 8, 8), ("ln_mix_g_2", 16, 8), ("ln_x_g_2", 24, 8),
               ("ln_mem_g_2", 32, 8), ("ln_ffn_g_2", 40, 8), ("conv_b_2", 48, 22), ("gla_b_alpha_2", 70, 2)]
        pairs = [(VR[o:o + n, 0, :], rows(A[nm][0], n)) for nm, o, n in vr0]
        pairs.append((VR[72:88, 0, :], A["cmp_pos_k_2"][0].rearrange("(j e) d -> j (e d)", e=2)))
        for tap in range(3):
            pairs.append((VR[22 * tap:22 * tap + 22, 1, :], rows(A["conv_w_2"][0, tap], 22)))
        pairs.append((VR[66:82, 1, :], A["cmp_pos_v_2"][0].rearrange("(j e) d -> j (e d)", e=2)))
        t_vr = load("act", "vr", *pairs)
        t_pos = P.dma("act", [lambda: nc.scalar.dma_start(posi[:], A["positions"][0].rearrange("(i p) -> p i", p=128), allow_slow_non_contiguous=True)], [], sem("l_pos"))
        t_lam = load("act", "lam", *[(lamv[:, j, :], A[nm][0:1].broadcast_to([128, 64]))
                                     for j, nm in enumerate(("lam_q1", "lam_k1", "lam_q2", "lam_k2"))])
        t_bc = load("act", "bc", (subg[:], A["subln_g"][0:1].broadcast_to([128, 128])),
                    (glag[:], A["gla_norm_g_2"][0:1].broadcast_to([128, 128])),
                    (gateb[:], A["nsa_gate_b_2"][0:1].broadcast_to([128, 24])),
                    (psc[:], A["pool_scale"][0:1].broadcast_to([128, 1024])))
        t_grow = load("act", "grow", (grow[:], A["final_norm_g"].rearrange("(a n) -> a n", a=1)
                                      .broadcast_to([128, 1024])))
        t_ws = load("act", "ws", (wpool[:], A["w_pool"][0].rearrange("g c d -> c g d")),
                    (walp[:], A["gla_w_alpha2_2"][0]),
                    (w2[:, 0, :], A["cmp_w2_k_2"][0]), (w2[:, 1, :], A["cmp_w2_k_2"][0]),
                    (w2[:, 2, :], A["cmp_w2_v_2"][0]))

        t_eps = P.put("dve", lambda: nc.vector.memset(eps[:, 0:1], 1.0), ())
        b = tpb.take()
        m1 = tr(b.ap[:, 0:88], VR[0:88, 0, :], [t_cst, t_vr])
        m2 = tr(b.ap[:, 128:210], VR[0:82, 1, :])
        t_vc0 = cp(VC[:, 0, 0:88], b.ap[:, 0:88], [m2])
        t_vc = cp(VC[:, 1, 0:82], b.ap[:, 128:210])
        b.free = [t_vc]
        G_ATT, G_MLP, G_MIX, G_X, G_MEM, G_FFN = (VC[:, 0, 8 * j:8 * j + 8] for j in range(6))
        CB = VC[:, 0, 48:70]
        BA = VC[:, 0, 70:72]
        POS = (VC[:, 0, 72:88], VC[:, 1, 66:82])

        def rms_rows(x, i, xn, after, s0):
            a = act(xn, x, ACT.Square, after, acc=st[:, s0:s0 + 1])
            d = ts(st[:, s0 + 1:s0 + 2], st[:, s0:s0 + 1], 1.0 / 1024, EPS, ALU.mult, ALU.add, [a])
            d = recip(st[:, s0 + 2:s0 + 3], st[:, s0 + 1:s0 + 2], [d])
            a = act(st[:, s0 + 3:s0 + 4], st[:, s0 + 2:s0 + 3], ACT.Sqrt, [d])
            return ts(xn, x, st[:, s0 + 3:s0 + 4], None, ALU.mult, after=[a])

        def turn(src, dst, n, i, gain, after, free, pool=None):
            out_t = []
            pool = pool or big
            for k0 in range(0, n, 4):
                b = pool.take()
                kk = min(4, n - k0)
                for k in range(kk):
                    m = tr(b.ap[:, 128 * k:128 * k + 128], src(k0 + k), [*after, *b.free, t_cst] if k == 0 else [])
                v = b.ap[:, 0:128 * kk].rearrange("p (k n) -> p k n", k=kk)
                o = dst[:, k0:k0 + kk, i * 128:i * 128 + 128]
                if gain is None:
                    e = evac(o, v, [m, *free])
                else:
                    e = tt(o, v, gain[:, k0:k0 + kk].unsqueeze(2).broadcast_to([128, kk, 128]), ALU.mult,
                           [m, t_vc0, *free])
                b.free = [e]
                out_t.append(e)
            return out_t

        def norm_turn(x, after, gain, dst, free=()):
            res = []
            for i in range(2):
                d = rms_rows(x[:, i, :], i, XN[:, i, :], [*after, *free], 4 * i)
                res += turn(lambda k: XN[:, i, 128 * k:128 * k + 128], dst, 8, i, gain, [d], free)
            return res

        Q = ar(0, 2, 1024)
        Kn = ar(2048, 2, 1024)
        QT = ar(4096, 8, 256)
        KT = ar(6144, 8, 256)
        V = ar(8192, 2, 1024)
        UP = ar(10240, 2, 512)
        DT = ar(11264, 4, 256)
        GT = ar(12288, 2, 2048)
        cs = ar(16384, 2, 4, 8)
        rt = ar(16448, 2, 2, 16, 8)

        ang = ar(16960, 2, 2, 8)
        d = cp(st[:, 8:10], posi[:], [t_pos, t_cst])
        freq = const("freq")
        red = []
        for i in range(2):
            u, k, r = ang[:, i, 0, :], ang[:, i, 1, :], cs[:, i, :, :]
            du = ts(u, freq, st[:, 8 + i:9 + i], None, ALU.mult, after=[d])
            for j, (sh, add) in enumerate(((0.0, 0.0), (0.25, math.pi / 2))):
                a = ts(k, u, 1.0 / TWO_PI, sh, ALU.mult, ALU.add, after=[du])
                a = ts(k, k, MAGIC, -MAGIC, ALU.add, ALU.add, after=[a])
                a = stt(r[:, 2 + j, :], k, -C1, u, ALU.mult, ALU.add, after=[a])
                a = stt(r[:, 2 + j, :], k, -C2, r[:, 2 + j, :], ALU.mult, ALU.add, after=[a])
                a = stt(r[:, 2 + j, :], k, -C3, r[:, 2 + j, :], ALU.mult, ALU.add, after=[a])
                a = ts(r[:, 2 + j, :], r[:, 2 + j, :], add, math.pi, ALU.add, ALU.min, after=[a])
                a = ts(r[:, 2 + j, :], r[:, 2 + j, :], -math.pi, None, ALU.max, after=[a])
                du = a
            d = a
            red.append(a)
        t_cs = act(cs[:, :, 0:2, :], cs[:, :, 2:4, :], ACT.Sin, red)
        lm = st[:, 16:32]
        junk = ar(17024, 4, 64)
        d = tt(junk[:, 0, :], lamv[:, 0, :], lamv[:, 1, :], ALU.mult, [t_lam])
        d2 = tt(junk[:, 1, :], lamv[:, 2, :], lamv[:, 3, :], ALU.mult)
        d = rsum(lm[:, 0:2], junk[:, 0:2, :], [d2])
        a = act(lm[:, 2:4], lm[:, 0:2], ACT.Exp, [d])
        t_nlam = stt(lm[:, 4:5], lm[:, 3:4], -(0.8 - 0.6 * math.exp(0.0)), lm[:, 2:3], ALU.add, ALU.subtract, [a])
        nlam = lm[:, 4:5]

        t_h = norm_turn(X, [t_x], G_ATT, HT)

        w_in = A["w_in"][0]

        def rope(buf, i, after):
            v = buf[:, i, :].rearrange("p (m d) -> p m d", d=64)
            t1, t2 = v[:, :, 0:8], v[:, :, 8:16]
            s = cs[:, i, 0, :].unsqueeze(1).broadcast_to([128, 16, 8])
            c = cs[:, i, 1, :].unsqueeze(1).broadcast_to([128, 16, 8])
            a = tt(rt[:, 0, 0], t1, s, ALU.mult, [*after, t_cs])
            b = tt(rt[:, 0, 1], t2, s, ALU.mult)
            c1 = tt(t1, t1, c, ALU.mult, [b])
            c2 = tt(t2, t2, c, ALU.mult)
            e1 = tt(t1, t1, rt[:, 0, 1], ALU.subtract, [c2])
            return [e1, tt(t2, t2, rt[:, 0, 0], ALU.add)]

        def project_natural(w, c0, n, dst, after, fn=None, cc=0):
            wv, t, s = wcols(w, c0, n)
            res = []
            for i in range(2):
                b, m = natural(wv, t, HT, i, 0, n, after)
                s["free"].append(m)
                e = (fn or evac)(dst[:, i, cc:cc + n], b.ap[:, 0:n], [m])
                b.free = [e]
                res.append(e)
            return res

        e_q = [project_natural(w_in, 512 * j, 512, Q, t_h, cc=512 * j) for j in range(2)]
        e_k = [project_natural(w_in, 1024 + 512 * j, 512, Kn, t_h, cc=512 * j) for j in range(2)]
        t_qT, t_kT = [], []
        for i in range(2):
            r = rope(Q, i, [e_q[0][i], e_q[1][i]])
            t_qT.append(turn(lambda k: Q[:, i, 128 * k:128 * k + 128], QT, 8, i, None, r, []))
            r = rope(Kn, i, [e_k[0][i], e_k[1][i]])
            t_kT.append(turn(lambda k: Kn[:, i, 128 * k:128 * k + 128], KT, 8, i, None, r, []))
        e_v = [project_natural(w_in, 2048 + 512 * j, 512, V, t_h, cc=512 * j) for j in range(2)]
        e_p = project_natural(w_in, 3072, 512, UP, t_h)

        def softmax_pairs(s, n, scale, after, o):
            mx, sm = st[:, o:o + n], st[:, o + n:o + 2 * n]
            d = rmax(mx, s, after)
            d = ts(mx, mx, -scale, None, ALU.mult, after=[d])
            for j in range(n):
                a = act(s[:, j, :], s[:, j, :], ACT.Exp, [d] if j == 0 else [], bias=mx[:, j:j + 1],
                        scale=scale, acc=sm[:, j:j + 1])
            return a

        cm = const("cm")
        AN = Q
        wk_free = [[], []]
        st_free = [[], []]
        wt_free = [[], []]
        e_a = {}

        def attn1():
            n = 0
            for i in range(2):
                kend = 128 * (i + 1)
                for hp in range(4):
                    par = n % 2
                    n += 1
                    S = wk(1024 * par, 4, 256)[:, :, 0:kend]
                    b = scb.take()
                    bv = b.ap.rearrange("p c (h n) -> p c h n", h=2)
                    for hh in range(2):
                        for c in range(2):
                            h = 2 * hp + hh
                            m = mm(bv[:, c, hh, 0:kend], QT[64 * c:64 * c + 64, h, i * 128:i * 128 + 128],
                                   KT[64 * c:64 * c + 64, h, 0:kend], True, True,
                                   [*b.free, *t_qT[i], *t_kT[0], *t_kT[i]])
                    sv = bv.rearrange("p c h n -> p (c h) n")[:, :, 0:kend]
                    d = tt(S, sv, cm[:, 256 - kend:256].unsqueeze(1).broadcast_to([128, 4, kend]), ALU.add,
                           [m, *wk_free[par]])
                    b.free = [d]
                    yield
                    o = 32 + 8 * par
                    a = softmax_pairs(S, 4, 0.125, [d], o)
                    r = st[:, 48 + 4 * par:52 + 4 * par]
                    d = recip(r, st[:, o + 4:o + 8], [a])
                    d = ts(r[:, 2:4], r[:, 2:4], nlam, None, ALU.mult, after=[d, t_nlam])
                    for hh in range(2):
                        d1 = ts(S[:, hh, :], S[:, hh, :], r[:, hh:hh + 1], None, ALU.mult, after=[d])
                    for hh in range(2):
                        d = stt(S[:, hh, :], S[:, 2 + hh, :], r[:, 2 + hh:3 + hh], S[:, hh, :], ALU.mult, ALU.add,
                                [d1] if hh == 0 else [])
                    yield
                    nk = i + 1
                    b = tpb.take()
                    for hh in range(2):
                        for kt in range(nk):
                            j = hh * nk + kt
                            m = tr(b.ap[:, 128 * j:128 * j + 128], S[:, hh, 128 * kt:128 * kt + 128],
                                   [d, *b.free] if j == 0 else [])
                    wT = wk(2048 + 512 * par, 512)
                    e = acp(wT[:, 0:256 * nk], b.ap[:, 0:256 * nk], [m, *wt_free[par]])
                    b.free = [e]
                    wk_free[par] = [m]
                    yield
                    b = ob.take()
                    for hh in range(2):
                        for kt in range(nk):
                            j = hh * nk + kt
                            h = 2 * hp + hh
                            m = mm(b.ap[:, 128 * hh:128 * hh + 128], wT[:, 128 * j:128 * j + 128],
                                   V[:, kt, 128 * h:128 * h + 128], kt == 0, kt == nk - 1,
                                   [e, *b.free, *e_v[0], *e_v[1]] if j == 0 else [])
                    wt_free[par] = [m]
                    e = cp(AN[:, i, 256 * hp:256 * hp + 256], b.ap[:, 0:256], [m])
                    b.free = [e]
                    e_a.setdefault(i, []).append(e)
                    yield

        e_g = []

        def sig_part(o, a, after):
            return act(o, a, ACT.Tanh, after, scale=0.5)

        def gates1():
            for j in range(4):
                wv, t, s = wcols(w_in, 3584 + 512 * j, 512)
                for i in range(2):
                    b, m = natural(wv, t, HT, i, 0, 512, t_h)
                    s["free"].append(m)
                    g = GT[:, i, 512 * j:512 * j + 512]
                    e = sig_part(g, b.ap, [m])
                    b.free = [e]
                    e_g.append(ts(g, g, 0.5, 0.5, ALU.mult, ALU.add, after=[e]))
                    yield

        def weave(main, fill, ratio):
            acc = 0.0
            for _ in main:
                acc += ratio
                while acc >= 1.0:
                    acc -= 1.0
                    next(fill, None)
            for _ in fill:
                pass

        def pool_branch():
            pm = const("pool").rearrange("p (g n t) -> p g n t", g=4, n=3)
            for g in range(4):
                b = big.take()
                u = [UP[:, i, 128 * g:128 * g + 128] for i in range(2)]
                mm(b.ap[:, 0:128], u[0], pm[:, g, 0, :], True, True, [*e_p, *b.free])
                mm(b.ap[:, 128:256], u[0], pm[:, g, 1, :], True, False)
                m = mm(b.ap[:, 128:256], u[1], pm[:, g, 2, :], False, True)
                e = evac(DT[:, g, :], b.ap[:, 0:256], [m])
                b.free = [e]
                yield e

        e_d = list(pool_branch())
        weave(attn1(), gates1(), 0.25)

        MG = Kn
        e_m = []
        for i in range(2):
            av = AN[:, i, :].rearrange("p (h d) -> p h d", h=8)
            sq = wk(2048 * i, 8, 128)
            s8 = st[:, 64 + 16 * i:80 + 16 * i]
            d = tt(sq, av, av, ALU.mult, [*e_a[i], *wk_free[0], *wk_free[1], *wt_free[0], *wt_free[1]])
            d = rsum(s8[:, 0:8], sq, [d])
            d = ts(s8[:, 0:8], s8[:, 0:8], 1.0 / 128, EPS, ALU.mult, ALU.add, after=[d])
            d = recip(s8[:, 8:16], s8[:, 0:8], [d])
            lam_init = 0.8 - 0.6 * math.exp(0.0)
            a = act(s8[:, 0:8], s8[:, 8:16], ACT.Sqrt, [d], scale=(1.0 - lam_init) ** 2)
            d = tt(av, av, s8[:, 0:8].unsqueeze(2).broadcast_to([128, 8, 128]), ALU.mult, [a])
            d = tt(av, av, subg[:].unsqueeze(1).broadcast_to([128, 8, 128]), ALU.mult, [d, t_bc])
            d_a = tt(AN[:, i, :], AN[:, i, :], GT[:, i, 0:1024], ALU.mult, [d, *e_g])
            parts = []
            for g2 in range(2):
                b = big.take()
                for gg in range(2):
                    g = 2 * g2 + gg
                    m = mm(b.ap[:, 256 * gg:256 * gg + 256], DT[:, g, i * 128:i * 128 + 128], wpool[:, g, :],
                           True, True, [*e_d, *b.free, t_ws])
                o = MG[:, i, 512 * g2:512 * g2 + 512]
                e = tt(o, b.ap, psc[:, 512 * g2:512 * g2 + 512], ALU.mult, [m, t_bc, *t_kT[0], *t_kT[1]])
                b.free = [e]
                d = tt(o, o, GT[:, i, 1024 + 512 * g2:1536 + 512 * g2], ALU.mult, [e, *e_g])
                parts.append(d)
            e_m.append(tt(MG[:, i, :], MG[:, i, :], AN[:, i, :], ALU.add, [*parts, d_a]))
        MT = QT
        t_mT = []
        for i in range(2):
            t_mT += turn(lambda k: MG[:, i, 128 * k:128 * k + 128], MT, 8, i, None, [e_m[i]], wt_free[0] + wt_free[1])

        def residual_natural(w, hT, after):
            res = []
            for j in range(2):
                wv, t, s = wcols(w, 512 * j, 512)
                for i in range(2):
                    b, m = natural(wv, t, hT, i, 0, 512, after)
                    s["free"].append(m)
                    xo = X[:, i, 512 * j:512 * j + 512]
                    e = tt(xo, b.ap, xo, ALU.add, [m])
                    b.free = [e]
                    res.append(e)
            return res

        t_x1 = residual_natural(A["w_out"][0], MT, t_mT)
        t_h2 = norm_turn(X, t_x1, G_MLP, HT)

        ZT = ar(0, 32, 256)
        z_t = []
        w_up = A["w_up"][0]
        for j in range(8):
            wv, t, s = wcols(w_up, 512 * j, 512)
            for mp in range(2):
                b = big.take()
                for h in range(2):
                    c = 256 * mp + 128 * h
                    m = turned(lambda k: wv[:, k, c:c + 128], t, HT, b.ap[:, 256 * h:256 * h + 256], b, 8, t_h2)
                s["free"].append(m)
                zi = 4 * j + 2 * mp
                o = ZT[:, zi:zi + 2, :]
                bv = b.ap.rearrange("p (a n) -> p a n", a=2)
                a = act(o, bv, ACT.Relu, [m, *t_mT, *t_x1])
                b.free = [a]
                z_t.append(tt(o, o, o, ALU.mult, [a]))

        def residual_rows(w, hT, ntile, z_of, after=()):
            bs = [big.take() for _ in range(4)]
            for b in bs:
                b.open = True
            for k0 in range(0, ntile, 4):
                K = min(4, ntile - k0)
                wv, t, s = wrows(w, k0, K)
                for i in range(2):
                    for j in range(2):
                        b = bs[2 * i + j]
                        for k in range(K):
                            kk = k0 + k
                            m = mm(b.ap, hT[:, kk, i * 128:i * 128 + 128], wv[:, k, 512 * j:512 * j + 512],
                                   kk == 0, kk == ntile - 1,
                                   [t, *z_of(kk), *after, *(b.free if kk == 0 else [])])
                        b.last = m
                s["free"].append(m)
            res = []
            for i in range(2):
                for j in range(2):
                    b = bs[2 * i + j]
                    xo = X[:, i, 512 * j:512 * j + 512]
                    e = tt(xo, b.ap, xo, ALU.add, [b.last])
                    b.free = [e]
                    res.append(e)
            return res

        t_x2 = residual_rows(A["w_down"][0], ZT, 32, lambda kk: [z_t[kk // 2]])

        t_xf = []
        for i in range(2):
            d = rms_rows(X[:, i, :], i, XN[:, i, :], t_x2, 4 * i)
            t_xf.append(tt(X[:, i, :], XN[:, i, :], grow[:], ALU.mult, [d, t_grow]))
        t_grow2 = load("act", "grow2", (grow[:], A["ln_final_g_2"].rearrange("(a n) -> a n", a=1)
                                        .broadcast_to([128, 1024])), after=t_xf)

        QA = ar(0, 4, 256)
        KSW = ar(1024, 2, 256)
        VSW = ar(1536, 2, 2, 128)
        XC = ar(2048, 2, 256)
        Z = ar(2560, 2, 16, 30)
        GN = ar(3520, 2, 24)
        AL = ar(3584, 256)
        QB = ar(4096, 2, 256)
        KB = ar(4608, 2, 256)
        EB = ar(5120, 2, 256)
        EN = ar(5632, 2, 256)
        EL = ar(6144, 2, 256)
        VB = ar(6656, 2, 512)
        RB = ar(7680, 2, 512)
        MRG = ar(8704, 16, 256)
        MEMT = ar(8704, 8, 256)
        MEM = ar(10752, 2, 1024)
        KX = ar(12800, 4, 256)
        VX = ar(13824, 2, 512)
        ONT = ar(14848, 4, 256)
        OGT = ar(15872, 4, 256)
        OG = ar(16896, 2, 512)

        t_mem = load("act", "mem", (MEM, A["mem_2"][0].rearrange("(i p) d -> p i d", p=128)), after=t_x2)
        t_mt = norm_turn(MEM, [t_mem, *t_xf], G_MEM, MEMT)
        wv, t, s = wcols(A["w_xkv_2"][0], 0, 512)
        t_kx = []
        for mp in range(2):
            b = big.take()
            for h in range(2):
                c = 256 * mp + 128 * h
                m = turned(lambda k: wv[:, k, c:c + 128], t, MEMT, b.ap[:, 256 * h:256 * h + 256], b, 8, t_mt)
            e = evac(KX[:, 2 * mp:2 * mp + 2, :], b.ap.rearrange("p (a n) -> p a n", a=2), [m])
            s["free"].append(m)
            b.free = [e]
            t_kx.append(e)
        wv, t, s = wcols(A["w_xkv_2"][0], 512, 512)
        t_vx = []
        for i in range(2):
            b, m = natural(wv, t, MEMT, i, 0, 512, t_mt)
            s["free"].append(m)
            e = evac(VX[:, i, :], b.ap, [m])
            b.free = [e]
            t_vx.append(e)
        t_memdone = m

        t_h = norm_turn(X, t_xf, G_MIX, HT, free=t_mt)
        w_in = A["w_in_2"][0]
        ap, t, s = chunk(*[(lambda a, k=k, v=v: v3(a, 8, 512)[:, k, :].rearrange("p (g v d) -> p g v d", g=4, v=2)[:, :, v],
                            w_in[128 * k:128 * k + 128, 256 * v:256 * v + 256].rearrange("p (g d) -> p g d", g=4))
                           for k in range(8) for v in range(2)])
        wv = v3(ap, 8, 512)
        t_qa = []
        for mp in range(2):
            b = big.take()
            for h in range(2):
                g = 2 * mp + h
                m = turned(lambda k: wv[:, k, 128 * g:128 * g + 128], t, HT,
                           b.ap[:, 256 * h:256 * h + 256], b, 8, t_h)
            e = P.put("act", lambda b=b, mp=mp: nc.scalar.activation(
                QA[:, 2 * mp:2 * mp + 2, :], b.ap.rearrange("p (a n) -> p a n", a=2), ACT.Copy, scale=0.125), [m])
            s["free"].append(m)
            b.free = [e]
            t_qa.append(e)
        wv, t, s = wcols(w_in, 512, 512)
        w1t = chunk((lambda a: a[:, 0:2048].rearrange("p (j n) -> p j n", j=16),
                     A["cmp_w1_k_2"][0].rearrange("(j p) n -> p j n", p=128)),
                    (lambda a: a[:, 2048:4096].rearrange("p (j n) -> p j n", j=16),
                     A["cmp_w1_v_2"][0].rearrange("(j p) n -> p j n", p=128)))
        t_z = []
        z_prev = []
        for c in range(2):
            b = big.take()
            m = turned(lambda k: wv[:, k, 128 * c:128 * c + 128], t, HT, b.ap[:, 0:256], b, 8, t_h)
            kct = ar(4096 + 256 * c, 256)
            e = evac(kct, b.ap[:, 0:256], [m])
            b.free = [e]
            e2 = load("pool", f"xc{c}", *[pr for h in range(2) for pr in (
                (XC[0:64, h, :], kct[64 * h:64 * h + 64, :]),
                (XC[64:128, h, 0:255], kct[64 * h:64 * h + 64, 1:256]))], after=[e, *z_prev])
            for h in range(2):
                for half in range(2):
                    sv = XC[:, h, 16 * half:16 * half + 240].rearrange("p (n j e) -> p j n e", n=15, j=8)[:, :, :, 0]
                    d = tt(Z[:, c, 8 * half:8 * half + 8, 15 * h:15 * h + 15], sv,
                           POS[c][:, 8 * half:8 * half + 8].unsqueeze(2).broadcast_to([128, 8, 15]), ALU.add,
                           [e2, t_vc])
            t_z.append(d)
            z_prev = [d]
        b = big.take()
        m = turned(lambda k: wv[:, k, 256:384], t, HT, b.ap[:, 0:256], b, 8, t_h)
        e_ks = evac(KSW[:, 0, :], b.ap[:, 0:256], [m])
        b.free = [e_ks]
        b = big.take()
        for i in range(2):
            for k in range(8):
                m = mm(b.ap[:, 128 * i:128 * i + 128], HT[:, k, i * 128:i * 128 + 128], wv[:, k, 384:512],
                       k == 0, k == 7, b.free)
        s["free"].append(m)
        e_vs = evac(VSW[:, 0], b.ap[:, 0:256].rearrange("p (a n) -> p a n", a=2), [m])
        b.free = [e_vs]
        ap, t, s = chunk((lambda a: v3(a, 8, 296)[:, :, 0:280],
                          w_in[:, 1024:1304].rearrange("(k p) n -> p k n", p=128)),
                         (lambda a: v3(a, 8, 296)[:, :, 280:296],
                          w_in[:, 2840:2856].rearrange("(k p) n -> p k n", p=128)))
        wv = v3(ap, 8, 296)
        b = big.take()
        m = turned(lambda k: wv[:, k, 0:128], t, HT, b.ap[:, 0:256], b, 8, t_h)
        e_kw = evac(KSW[:, 1, :], b.ap[:, 0:256], [m])
        b.free = [e_kw]
        b = big.take()
        for i in range(2):
            for k in range(8):
                m = mm(b.ap[:, 160 * i:160 * i + 152], HT[:, k, i * 128:i * 128 + 128], wv[:, k, 128:280],
                       k == 0, k == 7, b.free)
        bv = b.ap[:, 0:320].rearrange("p (a n) -> p a n", a=2)
        e_vw = cp(VSW[:, 1], bv[:, :, 0:128], [m])
        d = tt(GN[:], bv[:, :, 128:152], gateb[:].unsqueeze(1).broadcast_to([128, 2, 24]), ALU.add, [t_bc])
        b.free = [d]
        a = sig_part(GN[:], GN[:], [d])
        t_gn = ts(GN[:], GN[:], 0.5, 0.5, ALU.mult, ALU.add, after=[a])
        b = big.take()
        m = turned(lambda k: wv[:, k, 280:296], t, HT, b.ap[0:16, 0:256], b, 8, t_h)
        s["free"].append(m)
        e_al = evac(AL[0:16, :], b.ap[0:16, 0:256], [m])
        b.free = [e_al]
        KC = ar(3840, 2, 15)
        VC2 = ar(3872, 2, 64)
        HC = ar(17920, 2, 30)
        w1ap, t_w1, s_w1 = w1t
        t_c = []
        for c in range(2):
            w1v = w1ap[:, 2048 * c:2048 * c + 2048].rearrange("p (j n) -> p j n", j=16)
            b = big.take()
            for j in range(16):
                m = mm(b.ap[:, 0:30], w1v[:, j, :], Z[:, c, j, :], j == 0, j == 15,
                       [t_w1, t_z[c], *b.free] if j == 0 else [])
            s_w1["free"].append(m)
            x_, y_ = HC[:, c, :], ar(17984 + 32 * c, 30)
            e = cp(x_, b.ap[:, 0:30], [m])
            b.free = [e]
            d = tt(y_, x_, x_, ALU.mult, [e])
            d = ts(y_, y_, 0.044715, 1.0, ALU.mult, ALU.add, after=[d])
            d = tt(y_, y_, x_, ALU.mult, [d])
            a = act(y_, y_, ACT.Tanh, [d], scale=math.sqrt(2.0 / math.pi))
            d = ts(y_, y_, 0.5, 0.5, ALU.mult, ALU.add, after=[a])
            t_g = tt(x_, x_, y_, ALU.mult, [d])
            b = big.take()
            if c == 0:
                m = mm(b.ap[:, 0:30], w2[:, 0:2, :].rearrange("p a d -> p (a d)"), x_, True, True,
                       [t_g, t_ws, *b.free])
                e = cp(KC[0:64, 0, :], b.ap[0:64, 0:15], [m])
                e = cp(KC[64:128, 0, :], b.ap[64:128, 15:30])
            else:
                for h in range(2):
                    m = mm(b.ap[0:15, 64 * h:64 * h + 64], x_[:, 15 * h:15 * h + 15], w2[:, 2, :], True, True,
                           [t_g, t_ws, *b.free])
                e = cp(VC2[0:15], b.ap[0:15, 0:128].rearrange("p (h d) -> p h d", h=2), [m])
            b.free = [e]
            t_c.append(e)

        wv, t, s = wcols(w_in, 1304, 512)
        e_qk = []
        for mp, dst in enumerate((QB, KB)):
            b = big.take()
            for h in range(2):
                c = 256 * mp + 128 * h
                m = turned(lambda k: wv[:, k, c:c + 128], t, HT, b.ap[:, 256 * h:256 * h + 256], b, 8, t_h)
            e = evac(dst[:], b.ap.rearrange("p (a n) -> p a n", a=2), [m])
            s["free"].append(m)
            b.free = [e]
            e_qk.append(e)
        e_vb = project_natural(w_in, 1816, 512, VB, t_h)
        e_rb = project_natural(w_in, 2328, 512, RB, t_h)

        e_mg = []

        def merges():
            for j in range(4):
                wv, t, s = wcols(w_in, 2856 + 512 * j, 512)
                for mp in range(2):
                    b = big.take()
                    for h in range(2):
                        c = 256 * mp + 128 * h
                        m = turned(lambda k: wv[:, k, c:c + 128], t, HT, b.ap[:, 256 * h:256 * h + 256], b, 8,
                                   t_h)
                    s["free"].append(m)
                    o = MRG[:, 4 * j + 2 * mp:4 * j + 2 * mp + 2, :]
                    e = sig_part(o, b.ap.rearrange("p (a n) -> p a n", a=2), [m, t_memdone])
                    b.free = [e]
                    e_mg.append(ts(o, o, 0.5, 0.5, ALU.mult, ALU.add, after=[e]))
                    yield

        dist = const("dist")
        cdist = const("cdist").rearrange("p (i n) -> p i n", i=2)
        cmask = const("cmask").rearrange("p (i n) -> p i n", i=2)
        e_on = []

        def nsa():
            nonlocal wk_free, wt_free
            wk_free = [list(e_m), list(e_m)]
            wt_free = [list(e_m), list(e_m)]
            n = 0
            pc_all = wk(3328, 8, 16)
            for g in range(4):
                for i in range(2):
                    kend = 128 * (i + 1)
                    nk = i + 1
                    par = n % 2
                    n += 1
                    S = wk(1024 * par, 4, 256)
                    b = scb.take()
                    bv = b.ap.rearrange("p c (h n) -> p c h n", h=2)
                    b2 = (ob.take(), tpb.take())
                    for v in range(2):
                        q = QA[64 * v:64 * v + 64, g, i * 128:i * 128 + 128]
                        for br in range(2):
                            m = mm(bv[:, v, br, 0:kend], q, KSW[64 * v:64 * v + 64, br, 0:kend], True, True,
                                   [*b.free, *t_qa, e_ks, e_kw])
                    for v in range(2):
                        q = QA[64 * v:64 * v + 64, g, i * 128:i * 128 + 128]
                        m2 = mm(b2[v].ap[:, 0:15], q, KC[64 * v:64 * v + 64, 0, :], True, True,
                                [*b2[v].free, t_c[0]])
                    dd = dist[:, 0:128] if i == 0 else dist[:, 128:384]
                    pc = pc_all[:, 4 * par:4 * par + 2, 0:15]
                    for v in range(2):
                        slope = 2.0 ** -(4 * v + g + 1)
                        d = stt(S[:, 2 * v:2 * v + 2, 0:kend], dd.unsqueeze(1).broadcast_to([128, 2, kend]), -slope,
                                bv[:, v, :, 0:kend], ALU.mult, ALU.add, [m, *wk_free[par]])
                    b.free = [d]
                    for v in range(2):
                        slope = 2.0 ** -(4 * v + g + 1)
                        dc = stt(pc[:, v, :], cdist[:, i, :], -slope, b2[v].ap[:, 0:15], ALU.mult,
                                 ALU.add, [m2, *wk_free[par]])
                        b2[v].free = [dc]
                    yield
                    o = 32 + 12 * par
                    Sv = S[:, :, 0:kend]
                    d1 = rmax(st[:, o:o + 4], Sv, [d])
                    d1 = rmax(st[:, o + 4:o + 6], pc, [dc])
                    d1 = ts(st[:, o:o + 6], st[:, o:o + 6], -1.0, None, ALU.mult, after=[d1])
                    for j in range(6):
                        s_ = Sv[:, j, :] if j < 4 else pc[:, j - 4, :]
                        a = act(s_, s_, ACT.Exp, [d1] if j == 0 else [], bias=st[:, o + j:o + j + 1],
                                acc=st[:, o + 6 + j:o + 7 + j])
                    d = recip(st[:, o + 6:o + 12], st[:, o + 6:o + 12], [a])
                    gv = GN[:, i, :].rearrange("p (v g b) -> p v g b", v=2, g=4)[:, :, g, :]
                    r4 = st[:, o + 6:o + 10].rearrange("p (v b) -> p v b", v=2)
                    d = tt(r4, r4, gv[:, :, 1:3], ALU.mult, [d, t_gn])
                    d = tt(st[:, o + 10:o + 12], st[:, o + 10:o + 12], gv[:, :, 0], ALU.mult)
                    for j in range(4):
                        d = ts(Sv[:, j, :], Sv[:, j, :], st[:, o + 6 + j:o + 7 + j], None, ALU.mult,
                               after=[d] if j == 0 else [])
                    for v in range(2):
                        d = stt(pc[:, v, :], pc[:, v, :], st[:, o + 10 + v:o + 11 + v], cmask[:, i, :], ALU.mult,
                                ALU.mult)
                    yield
                    for v in range(2):
                        b = tpb.take()
                        for br in range(2):
                            for kt in range(nk):
                                j = br * nk + kt
                                m = tr(b.ap[:, 128 * j:128 * j + 128], S[:, 2 * v + br, 128 * kt:128 * kt + 128],
                                       [d, *b.free] if j == 0 else [])
                        wT = wk(2048 + 512 * v, 512)
                        e = acp(wT[:, 0:256 * nk], b.ap[:, 0:256 * nk], [m, *wt_free[v]])
                        b.free = [e]
                        b = tpb.take()
                        m = tr(b.ap[0:15, 0:128], pc[:, v, :], b.free)
                        cT = wk(3072 + 128 * v, 128)
                        e = acp(cT[0:15, :], b.ap[0:15, 0:128], [m])
                        b.free = [e]
                        if v == 1:
                            wk_free[par] = [m]
                        yield
                        b = ob.take()
                        oo = b.ap[64 * v:64 * v + 64, 0:128]
                        first = True
                        for br in range(2):
                            for kt in range(nk):
                                j = br * nk + kt
                                m = mm(oo, VSW[:, br, kt, 64 * v:64 * v + 64], wT[:, 128 * j:128 * j + 128],
                                       first, False, [e, *b.free, e_vs, e_vw] if first else [])
                                first = False
                        m = mm(oo, VC2[0:15, v, :], cT[0:15, :], False, True, [t_c[1]])
                        wt_free[v] = [m]
                        h = 4 * v + g
                        e = cp(ONT[64 * (h % 2):64 * (h % 2) + 64, h // 2, i * 128:i * 128 + 128], oo, [m])
                        b.free = [e]
                        e_on.append(e)
                        yield

        e_og = []

        def gla():
            reset = const("reset")
            zt = ar(17920 + 0, 2, 128)
            b = big.take()
            for c in range(2):
                m = mm(b.ap[:, 256 * c:256 * c + 256], walp[:, 128 * c:128 * c + 128], AL[0:16, :], True, True,
                       [e_al, t_ws, *b.free])
            for c in range(2):
                d = ts(EB[:, c, :], b.ap[:, 256 * c:256 * c + 256], BA[:, c:c + 1], None, ALU.add, after=[m, t_vc])
            b.free = [d]
            a = act(EN[:], EB[:], ACT.Abs, [d])
            a = act(EN[:], EN[:], ACT.Exp, [a], scale=-1.0)
            a = act(EN[:], EN[:], ACT.Ln, [a, t_eps], bias=eps[:, 0:1])
            d = ts(EB[:], EB[:], 0.0, None, ALU.min, after=[a])
            d = tt(EN[:], EB[:], EN[:], ALU.subtract, [d])
            d = ts(EN[:], EN[:], 1.0 / 16.0, None, ALU.mult, after=[d])
            for c in range(2):
                d = P.put("dve", lambda c=c: nc.vector.tensor_tensor_scan(EB[:, c, :], reset, EN[:, c, :], 0.0,
                                                                           ALU.mult, ALU.add), [d])
            ev = EB[:].rearrange("p c (n t) -> p (c n) t", t=64)
            lv = EL[:].rearrange("p c (n t) -> p (c n) t", t=64)
            d = tt(lv, ev[:, :, 63:64].broadcast_to([128, 8, 64]), ev, ALU.subtract, [d])
            act(EL[:], EL[:], ACT.Exp, [d])
            a1 = act(EN[:], EB[:], ACT.Exp, scale=-1.0)
            a = act(EB[:], EB[:], ACT.Exp, [a1])
            yield
            d = stt(QB[:], EB[:], 0.125, QB[:], ALU.mult, ALU.mult, [a, *e_qk])
            d = tt(EN[:], EN[:], KB[:], ALU.mult)
            d_el = tt(EL[:], EL[:], KB[:], ALU.mult)
            KN = wk(3456, 2, 256)
            b = big.take()
            for i in range(2):
                for c in range(2):
                    m = tr(b.ap[:, 256 * i + 128 * c:256 * i + 128 * c + 128], EL[:, c, 128 * i:128 * i + 128],
                           [d_el, *b.free])
            kn = KB
            e_kn = acp(kn[:], b.ap.rearrange("p (a n) -> p a n", a=2), [m])
            b.free = [e_kn]
            yield
            SS = EL
            SS3 = ar(17920 - 0, 256)
            views = [None, EL[:, 0, :].rearrange("p (a e) -> p a e", a=2),
                     EL[:, 1, :].rearrange("p (a e) -> p a e", a=2),
                     XC[:, 0, :].rearrange("p (a e) -> p a e", a=2)]
            d_s = [None] * 4
            for n in range(3):
                lo = 64 * (n % 2)
                b = big.take()
                for c in range(2):
                    m = mm(b.ap[:, 256 * c:256 * c + 256], kn[lo:lo + 64, n // 2, 128 * c:128 * c + 128],
                           VB[lo:lo + 64, n // 2, 256 * c:256 * c + 256], True, True, [e_kn, *e_vb, *b.free])
                for c in range(2):
                    for h in range(2):
                        rr = slice(64 * h, 64 * h + 64)
                        o = views[n + 1][rr, c, :]
                        inc = b.ap[rr, 256 * c + 128 * h:256 * c + 128 * h + 128]
                        if n == 0:
                            d = cp(o, inc, [m])
                        else:
                            d = stt(o, views[n][rr, c, :], EB[rr, c, 64 * n + 63:64 * n + 64], inc, ALU.mult,
                                    ALU.add, [m, d_s[n], *t_z])
                b.free = [d]
                d_s[n + 1] = d
                yield
            up, un = const("up"), const("un")
            AT = ar(17408 - 1536, 4, 128)
            for i in range(2):
                bb = (big.take(), big.take())
                at = OGT[:, 2 * i:2 * i + 2, :].rearrange("p a (b n) -> p (a b) n", b=2)
                for h in (0, 2, 1, 3):
                    p, q = h % 2, h // 2
                    rr = slice(64 * p, 64 * p + 64)
                    m = mm(bb[p].ap[:, 128 * q:128 * q + 128], EN[rr, q, 128 * i:128 * i + 128],
                           QB[rr, q, 128 * i:128 * i + 128], True, True, [d_el, *bb[p].free, *e_ao])
                for p in range(2):
                    d = tt(at[:, 2 * p:2 * p + 2, :], bb[p].ap[:, 0:256].rearrange("p (h n) -> p h n", h=2),
                           up.unsqueeze(1).broadcast_to([128, 2, 128]), ALU.min, [m])
                    bb[p].free = [d]
                d = tt(at, at, un.unsqueeze(1).broadcast_to([128, 4, 128]), ALU.max, [d])
                yield
                bb = (big.take(), big.take())
                for p in range(2):
                    for q in range(2):
                        h = 2 * q + p
                        m = mm(bb[p].ap[:, 128 * q:128 * q + 128], at[:, 2 * p + q, :],
                               VB[:, i, 128 * h:128 * h + 128], q == 0, False,
                               [d, *bb[p].free, *e_vb])
                    for half in range(2):
                        n = 2 * i + half
                        if n == 0:
                            continue
                        for q in range(2):
                            m = mm(bb[p].ap[64 * half:64 * half + 64, 128 * q:128 * q + 128],
                                   QB[64 * p:64 * p + 64, q, 64 * n:64 * n + 64], views[n][64 * p:64 * p + 64, q, :],
                                   False, True, [d_s[n]])
                og = OG[:, i, :].rearrange("p (h d) -> p h d", h=4)
                ogp = OG[:, i, :].rearrange("p (q s d) -> p q s d", q=2, s=2)
                for p in range(2):
                    e = acp(ogp[:, :, p, :], bb[p].ap[:, 0:256].rearrange("p (q d) -> p q d", q=2), [m])
                    bb[p].free = [e]
                yield
                s4 = st[:, 64 + 8 * i:72 + 8 * i]
                sq = MRGtmp[i]
                d = tt(sq, og, og, ALU.mult, [e])
                d = rsum(s4[:, 0:4], sq, [d])
                d = ts(s4[:, 0:4], s4[:, 0:4], 1.0 / 128, EPS, ALU.mult, ALU.add, after=[d])
                d = recip(s4[:, 4:8], s4[:, 0:4], [d])
                a = act(s4[:, 0:4], s4[:, 4:8], ACT.Sqrt, [d])
                rv = RB[:, i, :]
                a2 = sig_part(sq.rearrange("p h d -> p (h d)"), rv, [d, *e_rb])
                d = tt(og, og, s4[:, 0:4].unsqueeze(2).broadcast_to([128, 4, 128]), ALU.mult, [a])
                d = tt(og, og, glag[:].unsqueeze(1).broadcast_to([128, 4, 128]), ALU.mult, [d, t_bc])
                sf = sq.rearrange("p h d -> p (h d)")
                d1 = ts(sf, sf, 0.5, 0.5, ALU.mult, ALU.add, after=[a2])
                d1 = tt(rv, rv, sf, ALU.mult, [d1])
                d = tt(OG[:, i, :], OG[:, i, :], rv, ALU.mult, [d1, d])
                e_ao.append(d)
                yield
            for i in range(2):
                e_og.extend(turn(lambda k: OG[:, i, 128 * k:128 * k + 128], OGT, 4, i, None, [e_ao[i]], e_ao))
                yield

        e_ao = []
        MRGtmp = [XN[:, 0, 0:512].rearrange("p (h d) -> p h d", h=4),
                  XN[:, 1, 0:512].rearrange("p (h d) -> p h d", h=4)]

        def alternate(a, b, na, nb):
            while True:
                alive = False
                for gen, k in ((a, na), (b, nb)):
                    for _ in range(k):
                        try:
                            next(gen)
                            alive = True
                        except StopIteration:
                            break
                if not alive:
                    return
                yield

        weave(alternate(nsa(), gla(), 3, 1), merges(), 0.45)

        MX = ar(4096, 8, 256)
        t_bn = wrows(A["w_branch_nsa_2"][0], 0, 4)
        t_bg = wrows(A["w_branch_gla_2"][0], 0, 4)
        TMP = XN[:].rearrange("p i (a n) -> p (i a) n", n=256)
        t_mx = []
        for mp in range(4):
            ds = []
            for (wv, t, s), src, dep, dst, go in ((t_bn, ONT, e_on, TMP, 0), (t_bg, OGT, e_og, MX, 8)):
                b = big.take()
                for h in range(2):
                    c = 256 * mp + 128 * h
                    m = turned(lambda k: wv[:, k, c:c + 128], t, src, b.ap[:, 256 * h:256 * h + 256], b, 4, dep)
                s["free"].append(m)
                e = tt(dst[:, 2 * mp:2 * mp + 2, :], b.ap.rearrange("p (a n) -> p a n", a=2),
                       MRG[:, go + 2 * mp:go + 2 * mp + 2, :], ALU.mult, [m, *e_mg, *e_og, *e_on, *e_ao])
                b.free = [e]
                ds.append(e)
            v = slice(2 * mp, 2 * mp + 2)
            t_mx.append(tt(MX[:, v, :], MX[:, v, :], TMP[:, v, :], ALU.add, ds))
        t_x3 = residual_natural(A["w_out_2"][0], MX, t_mx)

        t_h = norm_turn(X, t_x3, G_X, HT, free=t_mx)
        QX = ar(0, 4, 256)
        OX = ar(1024, 4, 256)
        wv, t, s = wcols(A["w_xq_2"][0], 0, 512)
        t_qx = []
        for mp in range(2):
            b = big.take()
            for h in range(2):
                c = 256 * mp + 128 * h
                m = turned(lambda k: wv[:, k, c:c + 128], t, HT, b.ap[:, 256 * h:256 * h + 256], b, 8, t_h)
            e = evac(QX[:, 2 * mp:2 * mp + 2, :], b.ap.rearrange("p (a n) -> p a n", a=2), [m, *t_x3])
            s["free"].append(m)
            b.free = [e]
            t_qx.append(e)
        e_ox = []
        sc = 128.0 ** -0.5
        wk_f = [[], []]
        for n in range(2):
            S = wk(0, 4, 256)
            b = scb.take()
            bv = b.ap.rearrange("p h (i n) -> p h i n", i=2)
            for hh in range(2):
                h = 2 * n + hh
                for i in range(2):
                    m = mm(bv[:, hh, i, :], QX[:, h, i * 128:i * 128 + 128], KX[:, h, :], True, True,
                           [*b.free, *t_qx, *t_kx])
            d = cp(S, bv.rearrange("p h i n -> p (h i) n"), [m, *wk_f[0], *e_on])
            b.free = [d]
            a = softmax_pairs(S, 4, sc, [d], 32)
            d = recip(st[:, 48:52], st[:, 36:40], [a])
            for j in range(4):
                d = ts(S[:, j, :], S[:, j, :], st[:, 48 + j:49 + j], None, ALU.mult, after=[d] if j == 0 else [])
            for hh in range(2):
                b = tpb.take()
                for i in range(2):
                    for mt in range(2):
                        m = tr(b.ap[:, 256 * mt + 128 * i:256 * mt + 128 * i + 128],
                               S[:, 2 * hh + i, 128 * mt:128 * mt + 128], [d, *b.free])
                pT = wk(1024 + 512 * hh, 2, 256)
                e = acp(pT, b.ap.rearrange("p (a n) -> p a n", a=2), [m, *wk_f[1]])
                b.free = [e]
                b = ob.take()
                for mt in range(2):
                    h = 2 * n + hh
                    m2 = mm(b.ap[:, 0:256], VX[:, mt, 128 * h:128 * h + 128], pT[:, mt, :], mt == 0, mt == 1,
                            [e, *b.free, *t_vx])
                e = evac(OX[:, 2 * n + hh, :], b.ap[:, 0:256], [m2])
                b.free = [e]
                e_ox.append(e)
            wk_f = [[m], [m2]]
        t_x4 = residual_rows(A["w_xo_2"][0], OX, 4, lambda kk: [e_ox[kk]])

        t_h = norm_turn(X, t_x4, G_FFN, HT, free=t_qx)
        FT = ar(2048, 22, 256)
        w_up = A["w_up_2"][0]
        cw = VC[:, 1, 0:66].rearrange("p (t c) -> p t c", t=3)
        e_f = []
        fw_free = [[], []]
        for j in range(11):
            ap, t, s = chunk((lambda a: v3(a, 8, 512)[:, :, 0:256],
                              w_up[:, 256 * j:256 * j + 256].rearrange("(k p) n -> p k n", p=128)),
                             (lambda a: v3(a, 8, 512)[:, :, 256:512],
                              w_up[:, 2816 + 256 * j:3072 + 256 * j].rearrange("(k p) n -> p k n", p=128)))
            wv = v3(ap, 8, 512)
            bu, bg = big.take(), big.take()
            for b, off in ((bu, 0), (bg, 256)):
                for h in range(2):
                    m = turned(lambda k: wv[:, k, off + 128 * h:off + 128 * h + 128], t, HT,
                               b.ap[:, 256 * h:256 * h + 256], b, 8, t_h)
                b.m = m
            s["free"].append(m)
            par = j % 2
            U = wk(2048 * par, 2, 256)
            Y = wk(2048 * par + 512, 2, 256)
            for h in range(2):
                ch = 2 * j + h
                u = bu.ap[:, 256 * h:256 * h + 256]
                d = ts(U[:, h, :], u, cw[:, 2, ch:ch + 1], CB[:, ch:ch + 1], ALU.mult, ALU.add,
                       after=[bu.m, *fw_free[par], *e_ox, t_vc])
                d = stt(U[:, h, 1:256], u[:, 0:255], cw[:, 1, ch:ch + 1], U[:, h, 1:256], ALU.mult, ALU.add, [d])
                d = stt(U[:, h, 2:256], u[:, 0:254], cw[:, 0, ch:ch + 1], U[:, h, 2:256], ALU.mult, ALU.add, [d])
            bu.free = [d]
            d0 = d
            p1 = gtt(Y, U, U, ALU.mult, [d])
            p1 = P.put("pool", lambda Y=Y: nc.gpsimd.tensor_scalar(Y, Y, 0.044715, 1.0, ALU.mult, ALU.add), [p1])
            p1 = gtt(Y, Y, U, ALU.mult, [p1])
            a = act(Y, Y, ACT.Tanh, [p1], scale=math.sqrt(2.0 / math.pi))
            a = P.put("pool", lambda Y=Y: nc.gpsimd.tensor_scalar(Y, Y, 0.5, 0.5, ALU.mult, ALU.add), [a])
            o = FT[:, 2 * j:2 * j + 2, :]
            p1 = gtt(Y, Y, U, ALU.mult, [a])
            d = tt(o, Y, bg.ap.rearrange("p (a n) -> p a n", a=2), ALU.mult, [p1, bg.m])
            bg.free = [d]
            fw_free[par] = [d]
            e_f.append(d)
        t_x5 = residual_rows(A["w_down_2"][0], FT, 22, lambda kk: [e_f[kk // 2]])

        s_out = sem("s_out")
        outs = []
        ov = out[0].rearrange("(i p) d -> p i d", p=128)
        for i in range(2):
            d = rms_rows(X[:, i, :], i, XN[:, i, :], [*t_x5, *t_h], 4 * i)
            d = tt(XN[:, i, :], XN[:, i, :], grow[:], ALU.mult, [d, t_grow2])
            outs.append(P.dma("sp", [lambda i=i: nc.sync.dma_start(ov[:, i, :], XN[:, i, :])], [d], s_out))
        P.q["sp"].append((None, (outs[-1],), None, None))
        P.emit()


_INS = ['x', 'positions', 'norm_attn_g', 'w_in', 'lam_q1', 'lam_k1', 'lam_q2', 'lam_k2', 'subln_g', 'w_pool',
        'pool_scale', 'w_out', 'norm_mlp_g', 'w_up', 'w_down', 'final_norm_g', 'mem_2', 'ln_mix_g_2', 'w_in_2',
        'nsa_gate_b_2', 'cmp_pos_k_2', 'cmp_w1_k_2', 'cmp_w2_k_2', 'cmp_pos_v_2', 'cmp_w1_v_2', 'cmp_w2_v_2',
        'gla_w_alpha2_2', 'gla_b_alpha_2', 'gla_norm_g_2', 'w_branch_nsa_2', 'w_branch_gla_2', 'w_out_2',
        'ln_x_g_2', 'ln_mem_g_2', 'w_xq_2', 'w_xkv_2', 'w_xo_2', 'ln_ffn_g_2', 'w_up_2', 'conv_w_2', 'conv_b_2',
        'w_down_2', 'ln_final_g_2']


def kernel(**inputs):
    import numpy as _np
    import concourse.bacc as _bacc
    from concourse import mybir as _mybir
    from concourse.bass_utils import run_bass_kernel_spmd as _run

    nc = _bacc.Bacc("TRN2", target_bir_lowering=False, num_devices=1)
    arrays, args = {}, {}
    for name in _INS:
        a = _np.ascontiguousarray(inputs[name])
        arrays[f"in_{name}_dram"] = a
        args[name] = nc.dram_tensor(f"in_{name}_dram", a.shape, _mybir.dt.from_np(a.dtype),
                                    kind="ExternalInput").ap()
    a = shape_constants()
    arrays["shape_constants"] = a
    args["shape_constants"] = nc.dram_tensor("shape_constants", a.shape, _mybir.dt.float32,
                                             kind="ExternalInput").ap()
    o = nc.dram_tensor("out_0_dram", (1, 256, 1024), _mybir.dt.float32, kind="ExternalOutput").ap()
    two_blocks(nc, args, o)
    r = _run(nc, [arrays], core_ids=[0])
    return r.results[0]["out_0_dram"]
```

```python
import math
from contextlib import ExitStack

import numpy as np
import concourse.bass as bass
from concourse import mybir

F32 = mybir.dt.float32
I32 = mybir.dt.int32
ALU = mybir.AluOpType
ACT = mybir.ActivationFunctionType
AX = mybir.AxisListType.X
EPS = 1e-6
F32R = mybir.dt.float32r
NLOW = 4
NHIGH = 3
UNIT = 2048
ROPE_THETA = 500000.0
TWO_PI = 2.0 * math.pi
C1 = 6.28125
C2 = float(np.float32(np.round((TWO_PI - C1) * 2 ** 21) / 2 ** 21))
C3 = float(np.float32(TWO_PI - C1 - C2))
MAGIC = 12582912.0
FAR = 1e34

CONST = {}
_at = 0
for _name, _width in (("ident", 128), ("cm", 256), ("dist", 384), ("cdist", 30), ("cmask", 30), ("up", 128),
                      ("un", 128), ("reset", 256), ("freq", 8), ("pool", 1536)):
    CONST[_name] = (_at, _width)
    _at += _width
NCONST = _at


def shape_constants():
    c = np.zeros((128, NCONST), np.float32)

    def put(name, a):
        o, w = CONST[name]
        c[:, o:o + w] = np.asarray(a, np.float32).reshape(128, w)

    p = np.arange(128)
    put("ident", np.eye(128))
    causal = p[None, :] <= p[:, None]
    put("cm", np.concatenate([np.zeros((128, 128)), np.where(causal, 0.0, -1e30)], 1))
    d0 = np.where(causal, p[:, None] - p[None, :], FAR)
    d1 = np.where(np.arange(256)[None, :] <= p[:, None] + 128, p[:, None] + 128 - np.arange(256)[None, :], FAR)
    put("dist", np.concatenate([d0, d1], 1))
    end = np.arange(15) * 16 + 31
    t = p[:, None] + 128 * np.arange(2)[None, :]
    dc = t[:, :, None] - end
    put("cdist", np.where(dc >= 0, dc, FAR))
    put("cmask", dc >= 0)
    ok = (p[:, None] <= p[None, :]) & (p[:, None] // 64 == p[None, :] // 64)
    put("up", np.where(ok, 3.4028235e38, 0.0))
    put("un", np.where(ok, -3.4028235e38, 0.0))
    put("reset", np.broadcast_to((np.arange(256) % 64 != 0), (128, 256)))
    put("freq", np.broadcast_to(np.float32(ROPE_THETA) ** (-np.arange(0, 16, 2, dtype=np.float32) / 16), (128, 8)))
    pool = np.zeros((128, 4, 3, 128), np.float64)
    for g, w in enumerate((2, 4, 8, 16)):
        for n, (so, to) in enumerate(((0, 0), (0, 128), (128, 128))):
            s, tt = so + p[:, None], to + p[None, :]
            pool[:, g, n] = np.where((s <= tt) & (s > tt - w), 1.0 / np.minimum(tt + 1, w), 0.0) - (s == tt)
    put("pool", pool)
    return c


class Tok:

    def __init__(self, eng=None, sem=None, val=None):
        self.eng, self.sem, self.val, self.sig = eng, sem, val, False


class Prog:

    def __init__(self, nc, ctx):
        self.nc = nc
        self.ctx = ctx
        self.q = {e: [] for e in ("pe", "act", "dve", "pool", "sp")}
        self.sem = {e: ctx.enter_context(nc.semaphore("s_" + e)) for e in self.q}
        self.dmas = {}

    def put(self, eng, fn, after):
        t = Tok(eng=eng)
        self.q[eng].append((fn, tuple(after), t, None))
        return t

    def dma(self, eng, fns, after, sem):
        for fn in fns:
            self.dmas[sem] = self.dmas.get(sem, 0) + 16
            self.q[eng].append((fn, tuple(after), None, sem))
        return Tok(sem=sem, val=self.dmas[sem])

    def emit(self):
        for q in self.q.values():
            for _, after, _, _ in q:
                for t in after:
                    if t.sem is None:
                        t.sig = True
        for e, q in self.q.items():
            n = 0
            for _, _, t, _ in q:
                if t is not None and t.sig:
                    n += 1
                    t.val = n
        block = self.ctx.enter_context(self.nc.Block())

        def run(name):
            def body(eng):
                seen = {}
                for fn, after, t, dsem in self.q[name]:
                    need = {}
                    for a in after:
                        s = a.sem if a.sem is not None else self.sem[a.eng]
                        if a.val > seen.get(s, 0) and a.val > need.get(s, 0):
                            need[s] = a.val
                    for s, v in need.items():
                        eng.wait_ge(s, v)
                        seen[s] = v
                    if fn is None:
                        continue
                    ins = fn()
                    if dsem is not None:
                        ins.then_inc(dsem, 16)
                    elif t.sig:
                        ins.then_inc(self.sem[name], 1)
            return body

        block.tensor(run("pe"))
        block.scalar(run("act"))
        block.vector(run("dve"))
        block.gpsimd(run("pool"))
        block.sync(run("sp"))


class Bank:
    def __init__(self, ap):
        self.ap = ap
        self.free = []


class Split:

    def __init__(self, hi, lo, f):
        self.hi, self.lo, self.f = hi, lo, f

    def __getitem__(self, k):
        return Split(self.hi[k], self.lo[k], self.f[k])


class Banks:

    def __init__(self, aps):
        self.b = [Bank(a) for a in aps]
        self.n = 0

    def take(self):
        b = self.b[self.n % len(self.b)]
        self.n += 1
        return b


def two_blocks(nc, A, out):
    ctx = ExitStack()
    with ctx:
        P = Prog(nc, ctx)

        def sb(name, *shape, dt=F32):
            return ctx.enter_context(nc.sbuf_tensor(name, list(shape), dt))

        def sem(name):
            return ctx.enter_context(nc.semaphore(name))

        def mm(o, l, r, start, stop, after=()):
            return P.put("pe", lambda: nc.tensor.matmul(o, l, r, start=start, stop=stop,
                                                        skip_group_check=True), after)

        def tr(o, i, after=()):
            n = i.shape[0]
            return P.put("pe", lambda: nc.tensor.transpose(o, i, ident[0:n, 0:n]), after)

        def act(o, i, f, after=(), bias=0.0, scale=1.0, acc=None):
            if acc is None:
                return P.put("act", lambda: nc.scalar.activation(o, i, f, bias=bias, scale=scale), after)
            return P.put("act", lambda: nc.scalar.activation(o, i, f, bias=bias, scale=scale, accum_out=acc), after)

        def tt(o, a, b, op, after=()):
            return P.put("dve", lambda: nc.vector.tensor_tensor(o, a, b, op), after)

        def gtt(o, a, b, op, after=()):
            return P.put("pool", lambda: nc.gpsimd.tensor_tensor(o, a, b, op), after)

        def ts(o, a, s1, s2, op0, op1=None, after=()):
            if op1 is None:
                return P.put("dve", lambda: nc.vector.tensor_scalar(o, a, s1, None, op0), after)
            return P.put("dve", lambda: nc.vector.tensor_scalar(o, a, s1, s2, op0, op1), after)

        def stt(o, a, s, b, op0, op1, after=()):
            return P.put("dve", lambda: nc.vector.scalar_tensor_tensor(o, a, s, b, op0, op1), after)

        def cp(o, a, after=()):
            return P.put("dve", lambda: nc.vector.tensor_copy(o, a), after)

        def acp(o, a, after=()):
            return act(o, a, ACT.Copy, after)

        def rmax(o, a, after=()):
            return P.put("dve", lambda: nc.vector.reduce_max(o, a, AX), after)

        def rsum(o, a, after=()):
            return P.put("dve", lambda: nc.vector.reduce_sum(o, a, AX), after)

        def recip(o, a, after=()):
            return P.put("dve", lambda: nc.vector.reciprocal(o, a), after)

        def load(eng, name, *pairs, after=()):
            e = {"sp": nc.sync, "act": nc.scalar, "pool": nc.gpsimd}[eng]
            return P.dma(eng, [(lambda d=d, s=s: e.dma_start(d, s)) for d, s in pairs], after, sem("l_" + name))

        def both(name, *shape):
            at = (nc.sbuf_base + 31) // 32 * 32
            f = sb(name + "_f", *shape)
            return f, nc.alloc_sbuf_tensor_at(name + "_r", list(shape), F32R, offset=at)

        cst = sb("cst", 128, NCONST)

        def const(name):
            o, w = CONST[name]
            return cst[:, o:o + w]

        ident = const("ident")
        X = sb("X", 128, 2, 1024)
        XN = sb("XN", 128, 2, 1024)
        HTh = sb("HTh", 128, 8, 256, dt=F32R)
        HTf, HTl = both("HTl", 128, 8, 256)
        HT = Split(HTh[:], HTl[:], HTf[:])
        high = [sb(f"high{i}", 128, UNIT, dt=F32R) for i in range(NHIGH)]
        low = [both(f"low{i}", 128, UNIT) for i in range(NLOW)]
        grow = sb("grow", 128, 1024)
        psc = sb("psc", 128, 1024)
        subg = sb("subg", 128, 128)
        glag = sb("glag", 128, 128)
        gateb = sb("gateb", 128, 24)
        lamv = sb("lamv", 128, 4, 64)
        wpool = sb("wpool", 128, 4, 256)
        walp = sb("walp", 16, 256)
        w2 = sb("w2", 128, 3, 64)
        VR = sb("VR", 128, 2, 128)
        VC = sb("VC", 128, 2, 88)
        posi = sb("posi", 128, 2, dt=I32)
        st = sb("st", 128, 128)
        AR, ARr = both("AR", 128, 18432)
        WK, WKr = both("WK", 128, 4096)
        eps = sb("eps", 128, 2)

        def part(t, size, off, shape):
            n = int(np.prod(shape))
            assert off + n <= size, (off, shape)
            v = t[:, off:off + n]
            if len(shape) == 1:
                return v
            names = "abcd"[:len(shape)]
            return v.rearrange("p (" + " ".join(names) + ") -> p " + " ".join(names),
                               **{names[k]: shape[k] for k in range(len(shape) - 1)})

        def ar(off, *shape):
            return part(AR, 18432, off, shape)

        def wk(off, *shape):
            return part(WK, 4096, off, shape)

        def ars(off, off2, *shape):
            return Split(part(ARr, 18432, off, shape), part(ARr, 18432, off2, shape), part(AR, 18432, off2, shape))

        def wks(off, off2, *shape):
            return Split(part(WKr, 4096, off, shape), part(WKr, 4096, off2, shape), part(WK, 4096, off2, shape))

        PS = ctx.enter_context(nc.psum_tensor("PS", [128, 8, 512], F32))
        big = Banks([PS[:, i, :] for i in range(4)])
        scb = Banks([PS[:, 4:6, :]])
        tpb = Banks([PS[:, 6, :]])
        ob = Banks([PS[:, 7, :]])
        small = Banks([])
        small.b = [tpb.b[0], ob.b[0]]

        plan = []

        def v3(ap, K, n):
            return ap[:, 0:K * n].rearrange("p (k n) -> p k n", k=K)

        def block_of(w, k0, K, c0, n):
            return w[128 * k0:128 * (k0 + K), c0:c0 + n].rearrange("(k p) n -> p k n", p=128)

        def planned(key, w, k0, K, c0, n):
            plan.append((key, K, n, [(lambda a: v3(a, K, n), block_of(w, k0, K, c0, n))]))

        def plan_wide(key, w, c0, n=1024):
            for c in range(c0, c0 + n, 512):
                for k0 in range(0, w.shape[0] // 128, 4):
                    planned(key, w, k0, 4, c, 512)

        def plan_tall(key, w, c0, n):
            for c in range(c0, c0 + n, 256):
                planned(key, w, 0, 8, c, 256)

        def plan_rows(key, w):
            for k0 in range(0, w.shape[0] // 128, 2):
                planned(key, w, k0, 2, 0, 1024)

        w1, w2_ = A["w_in"][0], A["w_in_2"][0]
        plan_wide("q", w1, 0)
        plan_wide("k", w1, 1024)
        plan_wide("v", w1, 2048)
        plan_wide("pool", w1, 3072, 512)
        plan_wide("gate", w1, 3584, 2048)
        plan_wide("out", A["w_out"][0], 0)
        plan_tall("up", A["w_up"][0], 0, 4096)
        plan_rows("down", A["w_down"][0])
        plan_tall("kx", A["w_xkv_2"][0], 0, 512)
        plan_wide("vx", A["w_xkv_2"][0], 512, 512)
        for mp in range(2):
            plan.append(("qa", 8, 256, [
                (lambda a, v=v, k=k: v3(a, 8, 256)[:, k, :].rearrange("p (g v d) -> p g v d", g=2, v=2)[:, :, v],
                 w2_[128 * k:128 * k + 128, 256 * v + 128 * mp:256 * v + 128 * mp + 128]
                 .rearrange("p (g d) -> p g d", g=2)) for v in range(2) for k in range(8)]))
        planned("kvc", w2_, 0, 8, 512, 256)
        planned("kvs", w2_, 0, 8, 768, 256)
        planned("kvw", w2_, 0, 8, 1024, 256)
        plan.append(("small", 8, 40, [(lambda a: v3(a, 8, 40)[:, :, 0:24], block_of(w2_, 0, 8, 1280, 24)),
                                      (lambda a: v3(a, 8, 40)[:, :, 24:40], block_of(w2_, 0, 8, 2840, 16))]))
        planned("w1k", A["cmp_w1_k_2"][0], 0, 16, 0, 128)
        planned("w1v", A["cmp_w1_v_2"][0], 0, 16, 0, 128)
        plan_tall("qkb", w2_, 1304, 512)
        plan_wide("vb", w2_, 1816, 512)
        plan_wide("rb", w2_, 2328, 512)
        plan_tall("merge", w2_, 2856, 2048)
        for c in range(0, 1024, 512):
            planned("bn", A["w_branch_nsa_2"][0], 0, 4, c, 512)
            planned("bg", A["w_branch_gla_2"][0], 0, 4, c, 512)
        plan_wide("out2", A["w_out_2"][0], 0)
        plan_tall("xq", A["w_xq_2"][0], 0, 512)
        plan_rows("xo", A["w_xo_2"][0])
        for j in range(11):
            planned("up2", A["w_up_2"][0], 0, 8, 256 * j, 256)
            planned("up2", A["w_up_2"][0], 0, 8, 2816 + 256 * j, 256)
        plan_rows("down2", A["w_down_2"][0])

        low_sem = [sem(f"low_s{i}") for i in range(NLOW)]
        loaded, ready, done = [], [], []
        state = {"ev": 0}

        def load_unit():
            m = len(loaded)
            key, K, n, pieces = plan[m]
            slot = low[m % NLOW][0]
            free = [done[m - NLOW]] if m >= NLOW else []
            loaded.append(P.dma("sp", [(lambda d=f(slot[:]), src=src: nc.sync.dma_start(d, src))
                                       for f, src in pieces], free, low_sem[m % NLOW]))

        def split_unit():
            m = len(ready)
            key, K, n, _ = plan[m]
            f, r = low[m % NLOW]
            h = high[m % NHIGH]
            free = [done[m - NHIGH]] if m >= NHIGH else []
            half = K * n // 2
            for o in (0, half):
                a = acp(h[:, o:o + half], f[:, o:o + half], [loaded[m], *free])
                d = tt(r[:, o:o + half], f[:, o:o + half], h[:, o:o + half], ALU.subtract, [a])
            ready.append([d])

        def take(key):
            m = len(done)
            assert plan[m][0] == key, (plan[m][0], key)
            while len(loaded) < min(len(plan), m + NLOW):
                load_unit()
            while len(ready) < min(len(plan), m + 2):
                split_unit()
            K, n = plan[m][1:3]
            return Split(v3(high[m % NHIGH][:], K, n), v3(low[m % NLOW][1][:], K, n),
                         v3(low[m % NLOW][0][:], K, n)), ready[m]

        def mm3(o, l, r, first, last, after=()):
            mm(o, l.hi, r.hi, first, False, after)
            mm(o, l.hi, r.lo, False, False)
            return mm(o, l.lo, r.hi, False, last)

        def split_psum(dst, src, after, free=()):
            a = acp(dst.hi, src, [*after, *free])
            return tt(dst.lo, src, dst.hi, ALU.subtract, [a])

        def split_f(dst, after):
            a = acp(dst.hi, dst.f, after)
            return tt(dst.lo, dst.f, dst.hi, ALU.subtract, [a])

        def evac(o, a, after, scale=None):
            state["ev"] ^= 1
            return acp(o, a, after) if state["ev"] else cp(o, a, after)

        def wide(key, hT, after, fin, K=8, pool=None):
            bs = [(pool or big).take() for _ in range(2)]
            for k0 in range(0, K, 4):
                w, t = take(key)
                for i in range(2):
                    for k in range(4):
                        m = mm3(bs[i].ap, hT[:, k0 + k, i * 128:i * 128 + 128], w[:, k, :], k0 + k == 0,
                                k0 + k == K - 1, [*t, *after, *(bs[i].free if k0 == 0 else [])] if k == 0 else [])
                    if i == 1:
                        done.append(m)
                    if k0 == K - 4:
                        fin(i, bs[i], m)
                    yield

        def run_all(g):
            for _ in g:
                pass

        def turned(w, c, t, hT, o, b, K, after, n=256, width=128):
            for k in range(K):
                m = mm3(o, w[:, k, c:c + width], hT[:, k, 0:n], k == 0, k == K - 1,
                        [*t, *after, *b.free] if k == 0 else [])
            return m

        def tall(key, hT, after, fin, K=8, pool=None, nb=2):
            w, t = take(key)
            for m0 in range(0, nb, 2):
                b = (pool or big).take()
                for h in range(2):
                    m = turned(w, 128 * (m0 + h), t, hT, b.ap[:, 256 * h:256 * h + 256], b, K, after)
                    if h == 0:
                        yield
                if m0 + 2 >= nb:
                    done.append(m)
                fin(b, b.ap.rearrange("p (a n) -> p a n", a=2), m, m0)
                yield

        t_x = load("sp", "x", (X[:], A["x"][0].rearrange("(i p) d -> p i d", p=128)))
        t_cst = load("act", "cst", (cst[:], A["shape_constants"]))

        def rows(v, k):
            return v.rearrange("(k p) -> k p", p=128)

        vr0 = [("norm_attn_g", 0, 8), ("norm_mlp_g", 8, 8), ("ln_mix_g_2", 16, 8), ("ln_x_g_2", 24, 8),
               ("ln_mem_g_2", 32, 8), ("ln_ffn_g_2", 40, 8), ("conv_b_2", 48, 22), ("gla_b_alpha_2", 70, 2)]
        pairs = [(VR[o:o + n, 0, :], rows(A[nm][0], n)) for nm, o, n in vr0]
        pairs.append((VR[72:88, 0, :], A["cmp_pos_k_2"][0].rearrange("(j e) d -> j (e d)", e=2)))
        for tap in range(3):
            pairs.append((VR[22 * tap:22 * tap + 22, 1, :], rows(A["conv_w_2"][0, tap], 22)))
        pairs.append((VR[66:82, 1, :], A["cmp_pos_v_2"][0].rearrange("(j e) d -> j (e d)", e=2)))
        t_vr = load("act", "vr", *pairs)
        t_pos = P.dma("act", [lambda: nc.scalar.dma_start(posi[:], A["positions"][0].rearrange("(i p) -> p i", p=128), allow_slow_non_contiguous=True)], [], sem("l_pos"))
        t_lam = load("act", "lam", *[(lamv[:, j, :], A[nm][0:1].broadcast_to([128, 64]))
                                     for j, nm in enumerate(("lam_q1", "lam_k1", "lam_q2", "lam_k2"))])
        t_bc = load("act", "bc", (subg[:], A["subln_g"][0:1].broadcast_to([128, 128])),
                    (glag[:], A["gla_norm_g_2"][0:1].broadcast_to([128, 128])),
                    (gateb[:], A["nsa_gate_b_2"][0:1].broadcast_to([128, 24])),
                    (psc[:], A["pool_scale"][0:1].broadcast_to([128, 1024])))
        t_grow = load("act", "grow", (grow[:], A["final_norm_g"].rearrange("(a n) -> a n", a=1)
                                      .broadcast_to([128, 1024])))
        t_ws = load("act", "ws", (wpool[:], A["w_pool"][0].rearrange("g c d -> c g d")),
                    (walp[:], A["gla_w_alpha2_2"][0]),
                    (w2[:, 0, :], A["cmp_w2_k_2"][0]), (w2[:, 1, :], A["cmp_w2_k_2"][0]),
                    (w2[:, 2, :], A["cmp_w2_v_2"][0]))

        t_eps = P.put("dve", lambda: nc.vector.memset(eps[:, 0:1], 1.0), ())
        b = tpb.take()
        m1 = tr(b.ap[:, 0:88], VR[0:88, 0, :], [t_cst, t_vr])
        m2 = tr(b.ap[:, 128:210], VR[0:82, 1, :])
        t_vc0 = cp(VC[:, 0, 0:88], b.ap[:, 0:88], [m2])
        t_vc = cp(VC[:, 1, 0:82], b.ap[:, 128:210])
        b.free = [t_vc]
        G_ATT, G_MLP, G_MIX, G_X, G_MEM, G_FFN = (VC[:, 0, 8 * j:8 * j + 8] for j in range(6))
        CB = VC[:, 0, 48:70]
        BA = VC[:, 0, 70:72]
        POS = (VC[:, 0, 72:88], VC[:, 1, 66:82])

        def rms_rows(x, i, xn, after, s0, junk=None, after2=()):
            a = act(xn if junk is None else junk, x, ACT.Square, [*after, *after2], acc=st[:, s0:s0 + 1])
            d = ts(st[:, s0 + 1:s0 + 2], st[:, s0:s0 + 1], 1.0 / 1024, EPS, ALU.mult, ALU.add, [a])
            d = recip(st[:, s0 + 2:s0 + 3], st[:, s0 + 1:s0 + 2], [d])
            a = act(st[:, s0 + 3:s0 + 4], st[:, s0 + 2:s0 + 3], ACT.Sqrt, [d])
            return ts(xn, x, st[:, s0 + 3:s0 + 4], None, ALU.mult, after=[a])

        def turn(src, dst, n, i, gain, after, free, pool=None):
            out_t = []
            pool = pool or big
            for k0 in range(0, n, 4):
                b = pool.take()
                kk = min(4, n - k0)
                for k in range(kk):
                    m = tr(b.ap[:, 128 * k:128 * k + 128], src(k0 + k), [*after, *b.free, t_cst] if k == 0 else [])
                v = b.ap[:, 0:128 * kk].rearrange("p (k n) -> p k n", k=kk)
                o = dst[:, k0:k0 + kk, i * 128:i * 128 + 128]
                if gain is not None:
                    e = tt(o.f, v, gain[:, k0:k0 + kk].unsqueeze(2).broadcast_to([128, kk, 128]), ALU.mult,
                           [m, t_vc0, *free])
                    b.free = [e]
                    e = split_f(o, [e])
                elif isinstance(dst, Split):
                    e = split_psum(o, v, [m], free)
                    b.free = [e]
                else:
                    e = evac(o, v, [m, *free])
                    b.free = [e]
                out_t.append(e)
            return out_t

        def norm_turn(x, after, gain, dst, free=()):
            res = []
            for i in range(2):
                d = rms_rows(x[:, i, :], i, XN[:, i, :], [*after, *free], 4 * i)
                res += turn(lambda k: XN[:, i, 128 * k:128 * k + 128], dst, 8, i, gain, [d], free)
            return res

        Q = ar(0, 2, 1024)
        Kn = ar(2048, 2, 1024)
        QT = ar(4096, 8, 256)
        KT = ar(6144, 8, 256)
        V = ar(8192, 2, 1024)
        UP = ar(10240, 2, 512)
        DT = ar(11264, 4, 256)
        GT = ar(12288, 2, 2048)
        cs = ar(16384, 2, 4, 8)
        rt = ar(16448, 2, 2, 16, 8)

        ang = ar(16960, 2, 2, 8)
        d = cp(st[:, 8:10], posi[:], [t_pos, t_cst])
        freq = const("freq")
        red = []
        for i in range(2):
            u, k, r = ang[:, i, 0, :], ang[:, i, 1, :], cs[:, i, :, :]
            du = ts(u, freq, st[:, 8 + i:9 + i], None, ALU.mult, after=[d])
            for j, (sh, add) in enumerate(((0.0, 0.0), (0.25, math.pi / 2))):
                a = ts(k, u, 1.0 / TWO_PI, sh, ALU.mult, ALU.add, after=[du])
                a = ts(k, k, MAGIC, -MAGIC, ALU.add, ALU.add, after=[a])
                a = stt(r[:, 2 + j, :], k, -C1, u, ALU.mult, ALU.add, after=[a])
                a = stt(r[:, 2 + j, :], k, -C2, r[:, 2 + j, :], ALU.mult, ALU.add, after=[a])
                a = stt(r[:, 2 + j, :], k, -C3, r[:, 2 + j, :], ALU.mult, ALU.add, after=[a])
                a = ts(r[:, 2 + j, :], r[:, 2 + j, :], add, math.pi, ALU.add, ALU.min, after=[a])
                a = ts(r[:, 2 + j, :], r[:, 2 + j, :], -math.pi, None, ALU.max, after=[a])
                du = a
            d = a
            red.append(a)
        t_cs = act(cs[:, :, 0:2, :], cs[:, :, 2:4, :], ACT.Sin, red)
        lm = st[:, 16:32]
        junk = ar(17024, 4, 64)
        d = tt(junk[:, 0, :], lamv[:, 0, :], lamv[:, 1, :], ALU.mult, [t_lam])
        d2 = tt(junk[:, 1, :], lamv[:, 2, :], lamv[:, 3, :], ALU.mult)
        d = rsum(lm[:, 0:2], junk[:, 0:2, :], [d2])
        a = act(lm[:, 2:4], lm[:, 0:2], ACT.Exp, [d])
        t_nlam = stt(lm[:, 4:5], lm[:, 3:4], -(0.8 - 0.6 * math.exp(0.0)), lm[:, 2:3], ALU.add, ALU.subtract, [a])
        nlam = lm[:, 4:5]

        t_h = norm_turn(X, [t_x], G_ATT, HT)

        w_in = A["w_in"][0]

        def rope(buf, i, after):
            v = buf[:, i, :].rearrange("p (m d) -> p m d", d=64)
            t1, t2 = v[:, :, 0:8], v[:, :, 8:16]
            s = cs[:, i, 0, :].unsqueeze(1).broadcast_to([128, 16, 8])
            c = cs[:, i, 1, :].unsqueeze(1).broadcast_to([128, 16, 8])
            a = tt(rt[:, 0, 0], t1, s, ALU.mult, [*after, t_cs])
            b = tt(rt[:, 0, 1], t2, s, ALU.mult)
            c1 = tt(t1, t1, c, ALU.mult, [b])
            c2 = tt(t2, t2, c, ALU.mult)
            e1 = tt(t1, t1, rt[:, 0, 1], ALU.subtract, [c2])
            return [e1, tt(t2, t2, rt[:, 0, 0], ALU.add)]

        def project(key, dst, after, cc=0, K=8):
            res = []

            def fin(i, b, m):
                e = evac(dst[:, i, cc:cc + 512], b.ap, [m])
                b.free = [e]
                res.append(e)
            run_all(wide(key, HT, after, fin))
            return res

        e_q = [project("q", Q, t_h, cc=512 * j) for j in range(2)]
        e_k = [project("k", Kn, t_h, cc=512 * j) for j in range(2)]
        t_qT, t_kT = [], []
        for i in range(2):
            r = rope(Q, i, [e_q[0][i], e_q[1][i]])
            t_qT.append(turn(lambda k: Q[:, i, 128 * k:128 * k + 128], QT, 8, i, None, r, []))
            r = rope(Kn, i, [e_k[0][i], e_k[1][i]])
            t_kT.append(turn(lambda k: Kn[:, i, 128 * k:128 * k + 128], KT, 8, i, None, r, []))
        e_v = [project("v", V, t_h, cc=512 * j) for j in range(2)]
        e_p = project("pool", UP, t_h)

        def softmax_pairs(s, n, scale, after, o):
            mx, sm = st[:, o:o + n], st[:, o + n:o + 2 * n]
            d = rmax(mx, s, after)
            d = ts(mx, mx, -scale, None, ALU.mult, after=[d])
            for j in range(n):
                a = act(s[:, j, :], s[:, j, :], ACT.Exp, [d] if j == 0 else [], bias=mx[:, j:j + 1],
                        scale=scale, acc=sm[:, j:j + 1])
            return a

        cm = const("cm")
        AN = Q
        wk_free = [[], []]
        st_free = [[], []]
        wt_free = [[], []]
        e_a = {}

        def attn1(n):
            i, hp = divmod(n, 4)
            kend = 128 * (i + 1)
            nk = i + 1
            par = n % 2
            S = wk(1024 * par, 4, 256)[:, :, 0:kend]
            b = scb.take()
            bv = b.ap.rearrange("p c (h n) -> p c h n", h=2)
            for hh in range(2):
                for c in range(2):
                    h = 2 * hp + hh
                    m = mm(bv[:, c, hh, 0:kend], QT[64 * c:64 * c + 64, h, i * 128:i * 128 + 128],
                           KT[64 * c:64 * c + 64, h, 0:kend], True, True,
                           [*b.free, *t_qT[i], *t_kT[0], *t_kT[i]])
            sv = bv.rearrange("p c h n -> p (c h) n")[:, :, 0:kend]
            d = tt(S, sv, cm[:, 256 - kend:256].unsqueeze(1).broadcast_to([128, 4, kend]), ALU.add,
                   [m, *wk_free[par]])
            b.free = [d]
            o = 32 + 8 * par
            a = softmax_pairs(S, 4, 0.125, [d], o)
            yield
            r = st[:, 48 + 4 * par:52 + 4 * par]
            d = recip(r, st[:, o + 4:o + 8], [a])
            d = ts(r[:, 2:4], r[:, 2:4], nlam, None, ALU.mult, after=[d, t_nlam])
            for hh in range(2):
                d1 = ts(S[:, hh, :], S[:, hh, :], r[:, hh:hh + 1], None, ALU.mult, after=[d])
            for hh in range(2):
                d = stt(S[:, hh, :], S[:, 2 + hh, :], r[:, 2 + hh:3 + hh], S[:, hh, :], ALU.mult, ALU.add,
                        [d1] if hh == 0 else [])
            yield
            b = tpb.take()
            for hh in range(2):
                for kt in range(nk):
                    j = hh * nk + kt
                    m = tr(b.ap[:, 128 * j:128 * j + 128], S[:, hh, 128 * kt:128 * kt + 128],
                           [d, *b.free] if j == 0 else [])
            wT = wk(2048 + 512 * par, 512)
            e = acp(wT[:, 0:256 * nk], b.ap[:, 0:256 * nk], [m, *wt_free[par]])
            b.free = [e]
            wk_free[par] = [m]
            yield
            b = ob.take()
            for hh in range(2):
                for kt in range(nk):
                    j = hh * nk + kt
                    h = 2 * hp + hh
                    m = mm(b.ap[:, 128 * hh:128 * hh + 128], wT[:, 128 * j:128 * j + 128],
                           V[:, kt, 128 * h:128 * h + 128], kt == 0, kt == nk - 1,
                           [e, *b.free, *e_v[0], *e_v[1]] if j == 0 else [])
            wt_free[par] = [m]
            e = cp(AN[:, i, 256 * hp:256 * hp + 256], b.ap[:, 0:256], [m])
            b.free = [e]
            e_a.setdefault(i, []).append(e)
            yield

        def staggered(make, count):
            live = {}
            for n in range(count + 2):
                if n < count:
                    live[n] = make(n)
                    next(live[n], None)
                    yield
                if n - 1 in live:
                    next(live[n - 1], None)
                    yield
                if n - 2 in live:
                    for _ in live.pop(n - 2):
                        pass
                    yield
                if n - 1 in live:
                    next(live[n - 1], None)
                    yield

        e_g = []

        def sig_part(o, a, after):
            return act(o, a, ACT.Tanh, after, scale=0.5)

        def gates1():
            def fin(j):
                def f(i, b, m):
                    g = GT[:, i, 512 * j:512 * j + 512]
                    e = sig_part(g, b.ap, [m])
                    b.free = [e]
                    e_g.append(ts(g, g, 0.5, 0.5, ALU.mult, ALU.add, after=[e]))
                return f
            for j in range(4):
                yield from wide("gate", HT, t_h, fin(j))

        def weave(main, fill, ratio):
            acc = 0.0
            for _ in main:
                acc += ratio
                while acc >= 1.0:
                    acc -= 1.0
                    next(fill, None)
            for _ in fill:
                pass

        def pool_branch():
            pm = const("pool").rearrange("p (g n t) -> p g n t", g=4, n=3)
            for g in range(4):
                b = big.take()
                u = [UP[:, i, 128 * g:128 * g + 128] for i in range(2)]
                mm(b.ap[:, 0:128], u[0], pm[:, g, 0, :], True, True, [*e_p, *b.free])
                mm(b.ap[:, 128:256], u[0], pm[:, g, 1, :], True, False)
                m = mm(b.ap[:, 128:256], u[1], pm[:, g, 2, :], False, True)
                e = evac(DT[:, g, :], b.ap[:, 0:256], [m])
                b.free = [e]
                yield e

        e_d = list(pool_branch())
        weave(staggered(attn1, 8), gates1(), 0.45)

        MG = Kn
        e_m = []
        for i in range(2):
            av = AN[:, i, :].rearrange("p (h d) -> p h d", h=8)
            sq = wk(2048 * i, 8, 128)
            s8 = st[:, 64 + 16 * i:80 + 16 * i]
            d = tt(sq, av, av, ALU.mult, [*e_a[i], *wk_free[0], *wk_free[1], *wt_free[0], *wt_free[1]])
            d = rsum(s8[:, 0:8], sq, [d])
            d = ts(s8[:, 0:8], s8[:, 0:8], 1.0 / 128, EPS, ALU.mult, ALU.add, after=[d])
            d = recip(s8[:, 8:16], s8[:, 0:8], [d])
            lam_init = 0.8 - 0.6 * math.exp(0.0)
            a = act(s8[:, 0:8], s8[:, 8:16], ACT.Sqrt, [d], scale=(1.0 - lam_init) ** 2)
            d = tt(av, av, s8[:, 0:8].unsqueeze(2).broadcast_to([128, 8, 128]), ALU.mult, [a])
            d = tt(av, av, subg[:].unsqueeze(1).broadcast_to([128, 8, 128]), ALU.mult, [d, t_bc])
            d_a = tt(AN[:, i, :], AN[:, i, :], GT[:, i, 0:1024], ALU.mult, [d, *e_g])
            parts = []
            for g2 in range(2):
                b = big.take()
                for gg in range(2):
                    g = 2 * g2 + gg
                    m = mm(b.ap[:, 256 * gg:256 * gg + 256], DT[:, g, i * 128:i * 128 + 128], wpool[:, g, :],
                           True, True, [*e_d, *b.free, t_ws])
                o = MG[:, i, 512 * g2:512 * g2 + 512]
                e = tt(o, b.ap, psc[:, 512 * g2:512 * g2 + 512], ALU.mult, [m, t_bc, *t_kT[0], *t_kT[1]])
                b.free = [e]
                d = tt(o, o, GT[:, i, 1024 + 512 * g2:1536 + 512 * g2], ALU.mult, [e, *e_g])
                parts.append(d)
            e_m.append(tt(MG[:, i, :], MG[:, i, :], AN[:, i, :], ALU.add, [*parts, d_a]))
        MT = ars(4096, 6144, 8, 256)
        t_mT = []
        for i in range(2):
            t_mT += turn(lambda k: MG[:, i, 128 * k:128 * k + 128], MT, 8, i, None, [e_m[i]], wt_free[0] + wt_free[1])

        def residual_wide(key, hT, after):
            res = []

            def fin(j):
                def f(i, b, m):
                    xo = X[:, i, 512 * j:512 * j + 512]
                    e = tt(xo, b.ap, xo, ALU.add, [m])
                    b.free = [e]
                    res.append(e)
                return f
            for j in range(2):
                run_all(wide(key, hT, after, fin(j)))
            return res

        t_x1 = residual_wide("out", MT, t_mT)
        t_h2 = norm_turn(X, t_x1, G_MLP, HT)

        ZT = ars(0, 8192, 32, 256)
        z_t = []

        def z_fin(j):
            def f(b, bv, m, m0):
                o = ZT[:, 2 * j:2 * j + 2, :]
                a = act(o.f, bv, ACT.Relu, [m, *t_mT, *t_x1])
                b.free = [a]
                z_t.append(split_f(o, [tt(o.f, o.f, o.f, ALU.mult, [a])]))
            return f
        for j in range(16):
            run_all(tall("up", HT, t_h2, z_fin(j)))

        def residual_rows(key, hT, ntile, z_of):
            bs = [big.take() for _ in range(4)]
            for k0 in range(0, ntile, 2):
                w, t = take(key)
                for i in range(2):
                    for j in range(2):
                        b = bs[2 * i + j]
                        for k in range(2):
                            kk = k0 + k
                            m = mm3(b.ap, hT[:, kk, i * 128:i * 128 + 128], w[:, k, 512 * j:512 * j + 512],
                                    kk == 0, kk == ntile - 1, [*t, *z_of(kk), *(b.free if kk == 0 else [])])
                        b.last = m
                done.append(m)
                yield
            res = []
            for i in range(2):
                for j in range(2):
                    b = bs[2 * i + j]
                    xo = X[:, i, 512 * j:512 * j + 512]
                    e = tt(xo, b.ap, xo, ALU.add, [b.last])
                    b.free = [e]
                    res.append(e)
            rows_out.extend(res)

        MEM = ar(16384, 2, 1024)
        MEMT = wks(0, 2048, 8, 256)
        t_mem = load("act", "mem", (MEM, A["mem_2"][0].rearrange("(i p) d -> p i d", p=128)), after=t_mT)
        rows_out = []
        t_mt = []

        def memory_turn():
            for i in range(2):
                d = rms_rows(MEM[:, i, :], i, MEM[:, i, :], [t_mem], 8 + 4 * i, junk=XN[:, i, :], after2=t_h2)
                yield
                for k0 in (0, 4):
                    t_mt.extend(turn(lambda k: MEM[:, i, 128 * (k + k0):128 * (k + k0) + 128], MEMT[:, k0:k0 + 4, :],
                                     4, i, G_MEM[:, k0:k0 + 4], [d], e_m, pool=small))
                    yield
        weave(residual_rows("down", ZT, 32, lambda kk: [z_t[kk // 2]]), memory_turn(), 0.5)
        t_x2 = list(rows_out)

        t_xf = []
        for i in range(2):
            d = rms_rows(X[:, i, :], i, XN[:, i, :], t_x2, 4 * i)
            t_xf.append(tt(X[:, i, :], XN[:, i, :], grow[:], ALU.mult, [d, t_grow]))
        t_grow2 = load("act", "grow2", (grow[:], A["ln_final_g_2"].rearrange("(a n) -> a n", a=1)
                                        .broadcast_to([128, 1024])), after=t_xf)

        QA = ar(0, 4, 256)
        KSW = ar(1024, 2, 256)
        VSW = ar(1536, 2, 2, 128)
        XC = ar(2048, 2, 256)
        Z = ar(2560, 2, 16, 30)
        GN = ar(4000, 2, 24)
        AL = ar(3584, 256)
        QB = ar(4096, 2, 256)
        KB = ar(4608, 2, 256)
        EB = ar(5120, 2, 256)
        EN = ar(5632, 2, 256)
        EL = ar(6144, 2, 256)
        VB = ar(6656, 2, 512)
        RB = ar(7680, 2, 512)
        MRG = ar(8704, 16, 256)
        KX = ar(12800, 4, 256)
        VX = ar(13824, 2, 512)
        ONT = ars(2560, 14848, 4, 256)
        OGT = ars(15872, 16896, 4, 256)
        OG = XN[:].rearrange("p i n -> p (i n)")[:, 0:1024].rearrange("p (i n) -> p i n", i=2)

        t_kx, t_vx = [], []

        def kx_fin(j):
            def f(b, bv, m, m0):
                e = evac(KX[:, 2 * j:2 * j + 2, :], bv, [m])
                b.free = [e]
                t_kx.append(e)
            return f
        for j in range(2):
            run_all(tall("kx", MEMT, [*t_mt, *t_x2], kx_fin(j)))

        def vx_fin(i, b, m):
            e = evac(VX[:, i, :], b.ap, [m])
            b.free = [e]
            t_vx.append(e)
        run_all(wide("vx", MEMT, t_mt, vx_fin))
        t_memdone = done[-1]

        t_h = norm_turn(X, t_xf, G_MIX, HT)
        w_in = A["w_in_2"][0]
        t_qa = []

        def qa_fin(j):
            def f(b, bv, m, m0):
                e = act(QA[:, 2 * j:2 * j + 2, :], bv, ACT.Copy, [m, *t_x2], scale=0.125)
                b.free = [e]
                t_qa.append(e)
            return f
        for j in range(2):
            run_all(tall("qa", HT, t_h, qa_fin(j)))
        t_z = []
        z_prev = []

        def kvc_fin(b, bv, m, m0):
            nonlocal z_prev
            kct = ar(4096, 2, 256)
            ek = evac(kct, bv, [m, *t_x2])
            b.free = [ek]
            for c in range(2):
                e2 = load("pool", f"xc{c}", *[pr for h in range(2) for pr in (
                    (XC[0:64, h, :], kct[64 * h:64 * h + 64, c, :]),
                    (XC[64:128, h, 0:255], kct[64 * h:64 * h + 64, c, 1:256]))], after=[ek, *z_prev])
                for h in range(2):
                    for half in range(2):
                        sv = XC[:, h, 16 * half:16 * half + 240].rearrange("p (n j e) -> p j n e", n=15, j=8)[:, :, :, 0]
                        d = tt(Z[:, c, 8 * half:8 * half + 8, 15 * h:15 * h + 15], sv,
                               POS[c][:, 8 * half:8 * half + 8].unsqueeze(2).broadcast_to([128, 8, 15]), ALU.add,
                               [e2, t_vc])
                t_z.append(d)
                z_prev = [d]
        run_all(tall("kvc", HT, t_h, kvc_fin))

        def kv_unit(key, br):
            w, t = take(key)
            b = big.take()
            m = turned(w, 0, t, HT, b.ap[:, 0:256], b, 8, t_h)
            e1 = evac(KSW[:, br, :], b.ap[:, 0:256], [m])
            b.free = [e1]
            b = big.take()
            for i in range(2):
                for k in range(8):
                    m = mm3(b.ap[:, 128 * i:128 * i + 128], HT[:, k, i * 128:i * 128 + 128], w[:, k, 128:256],
                            k == 0, k == 7, b.free)
            done.append(m)
            e2 = evac(VSW[:, br], b.ap[:, 0:256].rearrange("p (a n) -> p a n", a=2), [m])
            b.free = [e2]
            return e1, e2
        e_ks, e_vs = kv_unit("kvs", 0)
        e_kw, e_vw = kv_unit("kvw", 1)
        w, t = take("small")
        b = big.take()
        for i in range(2):
            for k in range(8):
                m = mm3(b.ap[:, 64 * i:64 * i + 40], HT[:, k, i * 128:i * 128 + 128], w[:, k, :], k == 0, k == 7,
                        [*t, *b.free])
        done.append(m)
        bv = b.ap[:, 0:128].rearrange("p (a n) -> p a n", a=2)
        ALN = st[:, 96:128].rearrange("p (i n) -> p i n", i=2)
        e_aln = cp(ALN, bv[:, :, 24:40], [m])
        d = tt(GN[:], bv[:, :, 0:24], gateb[:].unsqueeze(1).broadcast_to([128, 2, 24]), ALU.add, [t_bc])
        b.free = [d]
        a = sig_part(GN[:], GN[:], [d])
        t_gn = ts(GN[:], GN[:], 0.5, 0.5, ALU.mult, ALU.add, after=[a])
        b = small.take()
        for i in range(2):
            m = tr(b.ap[0:16, 128 * i:128 * i + 128], ALN[:, i, :], [e_aln, *b.free])
        e_al = evac(AL[0:16, :], b.ap[0:16, 0:256], [m])
        b.free = [e_al]

        KC = ar(3840, 2, 15)
        VC2 = ar(3872, 2, 64)
        HC = ar(17920, 2, 30)
        Z2 = [ars(8704 + 480 * c, 2560 + 480 * c, 16, 30) for c in range(2)]
        t_z2 = [split_f(Z2[c], [t_z[c], t_memdone]) for c in range(2)]
        t_c = []
        for c in range(2):
            w, t = take(("w1k", "w1v")[c])
            b = big.take()
            for j in range(16):
                m = mm3(b.ap[:, 0:30], w[:, j, :], Z2[c][:, j, :], j == 0, j == 15,
                        [*t, t_z2[c], *b.free] if j == 0 else [])
            done.append(m)
            x_, y_ = HC[:, c, :], ar(17984 + 32 * c, 30)
            e = cp(x_, b.ap[:, 0:30], [m])
            b.free = [e]
            d = tt(y_, x_, x_, ALU.mult, [e])
            d = ts(y_, y_, 0.044715, 1.0, ALU.mult, ALU.add, after=[d])
            d = tt(y_, y_, x_, ALU.mult, [d])
            a = act(y_, y_, ACT.Tanh, [d], scale=math.sqrt(2.0 / math.pi))
            d = ts(y_, y_, 0.5, 0.5, ALU.mult, ALU.add, after=[a])
            t_g = tt(x_, x_, y_, ALU.mult, [d])
            b = big.take()
            if c == 0:
                m = mm(b.ap[:, 0:30], w2[:, 0:2, :].rearrange("p a d -> p (a d)"), x_, True, True,
                       [t_g, t_ws, *b.free])
                e = cp(KC[0:64, 0, :], b.ap[0:64, 0:15], [m])
                e = cp(KC[64:128, 0, :], b.ap[64:128, 15:30])
            else:
                for h in range(2):
                    m = mm(b.ap[0:15, 64 * h:64 * h + 64], x_[:, 15 * h:15 * h + 15], w2[:, 2, :], True, True,
                           [t_g, t_ws, *b.free])
                e = cp(VC2[0:15], b.ap[0:15, 0:128].rearrange("p (h d) -> p h d", h=2), [m])
            b.free = [e]
            t_c.append(e)

        e_qk = []

        def qk_fin(j):
            def f(b, bv, m, m0):
                e = evac((QB, KB)[j], bv, [m, *t_z])
                b.free = [e]
                e_qk.append(e)
            return f
        for j in range(2):
            run_all(tall("qkb", HT, t_h, qk_fin(j)))
        e_vb = project("vb", VB, t_h)
        e_rb = project("rb", RB, t_h)

        e_mg = []

        def merges():
            def fin(j):
                def f(b, bv, m, m0):
                    o = MRG[:, 2 * j:2 * j + 2, :]
                    e = sig_part(o, bv, [m, t_memdone, *t_c])
                    b.free = [e]
                    e_mg.append(ts(o, o, 0.5, 0.5, ALU.mult, ALU.add, after=[e]))
                return f
            for j in range(8):
                yield from tall("merge", HT, t_h, fin(j), pool=mbanks)

        dist = const("dist")
        cdist = const("cdist").rearrange("p (i n) -> p i n", i=2)
        cmask = const("cmask").rearrange("p (i n) -> p i n", i=2)
        e_on = []

        wk_free = [[t_memdone], [t_memdone]]
        wt_free = [[t_memdone], [t_memdone]]

        def nsa(n):
            i, g = divmod(n, 4)
            kend = 128 * (i + 1)
            nk = i + 1
            par = n % 2
            S = wk(1024 * par, 4, 256)
            b = scb.take()
            bv = b.ap.rearrange("p c (h n) -> p c h n", h=2)
            b2 = (ob.take(), tpb.take())
            for v in range(2):
                q = QA[64 * v:64 * v + 64, g, i * 128:i * 128 + 128]
                for br in range(2):
                    m = mm(bv[:, v, br, 0:kend], q, KSW[64 * v:64 * v + 64, br, 0:kend], True, True,
                           [*b.free, *t_qa, e_ks, e_kw])
            for v in range(2):
                q = QA[64 * v:64 * v + 64, g, i * 128:i * 128 + 128]
                m2 = mm(b2[v].ap[:, 0:15], q, KC[64 * v:64 * v + 64, 0, :], True, True,
                        [*b2[v].free, t_c[0]])
            dd = dist[:, 0:128] if i == 0 else dist[:, 128:384]
            pc = wk(3840 + 32 * par, 2, 16)[:, :, 0:15]
            for v in range(2):
                slope = 2.0 ** -(4 * v + g + 1)
                dc = stt(pc[:, v, :], cdist[:, i, :], -slope, b2[v].ap[:, 0:15], ALU.mult,
                         ALU.add, [m2, *wk_free[par]])
                b2[v].free = [dc]
            for v in range(2):
                slope = 2.0 ** -(4 * v + g + 1)
                d = stt(S[:, 2 * v:2 * v + 2, 0:kend], dd.unsqueeze(1).broadcast_to([128, 2, kend]), -slope,
                        bv[:, v, :, 0:kend], ALU.mult, ALU.add, [m, *wk_free[par]])
            b.free = [d]
            o = 32 + 12 * par
            Sv = S[:, :, 0:kend]
            d1 = rmax(st[:, o + 4:o + 6], pc, [dc])
            d1 = rmax(st[:, o:o + 4], Sv, [d])
            d1 = ts(st[:, o:o + 6], st[:, o:o + 6], -1.0, None, ALU.mult, after=[d1])
            for j in range(6):
                s_ = Sv[:, j, :] if j < 4 else pc[:, j - 4, :]
                a = act(s_, s_, ACT.Exp, [d1] if j == 0 else [], bias=st[:, o + j:o + j + 1],
                        acc=st[:, o + 6 + j:o + 7 + j])
            yield
            d = recip(st[:, o + 6:o + 12], st[:, o + 6:o + 12], [a])
            gv = GN[:, i, :].rearrange("p (v g b) -> p v g b", v=2, g=4)[:, :, g, :]
            r4 = st[:, o + 6:o + 10].rearrange("p (v b) -> p v b", v=2)
            d = tt(r4, r4, gv[:, :, 1:3], ALU.mult, [d, t_gn])
            d = tt(st[:, o + 10:o + 12], st[:, o + 10:o + 12], gv[:, :, 0], ALU.mult)
            for j in range(4):
                d = ts(Sv[:, j, :], Sv[:, j, :], st[:, o + 6 + j:o + 7 + j], None, ALU.mult,
                       after=[d] if j == 0 else [])
            for v in range(2):
                d = stt(pc[:, v, :], pc[:, v, :], st[:, o + 10 + v:o + 11 + v], cmask[:, i, :], ALU.mult,
                        ALU.mult)
            yield
            es = []
            for v in range(2):
                b = (tpb, ob)[v].take()
                for br in range(2):
                    for kt in range(nk):
                        j = br * nk + kt
                        m = tr(b.ap[:, 128 * j:128 * j + 128], S[:, 2 * v + br, 128 * kt:128 * kt + 128],
                               [d, *b.free] if j == 0 else [])
                wT = wk(2048 + 512 * v, 512)
                e = acp(wT[:, 0:256 * nk], b.ap[:, 0:256 * nk], [m, *wt_free[v]])
                b.free = [e]
                es.append(e)
            b = tpb.take()
            for v in range(2):
                m = tr(b.ap[0:15, 128 * v:128 * v + 128], pc[:, v, :], b.free)
            cT = wk(3072, 2, 128)
            e = acp(cT[0:15], b.ap[0:15, 0:256].rearrange("p (v n) -> p v n", v=2), [m, *wt_free[0], *wt_free[1]])
            b.free = [e]
            wk_free[par] = [m]
            yield
            for v in range(2):
                wT = wk(2048 + 512 * v, 512)
                b = ob.take()
                h = 4 * v + g
                hr = slice(64 * (h % 2), 64 * (h % 2) + 64)
                oo = b.ap[hr, 0:128]
                first = True
                for br in range(2):
                    for kt in range(nk):
                        j = br * nk + kt
                        m = mm(oo, VSW[:, br, kt, 64 * v:64 * v + 64], wT[:, 128 * j:128 * j + 128],
                               first, False, [es[v], e, *b.free, e_vs, e_vw] if first else [])
                        first = False
                m = mm(oo, VC2[0:15, v, :], cT[0:15, v, :], False, True, [t_c[1]])
                wt_free[v] = [m]
                o_ = ONT[hr, h // 2, i * 128:i * 128 + 128]
                e2 = split_psum(o_, oo, [m], t_c)
                b.free = [e2]
                e_on.append(e2)
            yield

        e_og = []

        def gla():
            reset = const("reset")
            b = gbanks.take()
            for c in range(2):
                m = mm(b.ap[:, 256 * c:256 * c + 256], walp[:, 128 * c:128 * c + 128], AL[0:16, :], True, True,
                       [e_al, t_ws, *b.free])
            for c in range(2):
                d = ts(EB[:, c, :], b.ap[:, 256 * c:256 * c + 256], BA[:, c:c + 1], None, ALU.add, after=[m, t_vc])
            b.free = [d]
            a = act(EN[:], EB[:], ACT.Abs, [d])
            a = act(EN[:], EN[:], ACT.Exp, [a], scale=-1.0)
            a = act(EN[:], EN[:], ACT.Ln, [a, t_eps], bias=eps[:, 0:1])
            d = ts(EB[:], EB[:], 0.0, None, ALU.min, after=[a])
            d = tt(EN[:], EB[:], EN[:], ALU.subtract, [d])
            d = ts(EN[:], EN[:], 1.0 / 16.0, None, ALU.mult, after=[d])
            for c in range(2):
                d = P.put("dve", lambda c=c: nc.vector.tensor_tensor_scan(EB[:, c, :], reset, EN[:, c, :], 0.0,
                                                                           ALU.mult, ALU.add), [d])
            ev = EB[:].rearrange("p c (n t) -> p (c n) t", t=64)
            lv = EL[:].rearrange("p c (n t) -> p (c n) t", t=64)
            d = tt(lv, ev[:, :, 63:64].broadcast_to([128, 8, 64]), ev, ALU.subtract, [d])
            act(EL[:], EL[:], ACT.Exp, [d])
            a1 = act(EN[:], EB[:], ACT.Exp, scale=-1.0)
            a = act(EB[:], EB[:], ACT.Exp, [a1])
            yield
            d = stt(QB[:], EB[:], 0.125, QB[:], ALU.mult, ALU.mult, [a, *e_qk])
            d = tt(EN[:], EN[:], KB[:], ALU.mult)
            d_el = tt(EL[:], EL[:], KB[:], ALU.mult)
            b = gbanks.take()
            for i in range(2):
                for c in range(2):
                    m = tr(b.ap[:, 256 * i + 128 * c:256 * i + 128 * c + 128], EL[:, c, 128 * i:128 * i + 128],
                           [d_el, *b.free])
            kn = KB
            e_kn = acp(kn[:], b.ap.rearrange("p (a n) -> p a n", a=2), [m])
            b.free = [e_kn]
            yield
            views = [None, EL[:, 0, :].rearrange("p (a e) -> p a e", a=2),
                     EL[:, 1, :].rearrange("p (a e) -> p a e", a=2),
                     XC[:, 0, :].rearrange("p (a e) -> p a e", a=2)]
            d_s = [None] * 4
            for n in range(3):
                lo = 64 * (n % 2)
                b = gbanks.take()
                for c in range(2):
                    m = mm(b.ap[:, 256 * c:256 * c + 256], kn[lo:lo + 64, n // 2, 128 * c:128 * c + 128],
                           VB[lo:lo + 64, n // 2, 256 * c:256 * c + 256], True, True, [e_kn, *e_vb, *b.free])
                for c in range(2):
                    for h in range(2):
                        rr = slice(64 * h, 64 * h + 64)
                        o = views[n + 1][rr, c, :]
                        inc = b.ap[rr, 256 * c + 128 * h:256 * c + 128 * h + 128]
                        if n == 0:
                            d = cp(o, inc, [m])
                        else:
                            d = stt(o, views[n][rr, c, :], EB[rr, c, 64 * n + 63:64 * n + 64], inc, ALU.mult,
                                    ALU.add, [m, d_s[n], *t_z])
                b.free = [d]
                d_s[n + 1] = d
                yield
            up, un = const("up"), const("un")
            AT = ar(1024 + 17920 - 1024 - 512, 4, 128)
            for i in range(2):
                bb = (gbanks.take(), gbanks.take())
                at = AT
                for h in (0, 2, 1, 3):
                    p, q = h % 2, h // 2
                    rr = slice(64 * p, 64 * p + 64)
                    m = mm(bb[p].ap[:, 128 * q:128 * q + 128], EN[rr, q, 128 * i:128 * i + 128],
                           QB[rr, q, 128 * i:128 * i + 128], True, True, [d_el, *bb[p].free, *e_ao])
                for p in range(2):
                    d = tt(at[:, 2 * p:2 * p + 2, :], bb[p].ap[:, 0:256].rearrange("p (h n) -> p h n", h=2),
                           up.unsqueeze(1).broadcast_to([128, 2, 128]), ALU.min, [m])
                    bb[p].free = [d]
                d = tt(at, at, un.unsqueeze(1).broadcast_to([128, 4, 128]), ALU.max, [d])
                yield
                bb = (gbanks.take(), gbanks.take())
                for p in range(2):
                    for q in range(2):
                        h = 2 * q + p
                        m = mm(bb[p].ap[:, 128 * q:128 * q + 128], at[:, 2 * p + q, :],
                               VB[:, i, 128 * h:128 * h + 128], q == 0, False,
                               [d, *bb[p].free, *e_vb])
                    for half in range(2):
                        n = 2 * i + half
                        if n == 0:
                            continue
                        for q in range(2):
                            m = mm(bb[p].ap[64 * half:64 * half + 64, 128 * q:128 * q + 128],
                                   QB[64 * p:64 * p + 64, q, 64 * n:64 * n + 64], views[n][64 * p:64 * p + 64, q, :],
                                   False, True, [d_s[n]])
                og = OG[:, i, :].rearrange("p (h d) -> p h d", h=4)
                ogp = OG[:, i, :].rearrange("p (q s d) -> p q s d", q=2, s=2)
                for p in range(2):
                    e = acp(ogp[:, :, p, :], bb[p].ap[:, 0:256].rearrange("p (q d) -> p q d", q=2), [m])
                    bb[p].free = [e]
                yield
                s4 = st[:, 64 + 8 * i:72 + 8 * i]
                sq = MRGtmp[i]
                d = tt(sq, og, og, ALU.mult, [e])
                d = rsum(s4[:, 0:4], sq, [d])
                d = ts(s4[:, 0:4], s4[:, 0:4], 1.0 / 128, EPS, ALU.mult, ALU.add, after=[d])
                d = recip(s4[:, 4:8], s4[:, 0:4], [d])
                a = act(s4[:, 0:4], s4[:, 4:8], ACT.Sqrt, [d])
                rv = RB[:, i, :]
                a2 = sig_part(sq.rearrange("p h d -> p (h d)"), rv, [d, *e_rb])
                d = tt(og, og, s4[:, 0:4].unsqueeze(2).broadcast_to([128, 4, 128]), ALU.mult, [a])
                d = tt(og, og, glag[:].unsqueeze(1).broadcast_to([128, 4, 128]), ALU.mult, [d, t_bc])
                sf = sq.rearrange("p h d -> p (h d)")
                d1 = ts(sf, sf, 0.5, 0.5, ALU.mult, ALU.add, after=[a2])
                d1 = tt(rv, rv, sf, ALU.mult, [d1])
                d = tt(OG[:, i, :], OG[:, i, :], rv, ALU.mult, [d1, d])
                e_ao.append(d)
                yield
            for i in range(2):
                e_og.extend(turn(lambda k: OG[:, i, 128 * k:128 * k + 128], OGT, 4, i, None, [e_ao[i]], e_ao, pool=gbanks))
                yield

        e_ao = []
        MRGtmp = [XN[:, 1, 512 * i:512 * i + 512].rearrange("p (h d) -> p h d", h=4) for i in range(2)]
        gbanks, mbanks = Banks([]), Banks([])
        gbanks.b, mbanks.b = big.b[0:2], big.b[2:4]

        def alternate(a, b, na, nb):
            while True:
                alive = False
                for gen, k in ((a, na), (b, nb)):
                    for _ in range(k):
                        try:
                            next(gen)
                            alive = True
                        except StopIteration:
                            break
                if not alive:
                    return
                yield

        weave(alternate(staggered(nsa, 8), gla(), 3, 1), merges(), 0.45)

        MX = ars(4096, 6144, 8, 256)
        TMP = XN[:].rearrange("p i (a n) -> p (i a) n", n=256)
        t_mx = []
        for half in range(2):
            ds = {}

            def mix_fin(dst, go, half=half):
                def f(b, bv, m, m0):
                    o = slice(4 * half + m0, 4 * half + m0 + 2)
                    e = tt(dst[:, o, :], bv, MRG[:, go + 4 * half + m0:go + 4 * half + m0 + 2, :], ALU.mult,
                           [m, *e_mg, *e_og, *e_on, *e_ao])
                    b.free = [e]
                    ds.setdefault(m0, []).append(e)
                return f
            run_all(tall("bn", ONT, e_on, mix_fin(TMP, 0), K=4, nb=4))
            run_all(tall("bg", OGT, e_og, mix_fin(MX.f, 8), K=4, nb=4))
            for m0 in (0, 2):
                v = MX[:, 4 * half + m0:4 * half + m0 + 2, :]
                e = tt(v.f, v.f, TMP[:, 4 * half + m0:4 * half + m0 + 2, :], ALU.add, ds[m0])
                t_mx.append(split_f(v, [e]))
        t_x3 = residual_wide("out2", MX, t_mx)

        t_h = norm_turn(X, t_x3, G_X, HT, free=t_mx)
        QX = ar(0, 4, 256)
        OX = ars(1024, 2048, 4, 256)
        t_qx = []

        def qx_fin(j):
            def f(b, bv, m, m0):
                e = evac(QX[:, 2 * j:2 * j + 2, :], bv, [m, *t_x3])
                b.free = [e]
                t_qx.append(e)
            return f
        for j in range(2):
            run_all(tall("xq", HT, t_h, qx_fin(j)))
        e_ox = []
        sc = 128.0 ** -0.5
        wk_f = [[], []]
        for n in range(2):
            S = wk(0, 4, 256)
            b = scb.take()
            bv = b.ap.rearrange("p h (i n) -> p h i n", i=2)
            for hh in range(2):
                h = 2 * n + hh
                for i in range(2):
                    m = mm(bv[:, hh, i, :], QX[:, h, i * 128:i * 128 + 128], KX[:, h, :], True, True,
                           [*b.free, *t_qx, *t_kx])
            d = cp(S, bv.rearrange("p h i n -> p (h i) n"), [m, *wk_f[0], *e_on])
            b.free = [d]
            a = softmax_pairs(S, 4, sc, [d], 32)
            d = recip(st[:, 48:52], st[:, 36:40], [a])
            for j in range(4):
                d = ts(S[:, j, :], S[:, j, :], st[:, 48 + j:49 + j], None, ALU.mult, after=[d] if j == 0 else [])
            for hh in range(2):
                b = tpb.take()
                for i in range(2):
                    for mt in range(2):
                        m = tr(b.ap[:, 256 * mt + 128 * i:256 * mt + 128 * i + 128],
                               S[:, 2 * hh + i, 128 * mt:128 * mt + 128], [d, *b.free])
                pT = wk(1024 + 512 * hh, 2, 256)
                e = acp(pT, b.ap.rearrange("p (a n) -> p a n", a=2), [m, *wk_f[1]])
                b.free = [e]
                b = ob.take()
                for mt in range(2):
                    h = 2 * n + hh
                    m2 = mm(b.ap[:, 0:256], VX[:, mt, 128 * h:128 * h + 128], pT[:, mt, :], mt == 0, mt == 1,
                            [e, *b.free, *t_vx])
                e = split_psum(OX[:, 2 * n + hh, :], b.ap[:, 0:256], [m2], t_x3)
                b.free = [e]
                e_ox.append(e)
            wk_f = [[m], [m2]]
        rows_out = []
        run_all(residual_rows("xo", OX, 4, lambda kk: [e_ox[kk]]))
        t_x4 = list(rows_out)

        t_h = norm_turn(X, t_x4, G_FFN, HT, free=t_qx)
        FT = ars(4096, 4096 + 5632, 22, 256)
        cw = VC[:, 1, 0:66].rearrange("p (t c) -> p t c", t=3)
        e_f = []
        fw_free = [[], []]
        for j in range(11):
            bu, bg = big.take(), big.take()
            for b in (bu, bg):
                w, t = take("up2")
                for h in range(2):
                    b.m = turned(w, 128 * h, t, HT, b.ap[:, 256 * h:256 * h + 256], b, 8, t_h)
                done.append(b.m)
            par = j % 2
            U = wk(2048 * par, 2, 256)
            Y = wk(2048 * par + 512, 2, 256)
            for h in range(2):
                ch = 2 * j + h
                u = bu.ap[:, 256 * h:256 * h + 256]
                d = ts(U[:, h, :], u, cw[:, 2, ch:ch + 1], CB[:, ch:ch + 1], ALU.mult, ALU.add,
                       after=[bu.m, *fw_free[par], *e_ox, t_vc])
                d = stt(U[:, h, 1:256], u[:, 0:255], cw[:, 1, ch:ch + 1], U[:, h, 1:256], ALU.mult, ALU.add, [d])
                d = stt(U[:, h, 2:256], u[:, 0:254], cw[:, 0, ch:ch + 1], U[:, h, 2:256], ALU.mult, ALU.add, [d])
            bu.free = [d]
            d0 = d
            p1 = gtt(Y, U, U, ALU.mult, [d])
            p1 = P.put("pool", lambda Y=Y: nc.gpsimd.tensor_scalar(Y, Y, 0.044715, 1.0, ALU.mult, ALU.add), [p1])
            p1 = gtt(Y, Y, U, ALU.mult, [p1])
            a = act(Y, Y, ACT.Tanh, [p1], scale=math.sqrt(2.0 / math.pi))
            a = P.put("pool", lambda Y=Y: nc.gpsimd.tensor_scalar(Y, Y, 0.5, 0.5, ALU.mult, ALU.add), [a])
            o = FT[:, 2 * j:2 * j + 2, :]
            p1 = gtt(Y, Y, U, ALU.mult, [a])
            d = tt(o.f, Y, bg.ap.rearrange("p (a n) -> p a n", a=2), ALU.mult, [p1, bg.m])
            bg.free = [d]
            d = split_f(o, [d])
            fw_free[par] = [d]
            e_f.append(d)
        rows_out = []
        run_all(residual_rows("down2", FT, 22, lambda kk: [e_f[kk // 2]]))
        t_x5 = list(rows_out)
        assert len(done) == len(plan)

        s_out = sem("s_out")
        outs = []
        ov = out[0].rearrange("(i p) d -> p i d", p=128)
        for i in range(2):
            d = rms_rows(X[:, i, :], i, XN[:, i, :], [*t_x5, *t_h], 4 * i)
            d = tt(XN[:, i, :], XN[:, i, :], grow[:], ALU.mult, [d, t_grow2])
            outs.append(P.dma("sp", [lambda i=i: nc.sync.dma_start(ov[:, i, :], XN[:, i, :])], [d], s_out))
        P.q["sp"].append((None, (outs[-1],), None, None))
        P.emit()


_INS = ['x', 'positions', 'norm_attn_g', 'w_in', 'lam_q1', 'lam_k1', 'lam_q2', 'lam_k2', 'subln_g', 'w_pool',
        'pool_scale', 'w_out', 'norm_mlp_g', 'w_up', 'w_down', 'final_norm_g', 'mem_2', 'ln_mix_g_2', 'w_in_2',
        'nsa_gate_b_2', 'cmp_pos_k_2', 'cmp_w1_k_2', 'cmp_w2_k_2', 'cmp_pos_v_2', 'cmp_w1_v_2', 'cmp_w2_v_2',
        'gla_w_alpha2_2', 'gla_b_alpha_2', 'gla_norm_g_2', 'w_branch_nsa_2', 'w_branch_gla_2', 'w_out_2',
        'ln_x_g_2', 'ln_mem_g_2', 'w_xq_2', 'w_xkv_2', 'w_xo_2', 'ln_ffn_g_2', 'w_up_2', 'conv_w_2', 'conv_b_2',
        'w_down_2', 'ln_final_g_2']


def kernel(**inputs):
    import numpy as _np
    import concourse.bacc as _bacc
    from concourse import mybir as _mybir
    from concourse.bass_utils import run_bass_kernel_spmd as _run

    nc = _bacc.Bacc("TRN2", target_bir_lowering=False, num_devices=1)
    arrays, args = {}, {}
    for name in _INS:
        a = _np.ascontiguousarray(inputs[name])
        arrays[f"in_{name}_dram"] = a
        args[name] = nc.dram_tensor(f"in_{name}_dram", a.shape, _mybir.dt.from_np(a.dtype),
                                    kind="ExternalInput").ap()
    a = shape_constants()
    arrays["shape_constants"] = a
    args["shape_constants"] = nc.dram_tensor("shape_constants", a.shape, _mybir.dt.float32,
                                             kind="ExternalInput").ap()
    o = nc.dram_tensor("out_0_dram", (1, 256, 1024), _mybir.dt.float32, kind="ExternalOutput").ap()
    two_blocks(nc, args, o)
    r = _run(nc, [arrays], core_ids=[0])
    return r.results[0]["out_0_dram"]
```

```python
import math
from contextlib import ExitStack

import numpy as np
import concourse.bass as bass
from concourse import mybir

F32 = mybir.dt.float32
I32 = mybir.dt.int32
ALU = mybir.AluOpType
ACT = mybir.ActivationFunctionType
AX = mybir.AxisListType.X
EPS = 1e-6
F32R = mybir.dt.float32r
NLOW = 4
NHIGH = 4
UNIT = 2048
ROPE_THETA = 500000.0
TWO_PI = 2.0 * math.pi
C1 = 6.28125
C2 = float(np.float32(np.round((TWO_PI - C1) * 2 ** 21) / 2 ** 21))
C3 = float(np.float32(TWO_PI - C1 - C2))
MAGIC = 12582912.0
FAR = 1e34
NSA_RATIO = 1.4
OUT_RATIO = 1.0
HOOK_AT = 6
TILE_POOL = 2
COMPRESS = "cqccclcqqffcfcf"
TILE_AHEAD = 2
POOL_SPLITS = ("vb", "rb", "merge", "qkb", "bn", "bg", "v", "pool", "gate")
TWO_NORMS = "M0MM0M1M0M10MM1MM1MM"
ATTN_RATIO = 0.85

CONST = {}
_at = 0
for _name, _width in (("ident", 128), ("cm", 256), ("dist", 384), ("cdist", 30), ("cmask", 30), ("up", 128),
                      ("un", 128), ("reset", 256), ("freq", 8)):
    CONST[_name] = (_at, _width)
    _at += _width
NCONST = _at
NPOOL = 1536


def shape_constants():
    c = np.zeros((128, NCONST + NPOOL), np.float32)

    def put(name, a):
        o, w = CONST[name]
        c[:, o:o + w] = np.asarray(a, np.float32).reshape(128, w)

    p = np.arange(128)
    put("ident", np.eye(128))
    causal = p[None, :] <= p[:, None]
    put("cm", np.concatenate([np.zeros((128, 128)), np.where(causal, 0.0, -1e30)], 1))
    d0 = np.where(causal, p[:, None] - p[None, :], FAR)
    d1 = np.where(np.arange(256)[None, :] <= p[:, None] + 128, p[:, None] + 128 - np.arange(256)[None, :], FAR)
    put("dist", np.concatenate([d0, d1], 1))
    end = np.arange(15) * 16 + 31
    t = p[:, None] + 128 * np.arange(2)[None, :]
    dc = t[:, :, None] - end
    put("cdist", np.where(dc >= 0, dc, FAR))
    put("cmask", dc >= 0)
    ok = (p[:, None] <= p[None, :]) & (p[:, None] // 64 == p[None, :] // 64)
    put("up", np.where(ok, 3.4028235e38, 0.0))
    put("un", np.where(ok, -3.4028235e38, 0.0))
    put("reset", np.broadcast_to((np.arange(256) % 64 != 0), (128, 256)))
    put("freq", np.broadcast_to(np.float32(ROPE_THETA) ** (-np.arange(0, 16, 2, dtype=np.float32) / 16), (128, 8)))
    pool = np.zeros((128, 4, 3, 128), np.float64)
    for g, w in enumerate((2, 4, 8, 16)):
        for n, (so, to) in enumerate(((0, 0), (0, 128), (128, 128))):
            s, tt = so + p[:, None], to + p[None, :]
            pool[:, g, n] = np.where((s <= tt) & (s > tt - w), 1.0 / np.minimum(tt + 1, w), 0.0) - (s == tt)
    c[:, NCONST:] = pool.reshape(128, NPOOL)
    return c


class Tok:

    def __init__(self, eng=None, sem=None, val=None):
        self.eng, self.sem, self.val, self.sig = eng, sem, val, False


class Prog:

    def __init__(self, nc, ctx):
        self.nc = nc
        self.ctx = ctx
        self.q = {e: [] for e in ("pe", "act", "dve", "pool", "sp")}
        self.sem = {e: ctx.enter_context(nc.semaphore("s_" + e)) for e in self.q}
        self.dmas = {}

    def put(self, eng, fn, after):
        t = Tok(eng=eng)
        self.q[eng].append((fn, tuple(after), t, None))
        return t

    def dma(self, eng, fns, after, sem):
        for fn in fns:
            self.dmas[sem] = self.dmas.get(sem, 0) + 16
            self.q[eng].append((fn, tuple(after), None, sem))
        return Tok(sem=sem, val=self.dmas[sem])

    def emit(self):
        for q in self.q.values():
            for _, after, _, _ in q:
                for t in after:
                    if t.sem is None:
                        t.sig = True
        for e, q in self.q.items():
            n = 0
            for _, _, t, _ in q:
                if t is not None and t.sig:
                    n += 1
                    t.val = n
        block = self.ctx.enter_context(self.nc.Block())

        def run(name):
            def body(eng):
                seen = {}
                for fn, after, t, dsem in self.q[name]:
                    need = {}
                    for a in after:
                        s = a.sem if a.sem is not None else self.sem[a.eng]
                        if a.val > seen.get(s, 0) and a.val > need.get(s, 0):
                            need[s] = a.val
                    for s, v in need.items():
                        eng.wait_ge(s, v)
                        seen[s] = v
                    if fn is None:
                        continue
                    ins = fn()
                    if dsem is not None:
                        ins.then_inc(dsem, 16)
                    elif t.sig:
                        ins.then_inc(self.sem[name], 1)
            return body

        block.tensor(run("pe"))
        block.scalar(run("act"))
        block.vector(run("dve"))
        block.gpsimd(run("pool"))
        block.sync(run("sp"))


class Bank:
    def __init__(self, ap):
        self.ap = ap
        self.free = []


class Split:

    def __init__(self, hi, lo, f):
        self.hi, self.lo, self.f = hi, lo, f

    def __getitem__(self, k):
        return Split(self.hi[k], self.lo[k], self.f[k])


class Pair:

    def __init__(self, banks, ap):
        self.banks, self.ap = banks, ap

    @property
    def free(self):
        return [t for b in self.banks for t in b.free]

    @free.setter
    def free(self, toks):
        for b in self.banks:
            b.free = toks


class Banks:

    def __init__(self, aps):
        self.b = [Bank(a) for a in aps]
        self.n = 0

    def take(self):
        b = self.b[self.n % len(self.b)]
        self.n += 1
        return b


def two_blocks(nc, A, out):
    ctx = ExitStack()
    with ctx:
        P = Prog(nc, ctx)

        def sb(name, *shape, dt=F32):
            return ctx.enter_context(nc.sbuf_tensor(name, list(shape), dt))

        def sem(name):
            return ctx.enter_context(nc.semaphore(name))

        def mm(o, l, r, start, stop, after=()):
            return P.put("pe", lambda: nc.tensor.matmul(o, l, r, start=start, stop=stop,
                                                        skip_group_check=True), after)

        def tr(o, i, after=()):
            n = i.shape[0]
            return P.put("pe", lambda: nc.tensor.transpose(o, i, ident[0:n, 0:n]), after)

        def act(o, i, f, after=(), bias=0.0, scale=1.0, acc=None):
            if acc is None:
                return P.put("act", lambda: nc.scalar.activation(o, i, f, bias=bias, scale=scale), after)
            return P.put("act", lambda: nc.scalar.activation(o, i, f, bias=bias, scale=scale, accum_out=acc), after)

        def tt(o, a, b, op, after=()):
            return P.put("dve", lambda: nc.vector.tensor_tensor(o, a, b, op), after)

        def gtt(o, a, b, op, after=()):
            return P.put("pool", lambda: nc.gpsimd.tensor_tensor(o, a, b, op), after)

        def ts(o, a, s1, s2, op0, op1=None, after=()):
            if op1 is None:
                return P.put("dve", lambda: nc.vector.tensor_scalar(o, a, s1, None, op0), after)
            return P.put("dve", lambda: nc.vector.tensor_scalar(o, a, s1, s2, op0, op1), after)

        def stt(o, a, s, b, op0, op1, after=()):
            return P.put("dve", lambda: nc.vector.scalar_tensor_tensor(o, a, s, b, op0, op1), after)

        def cp(o, a, after=()):
            return P.put("dve", lambda: nc.vector.tensor_copy(o, a), after)

        def acp(o, a, after=()):
            return act(o, a, ACT.Copy, after)

        def rmax(o, a, after=()):
            return P.put("dve", lambda: nc.vector.reduce_max(o, a, AX), after)

        def rsum(o, a, after=()):
            return P.put("dve", lambda: nc.vector.reduce_sum(o, a, AX), after)

        def recip(o, a, after=()):
            return P.put("dve", lambda: nc.vector.reciprocal(o, a), after)

        def load(eng, name, *pairs, after=()):
            e = {"sp": nc.sync, "act": nc.scalar, "pool": nc.gpsimd}[eng]
            return P.dma(eng, [(lambda d=d, s=s: e.dma_start(d, s)) for d, s in pairs], after, sem("l_" + name))

        def both(name, *shape):
            at = (nc.sbuf_base + 31) // 32 * 32
            f = sb(name + "_f", *shape)
            return f, nc.alloc_sbuf_tensor_at(name + "_r", list(shape), F32R, offset=at)

        cst = sb("cst", 128, NCONST)

        def const(name):
            o, w = CONST[name]
            return cst[:, o:o + w]

        ident = const("ident")
        X = sb("X", 128, 2, 1024)
        XN = sb("XN", 128, 2, 1024)
        HTh = sb("HTh", 128, 8, 256, dt=F32R)
        HTf, HTl = both("HTl", 128, 8, 256)
        HT = Split(HTh[:], HTl[:], HTf[:])
        high = [sb(f"high{i}", 128, UNIT, dt=F32R) for i in range(NHIGH)]
        low = [both(f"low{i}", 128, UNIT) for i in range(NLOW)]
        grow = sb("grow", 128, 1024)
        psc = grow
        subg = sb("subg", 128, 128)
        glag = sb("glag", 128, 128)
        gateb = sb("gateb", 128, 24)
        lamv = sb("lamv", 128, 4, 64)
        wpool = sb("wpool", 128, 4, 256)
        walp = sb("walp", 16, 256)
        w2 = sb("w2", 128, 3, 64)
        VR = sb("VR", 128, 2, 128)
        VC = sb("VC", 128, 2, 88)
        posi = sb("posi", 128, 2, dt=I32)
        st = sb("st", 128, 128)
        AR, ARr = both("AR", 128, 18432)
        WK, WKr = both("WK", 128, 4096)
        eps = sb("eps", 128, 2)

        def part(t, size, off, shape):
            n = int(np.prod(shape))
            assert off + n <= size, (off, shape)
            v = t[:, off:off + n]
            if len(shape) == 1:
                return v
            names = "abcd"[:len(shape)]
            return v.rearrange("p (" + " ".join(names) + ") -> p " + " ".join(names),
                               **{names[k]: shape[k] for k in range(len(shape) - 1)})

        def ar(off, *shape):
            return part(AR, 18432, off, shape)

        def wk(off, *shape):
            return part(WK, 4096, off, shape)

        def ars(off, off2, *shape):
            return Split(part(ARr, 18432, off, shape), part(ARr, 18432, off2, shape), part(AR, 18432, off2, shape))

        def wks(off, off2, *shape):
            return Split(part(WKr, 4096, off, shape), part(WKr, 4096, off2, shape), part(WK, 4096, off2, shape))

        PS = ctx.enter_context(nc.psum_tensor("PS", [128, 8, 512], F32))
        big = Banks([PS[:, i, :] for i in range(4)])
        scb = Banks([])
        scb.half = [Bank(PS[:, 4, :]), Bank(PS[:, 5, :])]
        scb.b = [Pair(scb.half, PS[:, 4:6, :])]
        tpb = Banks([PS[:, 6, :]])
        ob = Banks([PS[:, 7, :]])
        small = Banks([])
        small.b = [tpb.b[0], ob.b[0]]

        plan = []

        def v3(ap, K, n):
            return ap[:, 0:K * n].rearrange("p (k n) -> p k n", k=K)

        def block_of(w, k0, K, c0, n):
            return w[128 * k0:128 * (k0 + K), c0:c0 + n].rearrange("(k p) n -> p k n", p=128)

        def planned(key, w, k0, K, c0, n):
            plan.append((key, K, n, [(lambda a: v3(a, K, n), block_of(w, k0, K, c0, n))]))

        def plan_wide(key, w, c0, n=1024):
            for c in range(c0, c0 + n, 512):
                for k0 in range(0, w.shape[0] // 128, 4):
                    planned(key, w, k0, 4, c, 512)

        def plan_tiles(key, w):
            for k0 in range(0, w.shape[0] // 128, 4):
                for c in (0, 512):
                    planned(key, w, k0, 4, c, 512)

        def plan_tall(key, w, c0, n):
            for c in range(c0, c0 + n, 256):
                planned(key, w, 0, 8, c, 256)

        def plan_rows(key, w):
            for k0 in range(0, w.shape[0] // 128, 2):
                planned(key, w, k0, 2, 0, 1024)

        w1, w2_ = A["w_in"][0], A["w_in_2"][0]
        plan_wide("q", w1, 0)
        plan_wide("k", w1, 1024)
        plan_wide("v", w1, 2048)
        plan_wide("pool", w1, 3072, 512)
        plan_wide("gate", w1, 4608, 1024)
        plan_wide("gate", w1, 3584, 1024)
        plan_tiles("out", A["w_out"][0])
        plan_tall("up", A["w_up"][0], 0, 4096)
        plan_rows("down", A["w_down"][0])
        plan_tall("kx", A["w_xkv_2"][0], 0, 512)
        plan_wide("vx", A["w_xkv_2"][0], 512, 512)
        for mp in range(2):
            plan.append(("qa", 8, 256, [
                (lambda a, v=v, k=k: v3(a, 8, 256)[:, k, :].rearrange("p (g v d) -> p g v d", g=2, v=2)[:, :, v],
                 w2_[128 * k:128 * k + 128, 256 * v + 128 * mp:256 * v + 128 * mp + 128]
                 .rearrange("p (g d) -> p g d", g=2)) for v in range(2) for k in range(8)]))
        planned("kvc", w2_, 0, 8, 512, 256)
        planned("kvs", w2_, 0, 8, 768, 256)
        planned("kvw", w2_, 0, 8, 1024, 256)
        plan.append(("small", 8, 40, [(lambda a: v3(a, 8, 40)[:, :, 0:24], block_of(w2_, 0, 8, 1280, 24)),
                                      (lambda a: v3(a, 8, 40)[:, :, 24:40], block_of(w2_, 0, 8, 2840, 16))]))
        planned("w1k", A["cmp_w1_k_2"][0], 0, 16, 0, 128)
        planned("qkb", w2_, 0, 8, 1304, 256)
        planned("w1v", A["cmp_w1_v_2"][0], 0, 16, 0, 128)
        planned("qkb", w2_, 0, 8, 1560, 256)
        plan_wide("vb", w2_, 1816, 512)
        plan_wide("rb", w2_, 2328, 512)
        plan_tall("merge", w2_, 2856, 2048)
        for c in range(0, 1024, 512):
            planned("bn", A["w_branch_nsa_2"][0], 0, 4, c, 512)
            planned("bg", A["w_branch_gla_2"][0], 0, 4, c, 512)
        plan_tiles("out2", A["w_out_2"][0])
        plan_tall("xq", A["w_xq_2"][0], 0, 512)
        plan_tiles("xo", A["w_xo_2"][0])
        for j in range(11):
            planned("up2", A["w_up_2"][0], 0, 8, 256 * j, 256)
            planned("up2", A["w_up_2"][0], 0, 8, 2816 + 256 * j, 256)
        plan_rows("down2", A["w_down_2"][0])

        low_sem = [sem(f"low_s{i}") for i in range(NLOW)]
        loaded, ready, done = [], [], []
        state = {"ev": 0}

        def load_unit():
            m = len(loaded)
            key, K, n, pieces = plan[m]
            slot = low[m % NLOW][0]
            free = [done[m - NLOW]] if m >= NLOW else []
            loaded.append(P.dma("sp", [(lambda d=f(slot[:]), src=src: nc.sync.dma_start(d, src))
                                       for f, src in pieces], free, low_sem[m % NLOW]))

        def split_unit(on_pool=False):
            m = len(ready)
            key, K, n, _ = plan[m]
            f, r = low[m % NLOW]
            h = high[m % NHIGH]
            free = [done[m - NHIGH]] if m >= NHIGH else []
            half = K * n // 2
            for o in (0, half):
                a = acp(h[:, o:o + half], f[:, o:o + half], [loaded[m], *free])
                d = (gtt if on_pool or key in POOL_SPLITS else tt)(r[:, o:o + half], f[:, o:o + half], h[:, o:o + half],
                                                        ALU.subtract, [a])
            ready.append([d])

        def ahead(upto=None, on_pool=0):
            m = len(done)
            while len(loaded) < min(len(plan), m + NLOW):
                load_unit()
            while upto is not None and len(ready) < min(len(plan), upto, m + NHIGH):
                split_unit(on_pool > upto - 1 - len(ready))

        def take(key, skip=0):
            m = len(done) + skip
            assert plan[m][0] == key, (plan[m][0], key)
            while len(loaded) < min(len(plan), len(done) + NLOW):
                load_unit()
            while len(ready) < min(len(plan), m + 3, len(done) + NHIGH):
                split_unit()
            K, n = plan[m][1:3]
            return Split(v3(high[m % NHIGH][:], K, n), v3(low[m % NLOW][1][:], K, n),
                         v3(low[m % NLOW][0][:], K, n)), ready[m]

        def mm3(o, l, r, first, last, after=()):
            mm(o, l.hi, r.hi, first, False, after)
            mm(o, l.hi, r.lo, False, False)
            return mm(o, l.lo, r.hi, False, last)

        def split_psum(dst, src, after, free=()):
            a = acp(dst.hi, src, [*after, *free])
            return tt(dst.lo, src, dst.hi, ALU.subtract, [a])

        def split_f(dst, after):
            a = acp(dst.hi, dst.f, after)
            return tt(dst.lo, dst.f, dst.hi, ALU.subtract, [a])

        def evac(o, a, after, scale=None):
            state["ev"] ^= 1
            return acp(o, a, after) if state["ev"] else cp(o, a, after)

        def dep(after, k, i):
            return after(k, i) if callable(after) else after

        def wide(key, hT, after, fin, K=8, pool=None):
            bs = [(pool or big).take() for _ in range(2)]
            for k0 in range(0, K, 4):
                w, t = take(key)
                for i in range(2):
                    for k in range(4):
                        m = mm3(bs[i].ap, hT[:, k0 + k, i * 128:i * 128 + 128], w[:, k, :], k0 + k == 0,
                                k0 + k == K - 1, [*t, *dep(after, k0 + k, i), *(bs[i].free if k0 == 0 else [])])
                    if i == 1:
                        done.append(m)
                    if k0 == K - 4:
                        fin(i, bs[i], m)
                    yield

        def run_all(g):
            for _ in g:
                pass

        def turned(w, c, t, hT, o, b, K, after, n=256, width=128):
            for k in range(K):
                m = mm3(o, w[:, k, c:c + width], hT[:, k, 0:n], k == 0, k == K - 1,
                        [*t, *dep(after, k, None), *b.free])
            return m

        def tall(key, hT, after, fin, K=8, pool=None, nb=2):
            w, t = take(key)
            for m0 in range(0, nb, 2):
                b = (pool or big).take()
                for h in range(2):
                    m = turned(w, 128 * (m0 + h), t, hT, b.ap[:, 256 * h:256 * h + 256], b, K, after)
                    if h == 0:
                        yield
                if m0 + 2 >= nb:
                    done.append(m)
                fin(b, b.ap.rearrange("p (a n) -> p a n", a=2), m, m0)
                yield

        xd = A["x"][0].rearrange("(i p) d -> p i d", p=128)
        t_x0 = load("sp", "x0", (X[:, 0, :], xd[:, 0, :]))
        o_id = CONST["ident"][0]
        t_cst0 = load("act", "id", (cst[:, o_id:o_id + 128], A["shape_constants"][:, o_id:o_id + 128]))
        t_g0 = load("act", "g0", (VR[0:8, 0, :], A["norm_attn_g"][0].rearrange("(k p) -> k p", p=128)))
        t_x1_ = load("sp", "x1", (X[:, 1, :], xd[:, 1, :]))
        t_xi = [t_x0, t_x1_]
        load_unit()
        load_unit()
        assert o_id == 0
        t_cst = load("sp", "cst", (cst[:, 128:NCONST], A["shape_constants"][:, 128:NCONST]))
        ahead()

        vc_ready = []
        t_eps = P.put("dve", lambda: nc.vector.memset(eps[:, 0:1], 1.0), ())
        b = tpb.take()
        m1 = tr(b.ap[:, 0:8], VR[0:8, 0, :], [t_cst0, t_g0])
        t_vc0 = cp(VC[:, 0, 0:8], b.ap[:, 0:8], [m1])
        b.free = [t_vc0]

        def columns_of_rows():
            b = qbanks.take()
            tr(b.ap[:, 0:88], VR[0:88, 0, :], [t_vr, *b.free])
            m2 = tr(b.ap[:, 128:210], VR[0:82, 1, :])
            cp(VC[:, 0, 8:88], b.ap[:, 8:88], [m2])
            e = cp(VC[:, 1, 0:82], b.ap[:, 128:210])
            b.free = [e]
            return e
        G_ATT, G_MLP, G_MIX, G_X, G_MEM, G_FFN = (VC[:, 0, 8 * j:8 * j + 8] for j in range(6))
        CB = VC[:, 0, 48:70]
        BA = VC[:, 0, 70:72]
        POS = (VC[:, 0, 72:88], VC[:, 1, 66:82])

        def rms_rows(x, i, xn, after, s0, junk=None, after2=()):
            a = act(xn if junk is None else junk, x, ACT.Square, [*after, *after2], acc=st[:, s0:s0 + 1])
            d = ts(st[:, s0 + 1:s0 + 2], st[:, s0:s0 + 1], 1.0 / 1024, EPS, ALU.mult, ALU.add, [a])
            d = recip(st[:, s0 + 2:s0 + 3], st[:, s0 + 1:s0 + 2], [d])
            a = act(st[:, s0 + 3:s0 + 4], st[:, s0 + 2:s0 + 3], ACT.Sqrt, [d])
            return ts(xn, x, st[:, s0 + 3:s0 + 4], None, ALU.mult, after=[a])

        def turn(src, dst, n, i, gain, after, free, pool=None):
            out_t = []
            pool = pool or big
            for k0 in range(0, n, 4):
                b = pool.take()
                kk = min(4, n - k0)
                for k in range(kk):
                    m = tr(b.ap[:, 128 * k:128 * k + 128], src(k0 + k), [*after, *b.free, t_cst0] if k == 0 else [])
                v = b.ap[:, 0:128 * kk].rearrange("p (k n) -> p k n", k=kk)
                o = dst[:, k0:k0 + kk, i * 128:i * 128 + 128]
                if gain is not None:
                    e = tt(o.f, v, gain[:, k0:k0 + kk].unsqueeze(2).broadcast_to([128, kk, 128]), ALU.mult,
                           [m, t_vc0, *vc_ready, *free])
                    b.free = [e]
                    e = split_f(o, [e])
                elif isinstance(dst, Split):
                    e = split_psum(o, v, [m], free)
                    b.free = [e]
                else:
                    e = evac(o, v, [m, *free])
                    b.free = [e]
                out_t.append(e)
            return out_t

        def squares(i, j, after, s0):
            return act(XN[:, i, 512 * j:512 * j + 512], X[:, i, 512 * j:512 * j + 512], ACT.Square, after,
                       acc=st[:, s0 + j:s0 + j + 1])

        def row_rms(i, after):
            s0 = 4 * i
            for j in range(2):
                a = squares(i, j, after[j], s0)
            d = ts(st[:, s0 + 2:s0 + 3], st[:, s0:s0 + 1], st[:, s0 + 1:s0 + 2], 1024.0 * EPS, ALU.add, ALU.add, [a])
            d = recip(st[:, s0 + 2:s0 + 3], st[:, s0 + 2:s0 + 3], [d])
            return act(st[:, s0 + 3:s0 + 4], st[:, s0 + 2:s0 + 3], ACT.Sqrt, [d], scale=1024.0)

        def scaled(i, a):
            return ts(XN[:, i, :], X[:, i, :], st[:, 4 * i + 3:4 * i + 4], None, ALU.mult, after=[a])

        def scaled_turn(i, a, gain, deps):
            d = scaled(i, a)
            for k0 in (0, 4):
                e = turn(lambda k: XN[:, i, 128 * (k + k0):128 * (k + k0) + 128], HT[:, k0:k0 + 4, :], 4, i,
                         gain[:, k0:k0 + 4], [d], [], pool=small)
                for k in range(k0, k0 + 4):
                    deps[i, k] = e
                yield

        def deps_of(deps):
            return lambda k, i: deps[i, k] if i is not None else deps[0, k] + deps[1, k]

        def chain(*gens):
            for g in gens:
                yield from g

        def weave(main, fill, ratio, until=None):
            acc = 0.0
            for _ in main:
                if until is not None and until():
                    break
                acc += ratio
                while acc >= 1.0:
                    acc -= 1.0
                    next(fill, None)
            for _ in fill:
                pass

        Q = ar(0, 2, 1024)
        Kn = ar(2048, 2, 1024)
        QT = ar(4096, 8, 256)
        KT = ar(6144, 8, 256)
        V = ar(8192, 2, 1024)
        UP = ar(10240, 2, 512)
        DT = ar(11264, 4, 256)
        GT = ar(12288, 2, 2048)
        cs = ar(16384, 2, 4, 8)
        rt = ar(16448, 2, 2, 16, 8)

        def rows(v, k):
            return v.rearrange("(k p) -> k p", p=128)

        vr0 = [("norm_mlp_g", 8, 8), ("ln_mix_g_2", 16, 8), ("ln_x_g_2", 24, 8),
               ("ln_mem_g_2", 32, 8), ("ln_ffn_g_2", 40, 8), ("conv_b_2", 48, 22), ("gla_b_alpha_2", 70, 2)]
        pairs = [(VR[o:o + n, 0, :], rows(A[nm][0], n)) for nm, o, n in vr0]
        pairs.append((VR[72:88, 0, :], A["cmp_pos_k_2"][0].rearrange("(j e) d -> j (e d)", e=2)))
        for tap in range(3):
            pairs.append((VR[22 * tap:22 * tap + 22, 1, :], rows(A["conv_w_2"][0, tap], 22)))
        pairs.append((VR[66:82, 1, :], A["cmp_pos_v_2"][0].rearrange("(j e) d -> j (e d)", e=2)))
        t_vr = load("pool", "vr", *pairs)
        t_pos = P.dma("pool", [lambda: nc.gpsimd.dma_start(posi[:], A["positions"][0].rearrange("(i p) -> p i", p=128), allow_slow_non_contiguous=True)], [], sem("l_pos"))
        t_lam = load("pool", "lam", *[(lamv[:, j, :], A[nm][0:1].broadcast_to([128, 64]))
                                     for j, nm in enumerate(("lam_q1", "lam_k1", "lam_q2", "lam_k2"))])
        t_bc = load("pool", "bc", (subg[:], A["subln_g"][0:1].broadcast_to([128, 128])),
                    (glag[:], A["gla_norm_g_2"][0:1].broadcast_to([128, 128])),
                    (gateb[:], A["nsa_gate_b_2"][0:1].broadcast_to([128, 24])),
                    (psc[:], A["pool_scale"][0:1].broadcast_to([128, 1024])))
        t_ws = load("pool", "ws", (wpool[:], A["w_pool"][0].rearrange("g c d -> c g d")),
                    (walp[:], A["gla_w_alpha2_2"][0]),
                    (w2[:, 0, :], A["cmp_w2_k_2"][0]), (w2[:, 1, :], A["cmp_w2_k_2"][0]),
                    (w2[:, 2, :], A["cmp_w2_v_2"][0]))


        P.put("act", lambda: nc.scalar.activation(eps[:, 1:2], eps[:, 0:1], ACT.Sqrt), [t_eps])
        n0 = {}
        d = []
        for i in range(2):
            a = row_rms(i, [[t_xi[i]], [t_xi[i]]])
            d.append(scaled(i, a))
        for i, k0 in ((0, 0), (0, 4), (1, 0), (1, 4)):
            e = turn(lambda k: XN[:, i, 128 * (k + k0):128 * (k + k0) + 128], HT[:, k0:k0 + 4, :], 4, i,
                     G_ATT[:, k0:k0 + 4], [d[i]], [])
            for k in range(k0, k0 + 4):
                n0[i, k] = e
            if (i, k0) == (0, 0):
                ahead(1)
        ahead(2)
        t_h = deps_of(n0)

        def rope(buf, i, after):
            v = buf[:, i, :].rearrange("p (m d) -> p m d", d=64)
            t1, t2 = v[:, :, 0:8], v[:, :, 8:16]
            s = cs[:, i, 0, :].unsqueeze(1).broadcast_to([128, 16, 8])
            c = cs[:, i, 1, :].unsqueeze(1).broadcast_to([128, 16, 8])
            a = tt(rt[:, 0, 0], t1, s, ALU.mult, [*after, t_cs])
            b = tt(rt[:, 0, 1], t2, s, ALU.mult)
            c1 = tt(t1, t1, c, ALU.mult, [b])
            c2 = tt(t2, t2, c, ALU.mult)
            e1 = tt(t1, t1, rt[:, 0, 1], ALU.subtract, [c2])
            return [e1, tt(t2, t2, rt[:, 0, 0], ALU.add)]

        def project(key, dst, after, cc=0, K=8):
            res = []

            def fin(i, b, m):
                e = evac(dst[:, i, cc:cc + 512], b.ap, [m])
                b.free = [e]
                res.append(e)
            run_all(wide(key, HT, after, fin))
            return res

        def project_steps(key, dst, after, out_, n):
            for j in range(n):
                res = []

                def fin(i, b, m, cc=512 * j, res=res):
                    e = evac(dst[:, i, cc:cc + 512], b.ap, [m])
                    b.free = [e]
                    res.append(e)
                yield from wide(key, HT, after, fin)
                out_.append(res)

        def rope_steps(buf, e, dst, out_):
            for i in range(2):
                r = rope(buf, i, [e[0][i], e[1][i]])
                yield
                out_.append(turn(lambda k: buf[:, i, 128 * k:128 * k + 128], dst, 8, i, None, r, [], pool=qbanks))
                yield

        qbanks = Banks([])
        qbanks.b = [tpb.b[0], ob.b[0]]
        e_q, e_k, e_v, e_p, t_qT, t_kT = [], [], [], [], [], []
        run_all(project_steps("q", Q, t_h, e_q, 2))

        t_vc = columns_of_rows()
        vc_ready.append(t_vc)

        d = cp(st[:, 8:10], posi[:], [t_pos, t_cst])
        freq = const("freq")
        u, k, r = ar(16960, 2, 16), ar(16992, 2, 16), cs[:, :, 2:4, :].rearrange("p i j f -> p i (j f)")
        for i in range(2):
            for j in range(2):
                d = ts(u[:, i, 8 * j:8 * j + 8], freq, st[:, 8 + i:9 + i], None, ALU.mult,
                       after=[d] if i + j == 0 else [])
        for j, sh in enumerate((0.0, 0.25)):
            a = ts(k[:, :, 8 * j:8 * j + 8], u[:, :, 8 * j:8 * j + 8], 1.0 / TWO_PI, sh, ALU.mult, ALU.add, after=[d])
        a = ts(k, k, MAGIC, -MAGIC, ALU.add, ALU.add, after=[a])
        a = stt(r, k, -C1, u, ALU.mult, ALU.add, after=[a])
        a = stt(r, k, -C2, r, ALU.mult, ALU.add, after=[a])
        d = stt(r, k, -C3, r, ALU.mult, ALU.add, after=[a])
        for j, add in enumerate((0.0, math.pi / 2)):
            a = ts(r[:, :, 8 * j:8 * j + 8], r[:, :, 8 * j:8 * j + 8], add, math.pi, ALU.add, ALU.min, after=[d])
        red = [ts(r, r, -math.pi, None, ALU.max, after=[a])]
        t_cs = act(cs[:, :, 0:2, :], cs[:, :, 2:4, :], ACT.Sin, red)
        lm = st[:, 16:32]
        junk = ar(17024, 4, 64)
        d = tt(junk[:, 0, :], lamv[:, 0, :], lamv[:, 1, :], ALU.mult, [t_lam])
        d2 = tt(junk[:, 1, :], lamv[:, 2, :], lamv[:, 3, :], ALU.mult)
        d = rsum(lm[:, 0:2], junk[:, 0:2, :], [d2])
        a = act(lm[:, 2:4], lm[:, 0:2], ACT.Exp, [d])
        t_nlam = stt(lm[:, 4:5], lm[:, 3:4], -(0.8 - 0.6 * math.exp(0.0)), lm[:, 2:3], ALU.add, ALU.subtract, [a])
        nlam = lm[:, 4:5]

        weave(rope_steps(Q, e_q, QT, t_qT), project_steps("k", Kn, t_h, e_k, 2), 2.0)
        weave(rope_steps(Kn, e_k, KT, t_kT), project_steps("v", V, t_h, e_v, 2), 2.0)

        def softmax_pairs(s, n, scale, after, o):
            mx, sm = st[:, o:o + n], st[:, o + n:o + 2 * n]
            d = rmax(mx, s, after)
            d = ts(mx, mx, -scale, None, ALU.mult, after=[d])
            for j in range(n):
                a = act(s[:, j, :], s[:, j, :], ACT.Exp, [d] if j == 0 else [], bias=mx[:, j:j + 1],
                        scale=scale, acc=sm[:, j:j + 1])
            return a

        cm = const("cm")
        AN = Q
        wk_free = [[], []]
        st_free = [[], []]
        wt_free = [[], []]
        e_a = {}

        def attn1(n):
            i, hp = divmod(n, 4)
            kend = 128 * (i + 1)
            nk = i + 1
            par = n % 2
            S = wk(1024 * par, 4, 256)[:, :, 0:kend]
            b = scb.take()
            bv = b.ap.rearrange("p c (h n) -> p c h n", h=2)
            for hh in range(2):
                for c in range(2):
                    h = 2 * hp + hh
                    m = mm(bv[:, c, hh, 0:kend], QT[64 * c:64 * c + 64, h, i * 128:i * 128 + 128],
                           KT[64 * c:64 * c + 64, h, 0:kend], True, True,
                           [*b.free, *t_qT[i], *t_kT[0], *t_kT[i]])
            sv = bv.rearrange("p c h n -> p (c h) n")[:, :, 0:kend]
            d = tt(S, sv, cm[:, 256 - kend:256].unsqueeze(1).broadcast_to([128, 4, kend]), ALU.add,
                   [m, *wk_free[par], t_cst])
            b.free = [d]
            o = 32 + 8 * par
            a = softmax_pairs(S, 4, 0.125, [d], o)
            yield
            r = st[:, 48 + 4 * par:52 + 4 * par]
            d = recip(r, st[:, o + 4:o + 8], [a])
            d = ts(r[:, 2:4], r[:, 2:4], nlam, None, ALU.mult, after=[d, t_nlam])
            for hh in range(2):
                d1 = ts(S[:, hh, :], S[:, hh, :], r[:, hh:hh + 1], None, ALU.mult, after=[d])
            for hh in range(2):
                d = stt(S[:, hh, :], S[:, 2 + hh, :], r[:, 2 + hh:3 + hh], S[:, hh, :], ALU.mult, ALU.add,
                        [d1] if hh == 0 else [])
            yield
            b = tpb.take()
            for hh in range(2):
                for kt in range(nk):
                    j = hh * nk + kt
                    m = tr(b.ap[:, 128 * j:128 * j + 128], S[:, hh, 128 * kt:128 * kt + 128],
                           [d, *b.free] if j == 0 else [])
            wT = wk(2048 + 512 * par, 512)
            e = acp(wT[:, 0:256 * nk], b.ap[:, 0:256 * nk], [m, *wt_free[par]])
            b.free = [e]
            wk_free[par] = [m]
            yield
            b = ob.take()
            for hh in range(2):
                for kt in range(nk):
                    j = hh * nk + kt
                    h = 2 * hp + hh
                    m = mm(b.ap[:, 128 * hh:128 * hh + 128], wT[:, 128 * j:128 * j + 128],
                           V[:, kt, 128 * h:128 * h + 128], kt == 0, kt == nk - 1,
                           [e, *b.free, *e_v[0], *e_v[1]] if j == 0 else [])
            wt_free[par] = [m]
            e = cp(AN[:, i, 256 * hp:256 * hp + 256], b.ap[:, 0:256], [m])
            for hh in range(2):
                c = 64 + 16 * i + 2 * hp + hh
                a = act(wk(3072 + 128 * hh, 128), b.ap[:, 128 * hh:128 * hh + 128], ACT.Square, [e],
                        acc=st[:, c:c + 1])
            b.free = [a]
            e_a.setdefault(i, []).append(a)
            yield

        def staggered(make, count, hook=None):
            live = {}
            for n in range(count + 2):
                if n < count:
                    live[n] = make(n)
                    next(live[n], None)
                    yield
                if n - 1 in live:
                    next(live[n - 1], None)
                    yield
                if n - 2 in live:
                    for _ in live.pop(n - 2):
                        pass
                    yield
                    if hook is not None:
                        yield from hook(n - 2)
                if n - 1 in live:
                    next(live[n - 1], None)
                    yield

        e_g = {}

        def sig_part(o, a, after):
            return act(o, a, ACT.Tanh, after, scale=0.5)

        MG = Kn

        def gates1():
            def fin(j):
                def f(i, b, m):
                    g = GT[:, i, 512 * j:512 * j + 512]
                    e = sig_part(g, b.ap, [m])
                    b.free = [e]
                    d = ts(g, g, 0.5, 0.5, ALU.mult, ALU.add, after=[e])
                    if j >= 2:
                        e_g[i, j] = d
                        return
                    gv = g.rearrange("p (h d) -> p h d", h=4)
                    e_g[i, j] = gtt(gv, gv, subg[:].unsqueeze(1).broadcast_to([128, 4, 128]), ALU.mult, [d, t_bc])
                return f
            for j in (2, 3, 0, 1):
                yield from wide("gate", HT, t_h, fin(j), pool=gate_banks)

        def pool_out():
            for g2 in range(2):
                for i in range(2):
                    b = rest_banks.take()
                    for gg in range(2):
                        g = 2 * g2 + gg
                        m = mm(b.ap[:, 256 * gg:256 * gg + 256], DT[:, g, i * 128:i * 128 + 128], wpool[:, g, :],
                               True, True, [*e_d, *b.free, t_ws])
                    o = MG[:, i, 512 * g2:512 * g2 + 512]
                    e = tt(o, b.ap, psc[:, 512 * g2:512 * g2 + 512], ALU.mult, [m, t_bc, *t_kT[0], *t_kT[1]])
                    b.free = [e]
                    e_p2[i, g2] = gtt(o, o, GT[:, i, 1024 + 512 * g2:1536 + 512 * g2], ALU.mult,
                                      [e, e_g[i, 2 + g2]])
                    yield

        e_p2 = {}
        gate_banks, rest_banks = Banks([]), Banks([])
        gate_banks.b, rest_banks.b = big.b[0:2], big.b[2:4]

        t_pm = load("pool", "pm", (AR[:, 2048:2048 + NPOOL], A["shape_constants"][:, NCONST:NCONST + NPOOL]),
                    after=[*t_kT[0], *t_kT[1]])
        e_d = []

        def pool_branch():
            pm = ar(2048, 4, 3, 128)
            up_e = []

            def fin(i, b, m):
                e = evac(UP[:, i, :], b.ap, [m])
                b.free = [e]
                up_e.append(e)
            yield from wide("pool", HT, t_h, fin, pool=gate_banks)
            for g in range(4):
                b = rest_banks.take()
                u = [UP[:, i, 128 * g:128 * g + 128] for i in range(2)]
                mm(b.ap[:, 0:128], u[0], pm[:, g, 0, :], True, True, [*up_e, t_pm, *b.free])
                mm(b.ap[:, 128:256], u[0], pm[:, g, 1, :], True, False)
                m = mm(b.ap[:, 128:256], u[1], pm[:, g, 2, :], False, True)
                e = evac(DT[:, g, :], b.ap[:, 0:256], [m])
                b.free = [e]
                e_d.append(e)
                yield

        e_m = {}
        t_mT = {}
        MT = ars(4096, 6144, 8, 256)

        def merge_rows(i):
            s8 = st[:, 64 + 16 * i:80 + 16 * i]
            P.put("act", lambda: nc.scalar.activation(eps[:, 1:2], eps[:, 0:1], ACT.Sqrt), [t_eps])
            d = ts(s8[:, 0:8], s8[:, 0:8], 1.0 / 128, EPS, ALU.mult, ALU.add, after=e_a[i])
            d = recip(s8[:, 8:16], s8[:, 0:8], [d])
            lam_init = 0.8 - 0.6 * math.exp(0.0)
            a = act(s8[:, 0:8], s8[:, 8:16], ACT.Sqrt, [d], scale=(1.0 - lam_init) ** 2)
            yield
            for g2 in range(2):
                for h in range(4 * g2, 4 * g2 + 4):
                    hd = slice(128 * h, 128 * h + 128)
                    d = stt(AN[:, i, hd], AN[:, i, hd], s8[:, h:h + 1], GT[:, i, hd], ALU.mult, ALU.mult,
                            [a, e_g[i, g2]])
                hd = slice(512 * g2, 512 * g2 + 512)
                e_m[i, g2] = tt(MG[:, i, hd], MG[:, i, hd], AN[:, i, hd], ALU.add, [d, e_p2[i, g2]])
                yield

        def merge_turn(i):
            for g2 in range(2):
                e = turn(lambda k: MG[:, i, 128 * k + 512 * g2:128 * k + 512 * g2 + 128], MT[:, 4 * g2:4 * g2 + 4, :],
                         4, i, None, [e_m[i, g2]], wt_free[0] + wt_free[1], pool=small)
                for k in range(4):
                    t_mT[4 * g2 + k, i] = e
                yield

        def hook1(n):
            if n == HOOK_AT:
                yield from merge_rows(0)

        fill = chain(pool_branch(), gates1(), pool_out())
        for _ in range(2):
            next(fill)
        weave(staggered(attn1, 8, hook1), fill, ATTN_RATIO)
        m1 = merge_rows(1)
        next(m1)
        run_all(merge_turn(0))

        def residual_tiles(key, hT, after, K, out_):
            us = [take(key, a) for a in range(K // 2)]
            last = len(done) + len(us)
            bs = {(i, j): big.take() for i in range(2) for j in range(2)}
            steps = [(0, j, k0) for k0 in range(0, K, 4) for j in range(2)]
            steps += [(1, j, k0) for _, j, k0 in steps]
            for i, j, k0 in steps:
                b = bs[i, j]
                w, t = us[k0 // 2 + j]
                for k in range(4):
                    m = mm3(b.ap, hT[:, k0 + k, i * 128:i * 128 + 128], w[:, k, :], k0 + k == 0,
                            k0 + k == K - 1, [*t, *dep(after, k0 + k, i), *(b.free if k0 == 0 else [])])
                if i == 1:
                    done.append(m)
                if k0 == K - 4:
                    xo = X[:, i, 512 * j:512 * j + 512]
                    out_[i, j] = e = tt(xo, b.ap, xo, ALU.add, [m])
                    b.free = [e]
                if i == 1:
                    ahead(last + TILE_AHEAD, TILE_POOL)
                yield

        def raw_steps(x_e, gain, deps, nfree):
            for i in range(2):
                for j in range(2):
                    while (i, j) not in x_e:
                        yield
                    yield
                    e = turn(lambda k: X[:, i, 512 * j + 128 * k:512 * j + 128 * k + 128],
                             HT[:, 4 * j:4 * j + 4, :], 4, i, gain[:, 4 * j:4 * j + 4], [x_e[i, j]], [], pool=small)
                    for k in range(4 * j, 4 * j + 4):
                        deps[i, k] = e
                    a = squares(i, j, [x_e[i, j], *nfree], 4 * i)
                s0 = 4 * i
                d = ts(st[:, s0 + 2:s0 + 3], st[:, s0:s0 + 1], st[:, s0 + 1:s0 + 2], 1024.0 * EPS, ALU.add, ALU.add,
                       [a])
                d = ts(st[:, s0 + 2:s0 + 3], st[:, s0 + 2:s0 + 3], 1.0 / 1024, None, ALU.mult, after=[d])
                deps["inv", i] = recip(st[:, 112 + i:113 + i], st[:, s0 + 2:s0 + 3], [d])

        t_grow = load("pool", "grow", (grow[:], A["final_norm_g"].rearrange("(a n) -> a n", a=1)
                                      .broadcast_to([128, 1024])), after=[e_p2[i, j] for i in range(2) for j in range(2)])
        x1_e, n1 = {}, {}
        weave(residual_tiles("out", MT, lambda k, i: t_mT[k, i], 8, x1_e),
              chain(m1, merge_turn(1), raw_steps(x1_e, G_MLP, n1, [])), OUT_RATIO)
        t_x1, t_h2 = list(x1_e.values()), deps_of(n1)
        all_m = list(e_m.values())
        all_mT = [t for v in t_mT.values() for t in v]

        ZT = ars(0, 8192, 32, 256)
        z_t = []

        def z_fin(j):
            def f(b, bv, m, m0):
                o = ZT[:, 2 * j:2 * j + 2, :]
                a = act(o.f, bv, ACT.Relu, [m, *all_mT, *t_x1])
                b.free = [a]
                z_t.append(split_f(o, [tt(o.f, o.f, o.f, ALU.mult, [a])]))
            return f
        for j in range(16):
            run_all(tall("up", HT, t_h2, z_fin(j)))

        def residual_rows(key, hT, ntile, z_of, out_, scale=None):
            bs = {(i, j): big.take() for i in range(2) for j in range(2)}

            def part(i, k0, w, t):
                for j in range(2):
                    b = bs[i, j]
                    for k in range(2):
                        kk = k0 + k
                        m = mm3(b.ap, hT[:, kk, i * 128:i * 128 + 128], w[:, k, 512 * j:512 * j + 512],
                                kk == 0, kk == ntile - 1, [*t, *z_of(kk), *(b.free if kk == 0 else [])])
                    b.last = m
                return m

            for k0 in range(0, ntile - 8, 2):
                w, t = take(key)
                part(0, k0, w, t)
                done.append(part(1, k0, w, t))
                yield
            us = [take(key, a) for a in range(4)]
            last = len(done) + 4
            for i in range(2):
                for q, (w, t) in enumerate(us):
                    m = part(i, ntile - 8 + 2 * q, w, t)
                    if i == 1:
                        done.append(m)
                    if q == 3:
                        for j in range(2):
                            b = bs[i, j]
                            xo = X[:, i, 512 * j:512 * j + 512]
                            if scale is None:
                                e = tt(xo, b.ap, xo, ALU.add, [b.last])
                            else:
                                c, e = scale[i]
                                e = stt(xo, b.ap, c, xo, ALU.mult, ALU.add, [b.last, e])
                            out_[i, j] = e
                            b.free = [e]
                    if i == 1:
                        ahead(last + TILE_AHEAD, TILE_POOL)
                    yield

        MEM = ar(16384, 2, 1024)
        MEMT = wks(0, 2048, 8, 256)
        t_mem = load("pool", "mem", (MEM, A["mem_2"][0].rearrange("(i p) d -> p i d", p=128)), after=all_mT)
        t_mt = []

        def memory_turn():
            for i in range(2):
                d = rms_rows(MEM[:, i, :], i, MEM[:, i, :], [t_mem], 8 + 4 * i, junk=XN[:, i, :], after2=[n1["inv", 0], n1["inv", 1]])
                yield
                for k0 in (0, 4):
                    t_mt.extend(turn(lambda k: MEM[:, i, 128 * (k + k0):128 * (k + k0) + 128], MEMT[:, k0:k0 + 4, :],
                                     4, i, G_MEM[:, k0:k0 + 4], [d], all_m, pool=small))
                    yield
        x2_e = {}
        main = residual_rows("down", ZT, 32, lambda kk: [z_t[kk // 2]], x2_e,
                             scale=[(st[:, 112 + i:113 + i], n1["inv", i]) for i in range(2)])
        weave(main, memory_turn(), 0.5, until=lambda: (0, 1) in x2_e)

        xf_e, n2 = {}, {}

        def two_norms(i):
            P.put("act", lambda: nc.scalar.activation(eps[:, 1:2], eps[:, 0:1], ACT.Sqrt), [t_eps])
            a = row_rms(i, [[x2_e[i, j], *t_mt] for j in range(2)])
            yield
            for j in range(2):
                h = slice(512 * j, 512 * j + 512)
                xf_e[i, j] = stt(X[:, i, h], X[:, i, h], st[:, 4 * i + 3:4 * i + 4], grow[:, h], ALU.mult, ALU.mult,
                                 [a, t_grow])
            a = row_rms(i, [[xf_e[i, j]] for j in range(2)])
            yield
            yield from scaled_turn(i, a, G_MIX, n2)


        QA = ar(0, 4, 256)
        KSW = ar(1024, 2, 256)
        VSW = ar(1536, 2, 2, 128)
        XC = ar(2048, 2, 256)
        Z = ar(2560, 2, 16, 30)
        GN = ar(4000, 2, 24)
        AL = ar(3584, 256)
        QB = ar(4096, 2, 256)
        KB = ar(4608, 2, 256)
        EB = ar(5120, 2, 256)
        EN = ar(5632, 2, 256)
        EL = ar(6144, 2, 256)
        VB = ar(6656, 2, 512)
        RB = ar(7680, 2, 512)
        MRG = ar(8704, 16, 256)
        KX = ar(12800, 4, 256)
        VX = ar(13824, 2, 512)
        ONT = ars(2560, 14848, 4, 256)
        OGT = ars(15872, 16896, 4, 256)
        OG = XN[:].rearrange("p i n -> p (i n)")[:, 0:1024].rearrange("p (i n) -> p i n", i=2)

        t_kx, t_vx = [], []

        def memory_steps():
            def kx_fin(j):
                def f(b, bv, m, m0):
                    e = evac(KX[:, 2 * j:2 * j + 2, :], bv, [m])
                    b.free = [e]
                    t_kx.append(e)
                return f

            def vx_fin(i, b, m):
                e = evac(VX[:, i, :], b.ap, [m])
                b.free = [e]
                t_vx.append(e)
            for j in range(2):
                yield from tall("kx", MEMT, [*t_mt, *x2_e.values()], kx_fin(j), pool=xbanks)
            yield from wide("vx", MEMT, t_mt, vx_fin, pool=xbanks)

        xbanks = Banks([])
        xbanks.b = [scb.half[0], scb.half[1]]
        work, n0, n1_ = chain(main, memory_steps()), two_norms(0), two_norms(1)
        for c in TWO_NORMS:
            next({"M": work, "0": n0, "1": n1_}[c], None)
        run_all(work)
        run_all(n0)
        run_all(n1_)
        t_x2 = list(x2_e.values())
        t_h = deps_of(n2)
        t_xf = list(xf_e.values())
        t_grow2 = load("pool", "grow2", (grow[:], A["ln_final_g_2"].rearrange("(a n) -> a n", a=1)
                                        .broadcast_to([128, 1024])), after=t_xf)
        t_memdone = done[-1]
        t_qa = []

        def qa_fin(j):
            def f(b, bv, m, m0):
                e = act(QA[:, 2 * j:2 * j + 2, :], bv, ACT.Copy, [m, *t_x2], scale=0.125)
                b.free = [e]
                t_qa.append(e)
            return f
        for j in range(2):
            run_all(tall("qa", HT, t_h, qa_fin(j)))
        t_z = []

        def kvc_fin(b, bv, m, m0):
            kct = ar(4096, 2, 256)
            ek = evac(kct, bv, [m, *t_x2])
            b.free = [ek]
            xcs = (XC, ar(5120, 2, 256))
            e2 = []
            for c in range(2):
                e2.append(load("pool", f"xc{c}", *[pr for h in range(2) for pr in (
                    (xcs[c][0:64, h, :], kct[64 * h:64 * h + 64, c, :]),
                    (xcs[c][64:128, h, 0:255], kct[64 * h:64 * h + 64, c, 1:256]))], after=[ek]))
            for c in range(2):
                for h in range(2):
                    for half in range(2):
                        sv = xcs[c][:, h, 16 * half:16 * half + 240].rearrange("p (n j e) -> p j n e", n=15, j=8)[:, :, :, 0]
                        d = gtt(Z[:, c, 8 * half:8 * half + 8, 15 * h:15 * h + 15], sv,
                                POS[c][:, 8 * half:8 * half + 8].unsqueeze(2).broadcast_to([128, 8, 15]), ALU.add,
                                [e2[c], t_vc])
                t_z.append(d)
        run_all(tall("kvc", HT, t_h, kvc_fin))

        def kv_unit(key, br):
            w, t = take(key)
            b = big.take()
            m = turned(w, 0, t, HT, b.ap[:, 0:256], b, 8, t_h)
            e1 = evac(KSW[:, br, :], b.ap[:, 0:256], [m])
            b.free = [e1]
            b = big.take()
            m = turned(w, 128, t, HT, b.ap[:, 0:256], b, 8, t_h)
            done.append(m)
            e2 = evac(EN[:, br, :], b.ap[:, 0:256], [m, *t_x2])
            b.free = [e2]
            b = small.take()
            for i in range(2):
                m = tr(b.ap[:, 128 * i:128 * i + 128], EN[:, br, 128 * i:128 * i + 128], [e2, *b.free])
            e2 = evac(VSW[:, br], b.ap[:, 0:256].rearrange("p (a n) -> p a n", a=2), [m])
            b.free = [e2]
            return e1, e2
        e_ks, e_vs = kv_unit("kvs", 0)
        e_kw, e_vw = kv_unit("kvw", 1)
        KC = ar(3840, 2, 15)
        VC2 = ar(3872, 2, 64)
        HC = ar(17920, 2, 30)
        HG, HY = ar(16896, 2, 128), ar(17152, 2, 128)
        Z2 = [ars(8704 + 480 * c, 2560 + 480 * c, 16, 30) for c in range(2)]
        t_c = []

        def compress():
            for c in range(2):
                w, t = take(("w1k", "w1v")[c])
                b = gbanks.take()
                for j in range(16):
                    m = mm3(b.ap[0:30, 0:128], Z2[c][:, j, :], w[:, j, :], j == 0, j == 15,
                            [*t, t_z2[c], *b.free] if j == 0 else [])
                done.append(m)
                yield
                xn, y_ = HG[0:30, c, :], HY[0:30, c, :]
                e = cp(xn, b.ap[0:30, 0:128], [m, *t_x2])
                b.free = [e]
                d = tt(y_, xn, xn, ALU.mult, [e])
                d = ts(y_, y_, 0.044715, 1.0, ALU.mult, ALU.add, after=[d])
                d = tt(y_, y_, xn, ALU.mult, [d])
                a = act(y_, y_, ACT.Tanh, [d], scale=math.sqrt(2.0 / math.pi))
                d = ts(y_, y_, 0.5, 0.5, ALU.mult, ALU.add, after=[a])
                t_g = tt(xn, xn, y_, ALU.mult, [d])
                yield
                x_ = HC[:, c, :]
                b = small.take()
                m = tr(b.ap[:, 0:30], xn, [t_g, *b.free])
                t_g = cp(x_, b.ap[:, 0:30], [m])
                b.free = [t_g]
                yield
                b = gbanks.take()
                if c == 0:
                    m = mm(b.ap[:, 0:30], w2[:, 0:2, :].rearrange("p a d -> p (a d)"), x_, True, True,
                           [t_g, t_ws, *b.free])
                    e = cp(KC[0:64, 0, :], b.ap[0:64, 0:15], [m])
                    e = cp(KC[64:128, 0, :], b.ap[64:128, 15:30])
                else:
                    for h in range(2):
                        m = mm(b.ap[0:15, 64 * h:64 * h + 64], x_[:, 15 * h:15 * h + 15], w2[:, 2, :], True, True,
                               [t_g, t_ws, *b.free])
                    e = cp(VC2[0:15], b.ap[0:15, 0:128].rearrange("p (h d) -> p h d", h=2), [m])
                b.free = [e]
                t_c.append(e)
                yield

        e_qk = []

        def qk_fin(j):
            def f(b, bv, m, m0):
                e = evac((QB, KB)[j], bv, [m, *t_z])
                b.free = [e]
                e_qk.append(e)
            return f
        gbanks, mbanks = Banks([]), Banks([])
        gbanks.b, mbanks.b = big.b[0:2], big.b[2:4]
        e_og = []

        def gla():
            reset = const("reset")
            b = gbanks.take()
            for c in range(2):
                m = mm(b.ap[:, 256 * c:256 * c + 256], walp[:, 128 * c:128 * c + 128], AL[0:16, :], True, True,
                       [e_al, t_ws, *b.free])
            for c in range(2):
                d = ts(EB[:, c, :], b.ap[:, 256 * c:256 * c + 256], BA[:, c:c + 1], None, ALU.add, after=[m, t_vc, *t_z])
            b.free = [d]
            a = act(EN[:], EB[:], ACT.Abs, [d, e_vs, e_vw])
            a = act(EN[:], EN[:], ACT.Exp, [a], scale=-1.0)
            a = act(EN[:], EN[:], ACT.Ln, [a, t_eps], bias=eps[:, 0:1])
            d = ts(EB[:], EB[:], 0.0, None, ALU.min, after=[a])
            d = tt(EN[:], EB[:], EN[:], ALU.subtract, [d])
            d = ts(EN[:], EN[:], 1.0 / 16.0, None, ALU.mult, after=[d])
            for c in range(2):
                d = P.put("dve", lambda c=c: nc.vector.tensor_tensor_scan(EB[:, c, :], reset, EN[:, c, :], 0.0,
                                                                           ALU.mult, ALU.add), [d])
            ev = EB[:].rearrange("p c (n t) -> p (c n) t", t=64)
            lv = EL[:].rearrange("p c (n t) -> p (c n) t", t=64)
            d = tt(lv, ev[:, :, 63:64].broadcast_to([128, 8, 64]), ev, ALU.subtract, [d])
            act(EL[:], EL[:], ACT.Exp, [d])
            a1 = act(EN[:], EB[:], ACT.Exp, scale=-1.0)
            a = act(EB[:], EB[:], ACT.Exp, [a1])
            yield
            d = stt(QB[:], EB[:], 0.125, QB[:], ALU.mult, ALU.mult, [a, *e_qk])
            d = tt(EN[:], EN[:], KB[:], ALU.mult)
            d_el = tt(EL[:], EL[:], KB[:], ALU.mult)
            b = gbanks.take()
            for i in range(2):
                for c in range(2):
                    m = tr(b.ap[:, 256 * i + 128 * c:256 * i + 128 * c + 128], EL[:, c, 128 * i:128 * i + 128],
                           [d_el, *b.free])
            kn = KB
            e_kn = acp(kn[:], b.ap.rearrange("p (a n) -> p a n", a=2), [m])
            b.free = [e_kn]
            yield
            views = [None, EL[:, 0, :].rearrange("p (a e) -> p a e", a=2),
                     EL[:, 1, :].rearrange("p (a e) -> p a e", a=2),
                     XC[:, 0, :].rearrange("p (a e) -> p a e", a=2)]
            d_s = [None] * 4
            for n in range(3):
                lo = 64 * (n % 2)
                b = gbanks.take()
                for c in range(2):
                    m = mm(b.ap[:, 256 * c:256 * c + 256], kn[lo:lo + 64, n // 2, 128 * c:128 * c + 128],
                           VB[lo:lo + 64, n // 2, 256 * c:256 * c + 256], True, True, [e_kn, *e_vb, *b.free])
                for c in range(2):
                    for h in range(2):
                        rr = slice(64 * h, 64 * h + 64)
                        o = views[n + 1][rr, c, :]
                        inc = b.ap[rr, 256 * c + 128 * h:256 * c + 128 * h + 128]
                        if n == 0:
                            d = cp(o, inc, [m])
                        else:
                            d = stt(o, views[n][rr, c, :], EB[rr, c, 64 * n + 63:64 * n + 64], inc, ALU.mult,
                                    ALU.add, [m, d_s[n], *t_z])
                b.free = [d]
                d_s[n + 1] = d
                yield
            up, un = const("up"), const("un")
            AT = ar(1024 + 17920 - 1024 - 512, 4, 128)
            for i in range(2):
                bb = (gbanks.take(), gbanks.take())
                at = AT
                for h in (0, 2, 1, 3):
                    p, q = h % 2, h // 2
                    rr = slice(64 * p, 64 * p + 64)
                    m = mm(bb[p].ap[:, 128 * q:128 * q + 128], EN[rr, q, 128 * i:128 * i + 128],
                           QB[rr, q, 128 * i:128 * i + 128], True, True, [d_el, *bb[p].free, *e_ao])
                for p in range(2):
                    d = tt(at[:, 2 * p:2 * p + 2, :], bb[p].ap[:, 0:256].rearrange("p (h n) -> p h n", h=2),
                           up.unsqueeze(1).broadcast_to([128, 2, 128]), ALU.min, [m])
                    bb[p].free = [d]
                d = tt(at, at, un.unsqueeze(1).broadcast_to([128, 4, 128]), ALU.max, [d])
                yield
                bb = (gbanks.take(), gbanks.take())
                for p in range(2):
                    for q in range(2):
                        h = 2 * q + p
                        m = mm(bb[p].ap[:, 128 * q:128 * q + 128], at[:, 2 * p + q, :],
                               VB[:, i, 128 * h:128 * h + 128], q == 0, False,
                               [d, *bb[p].free, *e_vb])
                    for half in range(2):
                        n = 2 * i + half
                        if n == 0:
                            continue
                        for q in range(2):
                            m = mm(bb[p].ap[64 * half:64 * half + 64, 128 * q:128 * q + 128],
                                   QB[64 * p:64 * p + 64, q, 64 * n:64 * n + 64], views[n][64 * p:64 * p + 64, q, :],
                                   False, True, [d_s[n]])
                og = OG[:, i, :].rearrange("p (h d) -> p h d", h=4)
                ogp = OG[:, i, :].rearrange("p (q s d) -> p q s d", q=2, s=2)
                for p in range(2):
                    e = acp(ogp[:, :, p, :], bb[p].ap[:, 0:256].rearrange("p (q d) -> p q d", q=2), [m])
                    bb[p].free = [e]
                yield
                s4 = st[:, 64 + 8 * i:72 + 8 * i]
                sq = MRGtmp[i]
                d = tt(sq, og, og, ALU.mult, [e])
                d = rsum(s4[:, 0:4], sq, [d])
                d = ts(s4[:, 0:4], s4[:, 0:4], 1.0 / 128, EPS, ALU.mult, ALU.add, after=[d])
                d = recip(s4[:, 4:8], s4[:, 0:4], [d])
                a = act(s4[:, 0:4], s4[:, 4:8], ACT.Sqrt, [d])
                rv = RB[:, i, :]
                a2 = sig_part(sq.rearrange("p h d -> p (h d)"), rv, [d, *e_rb])
                d = tt(og, og, s4[:, 0:4].unsqueeze(2).broadcast_to([128, 4, 128]), ALU.mult, [a])
                d = tt(og, og, glag[:].unsqueeze(1).broadcast_to([128, 4, 128]), ALU.mult, [d, t_bc])
                sf = sq.rearrange("p h d -> p (h d)")
                d1 = ts(sf, sf, 0.5, 0.5, ALU.mult, ALU.add, after=[a2])
                d1 = tt(rv, rv, sf, ALU.mult, [d1])
                d = tt(OG[:, i, :], OG[:, i, :], rv, ALU.mult, [d1, d])
                e_ao.append(d)
                yield
            for i in range(2):
                e_og.extend(turn(lambda k: OG[:, i, 128 * k:128 * k + 128], OGT, 4, i, None, [e_ao[i]], e_ao, pool=gbanks))
                yield

        e_ao = []
        MRGtmp = [XN[:, 1, 512 * i:512 * i + 512].rearrange("p (h d) -> p h d", h=4) for i in range(2)]
        e_vb, e_rb = [], []
        w, t = take("small")
        b = big.take()
        for k in range(8):
            m = mm3(b.ap[0:40, 0:256], w[:, k, :], HT[:, k, :], k == 0, k == 7, [*t, *t_h(k, None), *b.free])
        done.append(m)
        gat = ar(6144, 256)
        e = evac(gat[0:40], b.ap[0:40, 0:256], [m, *t_x2])
        b.free = [e]
        t_z2 = [split_f(Z2[c], [t_z[c], t_memdone]) for c in range(2)]
        comp = compress()
        qk = chain(*[tall("qkb", HT, t_h, qk_fin(j), pool=mbanks) for j in range(2)])
        next(comp)
        ahead(len(done) + 2)
        b = small.take()
        for i in range(2):
            m = tr(b.ap[:, 64 * i:64 * i + 40], gat[0:40, 128 * i:128 * i + 128], [e, *b.free])
        bv = b.ap[:, 0:128].rearrange("p (a n) -> p a n", a=2)
        ALN = st[:, 96:128].rearrange("p (i n) -> p i n", i=2)
        e_aln = cp(ALN, bv[:, :, 24:40], [m])
        d = tt(GN[:], bv[:, :, 0:24], gateb[:].unsqueeze(1).broadcast_to([128, 2, 24]), ALU.add, [t_bc])
        b.free = [d]
        a = sig_part(GN[:], GN[:], [d])
        t_gn = ts(GN[:], GN[:], 0.5, 0.5, ALU.mult, ALU.add, after=[a])
        next(qk)
        b = small.take()
        for i in range(2):
            m = tr(b.ap[0:16, 128 * i:128 * i + 128], ALN[:, i, :], [e_aln, *b.free])
        e_al = evac(AL[0:16, :], b.ap[0:16, 0:256], [m])
        b.free = [e_al]
        lin = gla()
        def rows_to(key, dst, res):
            def fin(i, b, m):
                e = evac(dst[:, i, 0:512], b.ap, [m])
                b.free = [e]
                res.append(e)
            yield from wide(key, HT, t_h, fin, pool=mbanks)

        e_mg = []

        def merges():
            def fin(j):
                def f(b, bv, m, m0):
                    o = MRG[:, 2 * j:2 * j + 2, :]
                    e = sig_part(o, bv, [m, t_memdone, *t_c])
                    b.free = [e]
                    e_mg.append(ts(o, o, 0.5, 0.5, ALU.mult, ALU.add, after=[e]))
                return f
            for j in range(8):
                yield from tall("merge", HT, t_h, fin(j), pool=mbanks)

        dist = const("dist")
        cdist = const("cdist").rearrange("p (i n) -> p i n", i=2)
        cmask = const("cmask").rearrange("p (i n) -> p i n", i=2)
        e_on = []

        wk_free = [[t_memdone], [t_memdone]]
        wt_free = [[t_memdone], [t_memdone]]

        def nsa(n):
            i, g = divmod(n, 4)
            kend = 128 * (i + 1)
            nk = i + 1
            par = n % 2
            S = wk(1024 * par, 4, 256)
            b = scb.take()
            bv = b.ap.rearrange("p c (h n) -> p c h n", h=2)
            b2 = (ob.take(), tpb.take())
            for v in range(2):
                q = QA[64 * v:64 * v + 64, g, i * 128:i * 128 + 128]
                for br in range(2):
                    m = mm(bv[:, v, br, 0:kend], q, KSW[64 * v:64 * v + 64, br, 0:kend], True, True,
                           [*b.free, *t_qa, e_ks, e_kw])
            for v in range(2):
                q = QA[64 * v:64 * v + 64, g, i * 128:i * 128 + 128]
                m2 = mm(b2[v].ap[:, 0:15], q, KC[64 * v:64 * v + 64, 0, :], True, True,
                        [*b2[v].free, t_c[0]])
            dd = dist[:, 0:128] if i == 0 else dist[:, 128:384]
            pc = wk(3840 + 32 * par, 2, 16)[:, :, 0:15]
            for v in range(2):
                slope = 2.0 ** -(4 * v + g + 1)
                dc = stt(pc[:, v, :], cdist[:, i, :], -slope, b2[v].ap[:, 0:15], ALU.mult,
                         ALU.add, [m2, *wk_free[par]])
                b2[v].free = [dc]
            for v in range(2):
                slope = 2.0 ** -(4 * v + g + 1)
                d = stt(S[:, 2 * v:2 * v + 2, 0:kend], dd.unsqueeze(1).broadcast_to([128, 2, kend]), -slope,
                        bv[:, v, :, 0:kend], ALU.mult, ALU.add, [m, *wk_free[par]])
            b.free = [d]
            o = 32 + 12 * par
            Sv = S[:, :, 0:kend]
            d1 = rmax(st[:, o + 4:o + 6], pc, [dc])
            d1 = rmax(st[:, o:o + 4], Sv, [d])
            d1 = ts(st[:, o:o + 6], st[:, o:o + 6], -1.0, None, ALU.mult, after=[d1])
            for j in range(6):
                s_ = Sv[:, j, :] if j < 4 else pc[:, j - 4, :]
                a = act(s_, s_, ACT.Exp, [d1] if j == 0 else [], bias=st[:, o + j:o + j + 1],
                        acc=st[:, o + 6 + j:o + 7 + j])
            yield
            d = recip(st[:, o + 6:o + 12], st[:, o + 6:o + 12], [a])
            gv = GN[:, i, :].rearrange("p (v g b) -> p v g b", v=2, g=4)[:, :, g, :]
            r4 = st[:, o + 6:o + 10].rearrange("p (v b) -> p v b", v=2)
            d = tt(r4, r4, gv[:, :, 1:3], ALU.mult, [d, t_gn])
            d = tt(st[:, o + 10:o + 12], st[:, o + 10:o + 12], gv[:, :, 0], ALU.mult)
            for j in range(4):
                d = ts(Sv[:, j, :], Sv[:, j, :], st[:, o + 6 + j:o + 7 + j], None, ALU.mult,
                       after=[d] if j == 0 else [])
            for v in range(2):
                d = stt(pc[:, v, :], pc[:, v, :], st[:, o + 10 + v:o + 11 + v], cmask[:, i, :], ALU.mult,
                        ALU.mult)
            yield
            es = []
            for v in range(2):
                b = (tpb, ob)[v].take()
                for br in range(2):
                    for kt in range(nk):
                        j = br * nk + kt
                        m = tr(b.ap[:, 128 * j:128 * j + 128], S[:, 2 * v + br, 128 * kt:128 * kt + 128],
                               [d, *b.free] if j == 0 else [])
                wT = wk(2048 + 512 * v, 512)
                e = acp(wT[:, 0:256 * nk], b.ap[:, 0:256 * nk], [m, *wt_free[v]])
                b.free = [e]
                es.append(e)
            b = tpb.take()
            for v in range(2):
                m = tr(b.ap[0:15, 128 * v:128 * v + 128], pc[:, v, :], b.free)
            cT = wk(3072, 2, 128)
            e = acp(cT[0:15], b.ap[0:15, 0:256].rearrange("p (v n) -> p v n", v=2), [m, *wt_free[0], *wt_free[1]])
            b.free = [e]
            wk_free[par] = [m]
            yield
            for v in range(2):
                wT = wk(2048 + 512 * v, 512)
                b = ob.take()
                h = 4 * v + g
                hr = slice(64 * (h % 2), 64 * (h % 2) + 64)
                oo = b.ap[hr, 0:128]
                first = True
                for br in range(2):
                    for kt in range(nk):
                        j = br * nk + kt
                        m = mm(oo, VSW[:, br, kt, 64 * v:64 * v + 64], wT[:, 128 * j:128 * j + 128],
                               first, False, [es[v], e, *b.free, e_vs, e_vw] if first else [])
                        first = False
                m = mm(oo, VC2[0:15, v, :], cT[0:15, v, :], False, True, [t_c[1]])
                wt_free[v] = [m]
                o_ = ONT[hr, h // 2, i * 128:i * 128 + 128]
                e2 = split_psum(o_, oo, [m], t_c)
                b.free = [e2]
                e_on.append(e2)
            yield


        def alternate(a, b, na, nb):
            while True:
                alive = False
                for gen, k in ((a, na), (b, nb)):
                    for _ in range(k):
                        try:
                            next(gen)
                            alive = True
                        except StopIteration:
                            break
                if not alive:
                    return
                yield

        fill = chain(rows_to("vb", VB, e_vb), rows_to("rb", RB, e_rb), merges())
        for c in COMPRESS:
            next({"c": comp, "q": qk, "l": lin, "f": fill}[c])
        run_all(comp)
        assert len(e_qk) == 2 and len(e_vb) == 2
        next(lin)
        weave(alternate(staggered(nsa, 8), lin, 3, 1), fill, NSA_RATIO)

        MX = ars(4096, 6144, 8, 256)
        TMP = XN[:].rearrange("p i (a n) -> p (i a) n", n=256)
        t_mx = []
        for half in range(2):
            ds = {}

            def mix_fin(dst, go, half=half):
                def f(b, bv, m, m0):
                    o = slice(4 * half + m0, 4 * half + m0 + 2)
                    e = tt(dst[:, o, :], bv, MRG[:, go + 4 * half + m0:go + 4 * half + m0 + 2, :], ALU.mult,
                           [m, *e_mg, *e_og, *e_on, *e_ao])
                    b.free = [e]
                    ds.setdefault(m0, []).append(e)
                return f
            run_all(tall("bn", ONT, e_on, mix_fin(TMP, 0), K=4, nb=4))
            run_all(tall("bg", OGT, e_og, mix_fin(MX.f, 8), K=4, nb=4))
            for m0 in (0, 2):
                v = MX[:, 4 * half + m0:4 * half + m0 + 2, :]
                e = tt(v.f, v.f, TMP[:, 4 * half + m0:4 * half + m0 + 2, :], ALU.add, ds[m0])
                t_mx.append(split_f(v, [e]))
        x3_e, n3 = {}, {}
        weave(residual_tiles("out2", MX, lambda k, i: [t_mx[k // 2]], 8, x3_e),
              raw_steps(x3_e, G_X, n3, t_mx), 1.0)
        t_x3, t_h = list(x3_e.values()), deps_of(n3)
        sc = 128.0 ** -0.5
        rs = st[:, 114:116]
        t_rs = act(rs, st[:, 112:114], ACT.Sqrt, [n3["inv", 0], n3["inv", 1]], scale=sc * sc)
        QX = ar(0, 4, 256)
        OX = ars(1024, 2048, 4, 256)
        t_qx = []

        def qx_fin(j):
            def f(b, bv, m, m0):
                e = evac(QX[:, 2 * j:2 * j + 2, :], bv, [m, *t_x3])
                b.free = [e]
                t_qx.append(e)
            return f
        e_ox = []
        wk_f = [[], []]
        wt_f = [[], []]

        def xattn(h):
            par = h % 2
            S = wk(512 * par, 2, 256)
            b = xbanks.take()
            bv = b.ap.rearrange("p (i n) -> p i n", i=2)
            for i in range(2):
                m = mm(bv[:, i, :], QX[:, h, i * 128:i * 128 + 128], KX[:, h, :], True, True,
                       [*b.free, t_qx[h // 2], *t_kx])
            mx, sm = st[:, 32 + 4 * par:34 + 4 * par], st[:, 34 + 4 * par:36 + 4 * par]
            d = rmax(mx, bv, [m, *wk_f[par]])
            d = stt(mx, mx, -1.0, rs, ALU.mult, ALU.mult, [d, t_rs])
            for i in range(2):
                a = act(S[:, i, :], bv[:, i, :], ACT.Exp, [d, *wk_f[par], *e_on], bias=mx[:, i:i + 1], scale=rs[:, i:i + 1],
                        acc=sm[:, i:i + 1])
            b.free = [a]
            yield
            d = recip(sm, sm, [a])
            for i in range(2):
                d2 = ts(S[:, i, :], S[:, i, :], sm[:, i:i + 1], None, ALU.mult, after=[d])
            yield
            b = tpb.take()
            for i in range(2):
                for mt in range(2):
                    m = tr(b.ap[:, 256 * mt + 128 * i:256 * mt + 128 * i + 128],
                           S[:, i, 128 * mt:128 * mt + 128], [d2, *b.free])
            wk_f[par] = [m]
            pT = wk(1024 + 512 * par, 2, 256)
            e = acp(pT, b.ap.rearrange("p (a n) -> p a n", a=2), [m, *wt_f[par]])
            b.free = [e]
            yield
            b = ob.take()
            for mt in range(2):
                m2 = mm(b.ap[:, 0:256], VX[:, mt, 128 * h:128 * h + 128], pT[:, mt, :], mt == 0, mt == 1,
                        [e, *b.free, *t_vx])
            wt_f[par] = [m2]
            e2 = split_psum(OX[:, h, :], b.ap[:, 0:256], [m2], t_x3)
            b.free = [e2]
            e_ox.append(e2)
            yield

        run_all(tall("xq", HT, t_h, qx_fin(0)))
        q2 = tall("xq", HT, t_h, qx_fin(1))

        def hook_x(n):
            return iter(())

        def with_q2():
            g = staggered(xattn, 4)
            next(g)
            next(q2)
            next(q2)
            for _ in q2:
                pass
            yield from g
        run_all(with_q2())
        x4_e, n4 = {}, {}

        def ffn_norm():
            for i in range(2):
                while (i, 1) not in x4_e:
                    yield
                P.put("act", lambda: nc.scalar.activation(eps[:, 1:2], eps[:, 0:1], ACT.Sqrt), [t_eps])
                a = row_rms(i, [[x4_e[i, 0]], [x4_e[i, 1]]])
                yield
                yield from scaled_turn(i, a, G_FFN, n4)
        weave(residual_tiles("xo", OX, lambda k, i: [e_ox[k]], 4, x4_e), ffn_norm(), 1.0)
        t_h = deps_of(n4)
        FT = ars(4096, 4096 + 5632, 22, 256)
        cw = VC[:, 1, 0:66].rearrange("p (t c) -> p t c", t=3)
        e_f = []
        fw_free = [[], [], []]
        fbanks = Banks([])
        fbanks.b = big.b + scb.half + tpb.b + ob.b
        tails = []

        def ffn_tail():
            par, o, Y, bg, a = tails.pop(0)
            d = tt(o.f, Y, bg.ap.rearrange("p (a n) -> p a n", a=2), ALU.mult, [a, bg.m])
            bg.free = [d]
            fw_free[par] = [d]
            e_f.append(split_f(o, [d]))

        for j in range(11):
            bu, bg = fbanks.take(), fbanks.take()
            for b in (bu, bg):
                w, t = take("up2")
                for h in range(2):
                    b.m = turned(w, 128 * h, t, HT, b.ap[:, 256 * h:256 * h + 256], b, 8, t_h)
                done.append(b.m)
            par = j % 3
            U = wk(1024 * par, 2, 256)
            Y = wk(1024 * par + 512, 2, 256)
            for h in range(2):
                ch = 2 * j + h
                u = bu.ap[:, 256 * h:256 * h + 256]
                a = act(U[:, h, :], u, ACT.Identity, [bu.m, *fw_free[par], *e_ox, t_vc], scale=cw[:, 2, ch:ch + 1],
                        bias=CB[:, ch:ch + 1])
            for h in range(2):
                ch = 2 * j + h
                u = bu.ap[:, 256 * h:256 * h + 256]
                d = stt(U[:, h, 1:256], u[:, 0:255], cw[:, 1, ch:ch + 1], U[:, h, 1:256], ALU.mult, ALU.add, [a])
                d = stt(U[:, h, 2:256], u[:, 0:254], cw[:, 0, ch:ch + 1], U[:, h, 2:256], ALU.mult, ALU.add, [d])
            bu.free = [d]
            if tails:
                ffn_tail()
            p1 = gtt(Y, U, U, ALU.mult, [d])
            p1 = P.put("pool", lambda Y=Y: nc.gpsimd.tensor_scalar(Y, Y, 0.044715, 1.0, ALU.mult, ALU.add), [p1])
            p1 = gtt(Y, Y, U, ALU.mult, [p1])
            a = act(Y, Y, ACT.Tanh, [p1], scale=math.sqrt(2.0 / math.pi))
            a = P.put("pool", lambda Y=Y: nc.gpsimd.tensor_scalar(Y, Y, 0.5, 0.5, ALU.mult, ALU.add), [a])
            p1 = gtt(Y, Y, U, ALU.mult, [a])
            tails.append((par, FT[:, 2 * j:2 * j + 2, :], Y, bg, p1))
        ffn_tail()
        x5_e = {}
        main = residual_rows("down2", FT, 22, lambda kk: [e_f[kk // 2]], x5_e)
        s_out = sem("s_out")
        outs = []
        ov = out[0].rearrange("(i p) d -> p i d", p=128)
        for i in range(2):
            while (i, 1) not in x5_e:
                next(main)
            if i == 0:
                P.put("act", lambda: nc.scalar.activation(eps[:, 1:2], eps[:, 0:1], ACT.Sqrt), [t_eps])
            a = row_rms(i, [[x5_e[i, 0]], [x5_e[i, 1]]])
            for j in range(2):
                h = slice(512 * j, 512 * j + 512)
                d = stt(XN[:, i, h], X[:, i, h], st[:, 4 * i + 3:4 * i + 4], grow[:, h], ALU.mult, ALU.mult,
                        [a, t_grow2])
                outs.append(P.dma("sp", [lambda i=i, h=h: nc.sync.dma_start(ov[:, i, h], XN[:, i, h])], [d], s_out))
        run_all(main)
        assert len(done) == len(plan)
        P.q["sp"].append((None, (outs[-1],), None, None))
        P.emit()


_INS = ['x', 'positions', 'norm_attn_g', 'w_in', 'lam_q1', 'lam_k1', 'lam_q2', 'lam_k2', 'subln_g', 'w_pool',
        'pool_scale', 'w_out', 'norm_mlp_g', 'w_up', 'w_down', 'final_norm_g', 'mem_2', 'ln_mix_g_2', 'w_in_2',
        'nsa_gate_b_2', 'cmp_pos_k_2', 'cmp_w1_k_2', 'cmp_w2_k_2', 'cmp_pos_v_2', 'cmp_w1_v_2', 'cmp_w2_v_2',
        'gla_w_alpha2_2', 'gla_b_alpha_2', 'gla_norm_g_2', 'w_branch_nsa_2', 'w_branch_gla_2', 'w_out_2',
        'ln_x_g_2', 'ln_mem_g_2', 'w_xq_2', 'w_xkv_2', 'w_xo_2', 'ln_ffn_g_2', 'w_up_2', 'conv_w_2', 'conv_b_2',
        'w_down_2', 'ln_final_g_2']


def kernel(**inputs):
    import numpy as _np
    import concourse.bacc as _bacc
    from concourse import mybir as _mybir
    from concourse.bass_utils import run_bass_kernel_spmd as _run

    nc = _bacc.Bacc("TRN2", target_bir_lowering=False, num_devices=1)
    arrays, args = {}, {}
    for name in _INS:
        a = _np.ascontiguousarray(inputs[name])
        arrays[f"in_{name}_dram"] = a
        args[name] = nc.dram_tensor(f"in_{name}_dram", a.shape, _mybir.dt.from_np(a.dtype),
                                    kind="ExternalInput").ap()
    a = shape_constants()
    arrays["shape_constants"] = a
    args["shape_constants"] = nc.dram_tensor("shape_constants", a.shape, _mybir.dt.float32,
                                             kind="ExternalInput").ap()
    o = nc.dram_tensor("out_0_dram", (1, 256, 1024), _mybir.dt.float32, kind="ExternalOutput").ap()
    two_blocks(nc, args, o)
    r = _run(nc, [arrays], core_ids=[0])
    return r.results[0]["out_0_dram"]
```
